# Optimizing a Trainium2 kernel written in Bass

```python
import math
import jax
import jax.numpy as jnp
from jax import lax
import numpy as np

D_MODEL = 1024
BATCH = 1
SEQ = 256
DEPTH = 2

N_A_LAYERS = DEPTH // 2
N_B_LAYERS = DEPTH - N_A_LAYERS

A_HEADS = 8
A_DK = 128
A_DV = 128
A_KEY_W = A_HEADS * A_DK
A_VAL_W = A_HEADS * A_DV
A_CONV_CH = 2 * A_KEY_W + A_VAL_W
A_IN_W = A_CONV_CH + A_VAL_W + 2 * A_HEADS
CONV_W = 4
CHUNK = 64

B_HEADS = 8
B_DH = 128
B_W = B_HEADS * B_DH
MOBA_BLOCK = 256
MOBA_TOPK = 3
Q_SUB = 32

N_BUCKETS = 32
MAX_DIST = 2048
EPS = 1e-6


def rms_norm(x, g):
    xf = x.astype(jnp.float32)
    y = xf * lax.rsqrt(jnp.mean(xf * xf, axis=-1, keepdims=True) + EPS)
    return (y * g.astype(jnp.float32)).astype(x.dtype)

def l2_normalize(t):
    tf = t.astype(jnp.float32)
    return tf * lax.rsqrt(jnp.sum(tf * tf, axis=-1, keepdims=True) + EPS)

def causal_conv_silu(u, w):
    c = u.shape[-1]
    up = jnp.pad(u, ((0, 0), (CONV_W - 1, 0), (0, 0)))
    out = lax.conv_general_dilated(up, w[:, None, :].astype(u.dtype), window_strides=(1,), padding="VALID", dimension_numbers=("NWC", "WIO", "NWC"), feature_group_count=c)
    return jax.nn.silu(out)

def gated_delta_rule(q, k, v, g, beta):
    bsz, s, h, dk = q.shape
    dv = v.shape[-1]
    n = s // CHUNK
    f32 = jnp.float32

    def to_chunks(t):
        t = t.astype(f32).reshape((bsz, n, CHUNK) + t.shape[2:])
        return jnp.moveaxis(t, 3, 1)

    q, k, v, g, beta = (to_chunks(t) for t in (q, k, v, g, beta))
    g = jnp.cumsum(g, axis=-1)
    idx = jnp.arange(CHUNK)
    tril = idx[:, None] >= idx[None, :]
    strict = idx[:, None] > idx[None, :]
    decay = jnp.exp(jnp.where(tril, g[..., :, None] - g[..., None, :], -jnp.inf))
    k_beta = k * beta[..., None]
    a_mat = jnp.where(strict, jnp.einsum("bhncd,bhnsd->bhncs", k_beta, k) * decay, 0.0)
    rhs = jnp.concatenate([v * beta[..., None], k_beta * jnp.exp(g)[..., None]], axis=-1)
    sol = lax.linalg.triangular_solve(a_mat + jnp.eye(CHUNK, dtype=f32), rhs, left_side=True, lower=True, unit_diagonal=True)
    u, w = sol[..., :dv], sol[..., dv:]
    qk_intra = jnp.where(tril, jnp.einsum("bhncd,bhnsd->bhncs", q, k) * decay, 0.0)
    q_dec = q * jnp.exp(g)[..., None]
    k_dec = k * jnp.exp(g[..., -1:] - g)[..., None]
    g_last = jnp.exp(g[..., -1])

    def step(state, xs):
        u_c, w_c, qd_c, qk_c, kd_c, gl_c = xs
        v_new = u_c - jnp.einsum("bhck,bhkv->bhcv", w_c, state)
        o = jnp.einsum("bhck,bhkv->bhcv", qd_c, state) + jnp.einsum("bhcs,bhsv->bhcv", qk_c, v_new)
        state = state * gl_c[..., None, None] + jnp.einsum("bhck,bhcv->bhkv", kd_c, v_new)
        return state, o

    xs = tuple(jnp.moveaxis(t, 2, 0) for t in (u, w, q_dec, qk_intra, k_dec, g_last))
    state0 = jnp.zeros((bsz, h, dk, dv), f32)
    _, o = lax.scan(step, state0, xs)
    return o.transpose(1, 0, 3, 2, 4).reshape(bsz, s, h, dv)

def gated_deltanet_mixer(hn, w_in, conv_w, a_log, dt_bias, out_norm_g, w_out):
    bsz, s, _ = hn.shape
    f32 = jnp.float32
    proj = hn @ w_in
    qkv = causal_conv_silu(proj[..., :A_CONV_CH], conv_w)
    z = proj[..., A_CONV_CH:A_CONV_CH + A_VAL_W]
    a = proj[..., A_CONV_CH + A_VAL_W:A_CONV_CH + A_VAL_W + A_HEADS]
    b = proj[..., A_CONV_CH + A_VAL_W + A_HEADS:]
    q = l2_normalize(qkv[..., :A_KEY_W].reshape(bsz, s, A_HEADS, A_DK)) * (A_DK ** -0.5)
    k = l2_normalize(qkv[..., A_KEY_W:2 * A_KEY_W].reshape(bsz, s, A_HEADS, A_DK))
    v = qkv[..., 2 * A_KEY_W:].reshape(bsz, s, A_HEADS, A_DV)
    g = -jnp.exp(a_log.astype(f32)) * jax.nn.softplus(a.astype(f32) + dt_bias.astype(f32))
    beta = jax.nn.sigmoid(b.astype(f32))
    o = gated_delta_rule(q, k, v, g, beta)
    o = rms_norm(o, out_norm_g) * jax.nn.silu(z.astype(f32)).reshape(bsz, s, A_HEADS, A_DV)
    return o.reshape(bsz, s, A_VAL_W).astype(hn.dtype) @ w_out

def t5_bucket(rel):
    n = jnp.maximum(rel, 0)
    max_exact = N_BUCKETS // 2
    nf = jnp.maximum(n, 1).astype(jnp.float32)
    large = max_exact + (jnp.log(nf / max_exact) / math.log(MAX_DIST / max_exact) * (N_BUCKETS - max_exact)).astype(jnp.int32)
    large = jnp.minimum(large, N_BUCKETS - 1)
    return jnp.where(n < max_exact, n, large)

def shared_kv(x, kv_norm_g, w_kv):
    bsz, s, _ = x.shape
    kv = rms_norm(x, kv_norm_g) @ w_kv
    n_blk = -(-s // MOBA_BLOCK)
    s_pad = n_blk * MOBA_BLOCK

    def blocks(t):
        t = jnp.pad(t.reshape(bsz, s, B_HEADS, B_DH), ((0, 0), (0, s_pad - s), (0, 0), (0, 0)))
        return t.reshape(bsz, n_blk, MOBA_BLOCK, B_HEADS, B_DH).transpose(0, 3, 1, 2, 4)

    kb = blocks(kv[..., :B_W])
    vb = blocks(kv[..., B_W:])
    k_mean = jnp.mean(kb.astype(jnp.float32), axis=3)
    return kb, vb, k_mean

def moba_attention(q, kb, vb, k_mean, rel_bias):
    bsz, s, h, d = q.shape
    n_blk = kb.shape[2]
    topk = min(MOBA_TOPK, n_blk)
    scale = d ** -0.5
    f32 = jnp.float32
    n_sub = s // Q_SUB
    q_sub = q.transpose(0, 2, 1, 3).reshape(bsz, h, n_sub, Q_SUB, d).transpose(2, 0, 1, 3, 4)
    bias_t = rel_bias.T.astype(f32)
    b_ix = jnp.arange(bsz)[:, None, None, None]
    h_ix = jnp.arange(h)[None, :, None, None]
    blk_ids = jnp.arange(n_blk)
    offs = jnp.arange(MOBA_BLOCK)

    def one_sub(args):
        qs, s_idx = args
        q_pos = s_idx * Q_SUB + jnp.arange(Q_SUB)
        cur = (s_idx * Q_SUB) // MOBA_BLOCK
        qf = qs.astype(f32)
        gate = jnp.einsum("bhqd,bhnd->bhqn", qf, k_mean)
        gate = jnp.where(blk_ids < cur, gate, -jnp.inf)
        _, sel = lax.top_k(gate, topk)
        sel_ok = jnp.arange(topk) < cur
        k_sel = kb[b_ix, h_ix, sel].astype(f32)
        v_sel = vb[b_ix, h_ix, sel].astype(f32)
        k_pos_sel = sel[..., None] * MOBA_BLOCK + offs
        s_sel = jnp.einsum("bhqd,bhqkjd->bhqkj", qf, k_sel) * scale
        s_sel = s_sel + bias_t[h_ix[..., None], t5_bucket(q_pos[:, None, None] - k_pos_sel)]
        s_sel = jnp.where(sel_ok[:, None], s_sel, -jnp.inf).reshape(bsz, h, Q_SUB, topk * MOBA_BLOCK)
        k_own = lax.dynamic_index_in_dim(kb, cur, axis=2, keepdims=False).astype(f32)
        v_own = lax.dynamic_index_in_dim(vb, cur, axis=2, keepdims=False).astype(f32)
        rel_own = q_pos[:, None] - (cur * MOBA_BLOCK + offs)[None, :]
        s_own = jnp.einsum("bhqd,bhjd->bhqj", qf, k_own) * scale + bias_t[:, t5_bucket(rel_own)]
        s_own = jnp.where(rel_own >= 0, s_own, -jnp.inf)
        p = jax.nn.softmax(jnp.concatenate([s_sel, s_own], axis=-1), axis=-1)
        p_sel = p[..., :topk * MOBA_BLOCK].reshape(bsz, h, Q_SUB, topk, MOBA_BLOCK)
        p_own = p[..., topk * MOBA_BLOCK:]
        o = jnp.einsum("bhqkj,bhqkjd->bhqd", p_sel, v_sel) + jnp.einsum("bhqj,bhjd->bhqd", p_own, v_own)
        return o.astype(qs.dtype)

    o = lax.map(one_sub, (q_sub, jnp.arange(n_sub)))
    return o.transpose(1, 0, 3, 2, 4).reshape(bsz, s, h * d)

def moba_mixer(hn, w_in, w_out, kb, vb, k_mean, rel_bias):
    bsz, s, _ = hn.shape
    proj = hn @ w_in
    q = proj[..., :B_W].reshape(bsz, s, B_HEADS, B_DH)
    z = proj[..., B_W:]
    o = moba_attention(q, kb, vb, k_mean, rel_bias)
    return (o * jax.nn.silu(z)).astype(hn.dtype) @ w_out

def first_inputs(seed: int = 0) -> dict:
    key = jax.random.key(seed)
    ks = jax.random.split(key, 16)
    f32 = jnp.float32
    na, nb = N_A_LAYERS, N_B_LAYERS

    def gain(k, shape):
        return 1.0 + 0.01 * jax.random.normal(k, shape, f32)

    x = jax.random.normal(ks[0], (BATCH, SEQ, D_MODEL), f32)
    a_norm_g = gain(ks[1], (na, D_MODEL))
    a_w_in = jax.random.normal(ks[2], (na, D_MODEL, A_IN_W), f32) * D_MODEL ** -0.5
    a_conv_w = jax.random.normal(ks[3], (na, CONV_W, A_CONV_CH), f32) * CONV_W ** -0.5
    a_log = jnp.log(jax.random.uniform(ks[4], (na, A_HEADS), f32, 1.0, 16.0))
    dt = jnp.exp(jax.random.uniform(ks[5], (na, A_HEADS), f32, math.log(1e-3), math.log(1e-1)))
    a_dt_bias = dt + jnp.log(-jnp.expm1(-dt))
    a_out_norm_g = gain(ks[6], (na, A_DV))
    a_w_out = jax.random.normal(ks[7], (na, A_VAL_W, D_MODEL), f32) * A_VAL_W ** -0.5
    kv_norm_g = gain(ks[8], (D_MODEL,))
    w_kv = jax.random.normal(ks[9], (D_MODEL, 2 * B_W), f32) * D_MODEL ** -0.5
    b_norm_g = gain(ks[10], (nb, D_MODEL))
    b_w_in = jax.random.normal(ks[11], (nb, D_MODEL, 2 * B_W), f32) * D_MODEL ** -0.5
    b_w_out = jax.random.normal(ks[12], (nb, B_W, D_MODEL), f32) * B_W ** -0.5
    rel_bias = 0.2 * jax.random.normal(ks[13], (N_BUCKETS, B_HEADS), f32)
    final_norm_g = gain(ks[14], (D_MODEL,))
    return {"x": x, "a_norm_g": a_norm_g, "a_w_in": a_w_in, "a_conv_w": a_conv_w, "a_log": a_log, "a_dt_bias": a_dt_bias, "a_out_norm_g": a_out_norm_g, "a_w_out": a_w_out, "kv_norm_g": kv_norm_g, "w_kv": w_kv, "b_norm_g": b_norm_g, "b_w_in": b_w_in, "b_w_out": b_w_out, "rel_bias": rel_bias, "final_norm_g": final_norm_g}

def first_block(x, a_norm_g, a_w_in, a_conv_w, a_log, a_dt_bias, a_out_norm_g, a_w_out, kv_norm_g, w_kv, b_norm_g, b_w_in, b_w_out, rel_bias, final_norm_g):
    shared = None
    for layer in range(DEPTH):
        if layer < N_A_LAYERS:
            i = layer
            x = x + gated_deltanet_mixer(rms_norm(x, a_norm_g[i]), a_w_in[i], a_conv_w[i], a_log[i], a_dt_bias[i], a_out_norm_g[i], a_w_out[i])
        else:
            if shared is None:
                shared = shared_kv(x, kv_norm_g, w_kv)
            j = layer - N_A_LAYERS
            kb, vb, k_mean = shared
            x = x + moba_mixer(rms_norm(x, b_norm_g[j]), b_w_in[j], b_w_out[j], kb, vb, k_mean, rel_bias)
    return rms_norm(x, final_norm_g)


DEPTH_2 = 1

GRID_W = 64
CTX_LEN = 256
N_MOD = 6
NEG_INF = -1e30

D_MIX = D_MODEL
NA_HEAD_DIM = 64
D_NA = D_MIX // 2
NA_HEADS = D_NA // NA_HEAD_DIM
NA_WIN_H = 8
NA_WIN_W = 16
RPB_H = 2 * NA_WIN_H - 1
RPB_W = 2 * NA_WIN_W - 1
D_HY = D_MIX // 4
HY_ORDER = 2
HY_SHORT = 3
HY_EMB = 33
HY_FILT = 64
HY_FAST_DECAY = 0.3
HY_SLOW_DECAY = 1.5
HY_TARGET = 1e-2
D_CF = D_MIX - D_NA - D_HY
CF_KERNEL = 31
D_IN = 3 * D_NA + (HY_ORDER + 1) * D_HY + 2 * D_CF
N_EXPERTS = 16
EC_CAPACITY = 2
EXPERT_FF = 2 * D_MODEL


def rmsnorm(x, g):
    x32 = x.astype(jnp.float32)
    y = x32 * lax.rsqrt(jnp.mean(x32 * x32, axis=-1, keepdims=True) + EPS)
    return (y * g.astype(jnp.float32)).astype(x.dtype)

def modulate(h, shift, scale):
    return h * (1 + scale) + shift

def adaln(cvec, w_mod, b_mod):
    m = jax.nn.silu(cvec) @ w_mod + b_mod
    return jnp.split(m, N_MOD, axis=-1)

def heads(t):
    return t.reshape(t.shape[0], t.shape[1], NA_HEADS, NA_HEAD_DIM)

def depthwise_conv(x, w, b):
    k = w.shape[0]
    pad = (k - 1) // 2
    y = lax.conv_general_dilated(
        x, w.astype(x.dtype)[:, None, :], window_strides=(1,), padding=[(pad, k - 1 - pad)],
        dimension_numbers=('NWC', 'WIO', 'NWC'), feature_group_count=x.shape[-1])
    return y + b.astype(x.dtype)

def neighbourhood_attention(q, k, v, k_ctx, v_ctx, rpb):
    B, S, H, Dh = q.shape
    rows = S // GRID_W
    wh = min(NA_WIN_H, rows)
    nk = wh * GRID_W
    scale = Dh ** -0.5
    qg = q.reshape(B, rows, GRID_W, H, Dh)
    kg = k.reshape(B, rows, GRID_W, H, Dh)
    vg = v.reshape(B, rows, GRID_W, H, Dh)
    col = jnp.arange(GRID_W)
    c0 = jnp.clip(col - NA_WIN_W // 2, 0, GRID_W - NA_WIN_W)
    col_ok = (col[None, :] >= c0[:, None]) & (col[None, :] < c0[:, None] + NA_WIN_W)
    mask = jnp.broadcast_to(col_ok[:, None, :], (GRID_W, wh, GRID_W)).reshape(GRID_W, nk)
    dc = jnp.clip(col[None, :] - col[:, None], 1 - NA_WIN_W, NA_WIN_W - 1) + NA_WIN_W - 1
    rpb32 = rpb.astype(jnp.float32)

    def row_block(r):
        r0 = jnp.clip(r - wh // 2, 0, rows - wh)
        qb = lax.dynamic_index_in_dim(qg, r, axis=1, keepdims=False)
        kb = lax.dynamic_slice_in_dim(kg, r0, wh, axis=1).reshape(B, nk, H, Dh)
        vb = lax.dynamic_slice_in_dim(vg, r0, wh, axis=1).reshape(B, nk, H, Dh)
        dr = r0 + jnp.arange(wh) - r + NA_WIN_H - 1
        bias = rpb32[:, dr[None, :, None], dc[:, None, :]].reshape(H, GRID_W, nk)
        s_nb = jnp.einsum('bqhd,bkhd->bhqk', qb, kb).astype(jnp.float32) * scale + bias
        s_nb = jnp.where(mask, s_nb, NEG_INF)
        s_cx = jnp.einsum('bqhd,bkhd->bhqk', qb, k_ctx).astype(jnp.float32) * scale
        p = jax.nn.softmax(jnp.concatenate([s_nb, s_cx], axis=-1), axis=-1).astype(v.dtype)
        return (jnp.einsum('bhqk,bkhd->bqhd', p[..., :nk], vb)
                + jnp.einsum('bhqk,bkhd->bqhd', p[..., nk:], v_ctx))

    out = lax.map(row_block, jnp.arange(rows))
    return out.transpose(1, 0, 2, 3, 4).reshape(B, S, H * Dh)

def context_attention(q, k, v):
    s = jnp.einsum('bqhd,bkhd->bhqk', q, k).astype(jnp.float32) * (q.shape[-1] ** -0.5)
    p = jax.nn.softmax(s, axis=-1).astype(v.dtype)
    o = jnp.einsum('bhqk,bkhd->bqhd', p, v)
    return o.reshape(o.shape[0], o.shape[1], -1)

def hyena_filter_spectrum(L, w1, b1, freq, w2, b2, w3):
    f32 = jnp.float32
    pos = jnp.arange(L, dtype=f32)[:, None]
    t = pos / max(L - 1, 1)
    bands = (HY_EMB - 1) // 2
    fb = jnp.linspace(1e-4, bands - 1, bands, dtype=f32)[None, :]
    ang = fb * (2.0 * math.pi) * pos / L
    z = jnp.concatenate([t, jnp.cos(ang), -jnp.sin(ang)], axis=-1)
    fr = freq.astype(f32)
    h = jnp.sin(fr * (z @ w1.astype(f32) + b1.astype(f32)))
    h = jnp.sin(fr * (h @ w2.astype(f32) + b2.astype(f32)))
    h = (h @ w3.astype(f32)).reshape(L, 2, HY_ORDER, D_HY)
    min_decay = math.log(HY_TARGET) / HY_SLOW_DECAY
    max_decay = math.log(HY_TARGET) / HY_FAST_DECAY
    rate = jnp.abs(jnp.linspace(min_decay, max_decay, D_HY, dtype=f32))
    h = h * jnp.exp(-t * rate)[:, None, None, :]
    fwd, bwd = h[:, 0], h[:, 1]
    k_circ = jnp.concatenate([fwd, jnp.zeros_like(fwd[:1]), bwd[1:][::-1]], axis=0)
    return jnp.fft.rfft(k_circ, axis=0)

def hyena_mixer(u, short_w, short_b, bias_d, w1, b1, freq, w2, b2, w3):
    dt = u.dtype
    L = u.shape[1]
    u = depthwise_conv(u, short_w, short_b).astype(jnp.float32)
    x1, x2, v = jnp.split(u, 3, axis=-1)
    k_spec = hyena_filter_spectrum(L, w1, b1, freq, w2, b2, w3)
    d = bias_d.astype(jnp.float32)
    z = v
    for n, gate in enumerate((x1, x2)):
        z_f = jnp.fft.rfft(z, n=2 * L, axis=1)
        conv = jnp.fft.irfft(z_f * k_spec[None, :, n], n=2 * L, axis=1)[:, :L]
        z = gate * (conv + d[n] * z)
    return z.astype(dt)

def conformer_conv(u, dw_w, dw_b, ln_g, ln_b):
    a, g = jnp.split(u, 2, axis=-1)
    y = depthwise_conv(a * jax.nn.sigmoid(g), dw_w, dw_b).astype(jnp.float32)
    mu = jnp.mean(y, axis=-1, keepdims=True)
    var = jnp.mean(jnp.square(y - mu), axis=-1, keepdims=True)
    y = (y - mu) * lax.rsqrt(var + EPS) * ln_g.astype(jnp.float32) + ln_b.astype(jnp.float32)
    return jax.nn.silu(y).astype(u.dtype)

def expert_choice_ffn(h, w_router, w1, w3, w2):
    B, L, _ = h.shape
    cap = EC_CAPACITY * L // N_EXPERTS
    aff = jax.nn.softmax((h @ w_router).astype(jnp.float32), axis=-1)
    gate, idx = lax.top_k(jnp.swapaxes(aff, 1, 2), cap)
    b_idx = jnp.arange(B)[:, None, None]
    xe = h[b_idx, idx]
    a = jnp.einsum('becd,edf->becf', xe, w1)
    u = jnp.einsum('becd,edf->becf', xe, w3)
    y = jnp.einsum('becf,efd->becd', jax.nn.silu(a) * u, w2)
    y = y * gate[..., None].astype(y.dtype)
    return jnp.zeros_like(h).at[b_idx, idx].add(y)

def second_inputs(seed: int = 0) -> dict:
    key = jax.random.key(seed)
    ks = jax.random.split(key, 32)
    f32 = jnp.float32

    def nrm(k, shape, scale):
        return scale * jax.random.normal(k, shape, f32)

    L = DEPTH_2
    return {
        'x': nrm(ks[0], (BATCH, SEQ, D_MODEL), 1.0),
        'c': nrm(ks[1], (BATCH, D_MODEL), 1.0),
        'ctx': nrm(ks[2], (BATCH, CTX_LEN, D_MODEL), 1.0),
        'c_ctx': nrm(ks[3], (D_MODEL,), 1.0),
        'w_mod': nrm(ks[4], (L, D_MODEL, N_MOD * D_MODEL), 0.5 * D_MODEL ** -0.5),
        'b_mod': nrm(ks[5], (L, N_MOD * D_MODEL), 0.02),
        'norm1_g': 1.0 + nrm(ks[6], (L, D_MODEL), 0.02),
        'norm2_g': 1.0 + nrm(ks[7], (L, D_MODEL), 0.02),
        'w_in': nrm(ks[8], (L, D_MODEL, D_IN), D_MODEL ** -0.5),
        'na_rpb': nrm(ks[9], (L, NA_HEADS, RPB_H, RPB_W), 0.1),
        'hy_short_w': nrm(ks[10], (L, HY_SHORT, (HY_ORDER + 1) * D_HY), HY_SHORT ** -0.5),
        'hy_short_b': nrm(ks[11], (L, (HY_ORDER + 1) * D_HY), 0.02),
        'hy_filt_w1': nrm(ks[12], (L, HY_EMB, HY_FILT), HY_EMB ** -0.5),
        'hy_filt_b1': nrm(ks[13], (L, HY_FILT), 0.02),
        'hy_filt_freq': 1.0 + nrm(ks[14], (L, HY_FILT), 0.02),
        'hy_filt_w2': nrm(ks[15], (L, HY_FILT, HY_FILT), HY_FILT ** -0.5),
        'hy_filt_b2': nrm(ks[16], (L, HY_FILT), 0.02),
        'hy_filt_w3': nrm(ks[17], (L, HY_FILT, 2 * HY_ORDER * D_HY), 0.05 * HY_FILT ** -0.5),
        'hy_bias_d': nrm(ks[18], (L, HY_ORDER, D_HY), 0.5),
        'cf_dw_w': nrm(ks[19], (L, CF_KERNEL, D_CF), CF_KERNEL ** -0.5),
        'cf_dw_b': nrm(ks[20], (L, D_CF), 0.02),
        'cf_ln_g': 1.0 + nrm(ks[21], (L, D_CF), 0.02),
        'cf_ln_b': nrm(ks[22], (L, D_CF), 0.02),
        'w_out': nrm(ks[23], (L, D_MIX, D_MODEL), D_MIX ** -0.5),
        'router_w': nrm(ks[24], (L, D_MODEL, N_EXPERTS), D_MODEL ** -0.5),
        'expert_w1': nrm(ks[25], (L, N_EXPERTS, D_MODEL, EXPERT_FF), D_MODEL ** -0.5),
        'expert_w3': nrm(ks[26], (L, N_EXPERTS, D_MODEL, EXPERT_FF), D_MODEL ** -0.5),
        'expert_w2': nrm(ks[27], (L, N_EXPERTS, EXPERT_FF, D_MODEL), EXPERT_FF ** -0.5),
        'final_norm_g': 1.0 + nrm(ks[28], (D_MODEL,), 0.02),
    }

def second_block(x, c, ctx, c_ctx, w_mod, b_mod, norm1_g, norm2_g, w_in, na_rpb,
              hy_short_w, hy_short_b, hy_filt_w1, hy_filt_b1, hy_filt_freq, hy_filt_w2,
              hy_filt_b2, hy_filt_w3, hy_bias_d, cf_dw_w, cf_dw_b, cf_ln_g, cf_ln_b,
              w_out, router_w, expert_w1, expert_w3, expert_w2, final_norm_g):
    splits = [D_NA, 2 * D_NA, 3 * D_NA, 3 * D_NA + (HY_ORDER + 1) * D_HY]
    xc = ctx
    for l in range(DEPTH_2):
        last = l == DEPTH_2 - 1
        sh1, sc1, g1, sh2, sc2, g2 = [m[:, None, :] for m in adaln(c, w_mod[l], b_mod[l])]
        csh1, csc1, cg1, csh2, csc2, cg2 = adaln(c_ctx, w_mod[l], b_mod[l])

        def head_groups(attn, hy_in, cf_in):
            hy = hyena_mixer(hy_in, hy_short_w[l], hy_short_b[l], hy_bias_d[l], hy_filt_w1[l], hy_filt_b1[l],
                             hy_filt_freq[l], hy_filt_w2[l], hy_filt_b2[l], hy_filt_w3[l])
            cf = conformer_conv(cf_in, cf_dw_w[l], cf_dw_b[l], cf_ln_g[l], cf_ln_b[l])
            return jnp.concatenate([attn, hy, cf], axis=-1) @ w_out[l]

        h = modulate(rmsnorm(x, norm1_g[l]), sh1, sc1)
        q, k, v, hy_in, cf_in = jnp.split(h @ w_in[l], splits, axis=-1)
        hc = modulate(rmsnorm(xc, norm1_g[l]), csh1, csc1)
        if last:
            kc, vc = jnp.split(hc @ w_in[l][:, D_NA:3 * D_NA], 2, axis=-1)
        else:
            qc, kc, vc, hyc_in, cfc_in = jnp.split(hc @ w_in[l], splits, axis=-1)
        attn = neighbourhood_attention(heads(q), heads(k), heads(v), heads(kc), heads(vc), na_rpb[l])
        x = x + g1 * head_groups(attn, hy_in, cf_in)
        h2 = modulate(rmsnorm(x, norm2_g[l]), sh2, sc2)
        x = x + g2 * expert_choice_ffn(h2, router_w[l], expert_w1[l], expert_w3[l], expert_w2[l])

        if not last:
            attn_c = context_attention(heads(qc), heads(kc), heads(vc))
            xc = xc + cg1 * head_groups(attn_c, hyc_in, cfc_in)
            hc2 = modulate(rmsnorm(xc, norm2_g[l]), csh2, csc2)
            xc = xc + cg2 * expert_choice_ffn(hc2, router_w[l], expert_w1[l], expert_w3[l], expert_w2[l])
    return rmsnorm(x, final_norm_g)


def setup_inputs(seed=0):
    out = dict(first_inputs(seed))
    for name, value in second_inputs(seed + 1).items():
        if name != "x":
            out[name + "_2"] = value
    return out


def reference(
    x, a_norm_g, a_w_in, a_conv_w, a_log, a_dt_bias, a_out_norm_g, a_w_out, kv_norm_g, w_kv,
    b_norm_g, b_w_in, b_w_out, rel_bias, final_norm_g, c_2, ctx_2, c_ctx_2, w_mod_2, b_mod_2,
    norm1_g_2, norm2_g_2, w_in_2, na_rpb_2, hy_short_w_2, hy_short_b_2, hy_filt_w1_2,
    hy_filt_b1_2, hy_filt_freq_2, hy_filt_w2_2, hy_filt_b2_2, hy_filt_w3_2, hy_bias_d_2,
    cf_dw_w_2, cf_dw_b_2, cf_ln_g_2, cf_ln_b_2, w_out_2, router_w_2, expert_w1_2, expert_w3_2,
    expert_w2_2, final_norm_g_2,
):
    x = first_block(
        x, a_norm_g, a_w_in, a_conv_w, a_log, a_dt_bias, a_out_norm_g, a_w_out, kv_norm_g, w_kv,
        b_norm_g, b_w_in, b_w_out, rel_bias, final_norm_g,
    )
    return second_block(
        x, c_2, ctx_2, c_ctx_2, w_mod_2, b_mod_2, norm1_g_2, norm2_g_2, w_in_2, na_rpb_2,
        hy_short_w_2, hy_short_b_2, hy_filt_w1_2, hy_filt_b1_2, hy_filt_freq_2, hy_filt_w2_2,
        hy_filt_b2_2, hy_filt_w3_2, hy_bias_d_2, cf_dw_w_2, cf_dw_b_2, cf_ln_g_2, cf_ln_b_2,
        w_out_2, router_w_2, expert_w1_2, expert_w3_2, expert_w2_2, final_norm_g_2,
    )


_drawn_inputs = setup_inputs


def setup_inputs(seed=0):
    import zlib

    import numpy as np

    out = dict(_drawn_inputs(seed))
    spreads = {}
    factors = {'a_norm_g': 5.617,
     'a_out_norm_g': 8.0,
     'kv_norm_g': 8.0,
     'b_norm_g': 8.0,
     'rel_bias': 3.21,
     'final_norm_g': 5.61,
     'ctx_2': 2.694,
     'b_mod_2': 4.632,
     'norm1_g_2': 8.0,
     'norm2_g_2': 8.0,
     'na_rpb_2': 64.0,
     'hy_short_b_2': 8.0,
     'hy_filt_b1_2': 8.0,
     'hy_filt_freq_2': 8.0,
     'hy_filt_b2_2': 8.0,
     'cf_dw_b_2': 64.0,
     'cf_ln_g_2': 200.0,
     'cf_ln_b_2': 200.0,
     'final_norm_g_2': 25.511}
    for name, (base, spread) in spreads.items():
        noise = np.random.default_rng([zlib.crc32(name.encode()), seed]).standard_normal(out[name].shape)
        drawn = base * np.exp(spread * noise) if base else spread * noise
        out[name] = jnp.asarray(drawn.astype(out[name].dtype))
    for name, factor in factors.items():
        out[name] = (out[name] * factor).astype(out[name].dtype)
    return out
```

```python
from contextlib import ExitStack

import concourse.bass as bass
from concourse import mybir
from concourse.alu_op_type import AluOpType as ALU

F32 = mybir.dt.float32
ACT = mybir.ActivationFunctionType
AX = mybir.AxisListType

P = 128
S = 256
T = S // P
D = 1024
K = D // P
H = 8
EPS = 1e-6
RING = 6
PIECE = 4096
NEXP, CAP, FF = 16, 32, 2048
GROUPS = NEXP // 4
BIG = -1e30

C_ID, C_INC, C_STR, C_ONE, C_LEV = 0, 128, 256, 384, 512
LEVELS = 7
C_IOTA = C_LEV + LEVELS * P
C_COLM = C_IOTA + CAP
C_END = C_COLM + 64

CW = 0
R2 = 96
CFW, CFB, LNG, LNB, HYW, HYB, HYD = R2, R2 + 62, R2 + 64, R2 + 66, R2 + 68, R2 + 86, R2 + 92
R3 = R2 + 96
NCOLS = R3 + 16


def arrays_of_shapes():
    import numpy as np
    import math
    i = np.arange(P)
    c = np.zeros((P, C_END), np.float32)
    c[:, C_ID:C_ID + P] = np.eye(P)
    c[:, C_INC:C_INC + P] = i[:, None] <= i[None, :]
    c[:, C_STR:C_STR + P] = i[:, None] < i[None, :]
    c[:, C_ONE:C_ONE + P] = 1
    for lv in range(LEVELS):
        m = 1 << lv
        c[:, C_LEV + lv * P:C_LEV + (lv + 1) * P] = ((i[:, None] // (2 * m) == i[None, :] // (2 * m))
                                                    & (i[:, None] % (2 * m) < m) & (i[None, :] % (2 * m) >= m))
    c[:, C_IOTA:C_IOTA + CAP] = np.arange(CAP)
    col = np.arange(64)
    c0 = np.clip(col - 8, 0, 48)
    ok = (col[None, :] >= c0[:, None]) & (col[None, :] < c0[:, None] + 16)
    c[:, C_COLM:C_COLM + 64] = np.tile(np.where(ok, 0, BIG)[::-1], (2, 1))
    n = np.arange(256)
    nf = np.maximum(n, 1).astype(np.float32)
    large = 16 + (np.log(nf / np.float32(16)) / np.float32(math.log(2048 / 16)) * np.float32(16)).astype(np.int32)
    bucket = np.where(n < 16, n, np.minimum(large, 31))
    hot = np.zeros((32, 384), np.float32)
    hot[bucket, 255 - n] = 1
    caus = np.zeros((H, 384), np.float32)
    caus[:, 256:] = BIG
    tt, ff = np.arange(S, dtype=np.float64), np.arange(S, dtype=np.float64)
    th = np.pi * (2 * ff[None, :] + 1) * tt[:, None] / 512
    fold = lambda a: a.reshape(T, P, S).transpose(1, 0, 2).reshape(P, T * S)
    dft = np.concatenate([fold(np.cos(th)), fold(np.sin(th)), fold(np.cos(th).T / 256), fold(np.sin(th).T / 256)],
                         axis=1).astype(np.float32)
    pos = np.arange(S, dtype=np.float32)[:, None]
    t = pos / np.float32(255)
    rate = np.abs(np.linspace(math.log(1e-2) / 1.5, math.log(1e-2) / 0.3, 256, dtype=np.float32))
    dec = np.exp(-t * rate)
    decb = dec.copy()
    decb[0] = 0
    dec = np.concatenate([fold(dec), fold(decb)], axis=1).astype(np.float32)
    fb = np.linspace(1e-4, 15, 16, dtype=np.float32)[None, :]
    ang = fb * np.float32(2 * math.pi) * pos / np.float32(256)
    feat = np.concatenate([t, np.cos(ang), -np.sin(ang)], axis=-1).astype(np.float32).T.copy()
    return {"t_const": c, "t_hot": hot, "t_causal": caus, "t_dft": dft, "t_decay": dec, "t_feat": feat}


def program(nc, a, out, dbg=None):
    ctx = ExitStack()
    with ctx:
        def sb(name, shape):
            return ctx.enter_context(nc.sbuf_tensor(name, shape, F32))

        def sem(name):
            return ctx.enter_context(nc.semaphore(name))

        ring = [sb(f"ring{r}", [P, PIECE]) for r in range(RING)]
        slots = sb("slots", [P, 10 * 2048])
        x = sb("x_state", [P, T, D])
        cst = sb("cst", [P, C_END])
        gains = sb("gains", [P, 2 * D])
        small = sb("small", [P, 1100])
        bank = [ctx.enter_context(nc.psum_tensor(f"bank{b}", [P, 512], F32)) for b in range(8)]
        bias_dram = nc.dram_tensor("t5_by_distance", [H, 384], F32, kind="Internal").ap()
        rpb_dram = nc.dram_tensor("rpb_extended", [2, H, 6, P], F32, kind="Internal").ap()
        mod_dram = nc.dram_tensor("modulation", [2, 6 * D], F32, kind="Internal").ap()

        def slot(i, c0=0, c1=2048):
            return slots[:, i * 2048 + c0:i * 2048 + c1]

        def tok(ap):
            return ap.rearrange("p (t d) -> p t d", t=T)

        def chan(ap):
            return ap.rearrange("p (c s) -> p c s", s=S)

        def flipped(ap, n):
            (step, parts), cols_ = ap.ap[0], ap.ap[-1][1]
            assert len(ap.ap) == 2 and ap.ap[-1][0] == 1
            return bass.AP(ap.tensor, ap.offset + n - 1, [[step, parts], [n, cols_ // n], [-1, n]])

        gain_a, gain_b = gains[:, 0:D], gains[:, D:2 * D]
        ident = cst[:, C_ID:C_ID + P]
        incl = cst[:, C_INC:C_INC + P]
        strict = cst[:, C_STR:C_STR + P]
        ones = cst[:, C_ONE:C_ONE + P]
        off = [0]

        def piece_of_small(n):
            off[0] += n
            assert off[0] <= 1100
            return small[:, off[0] - n:off[0]]

        cols = piece_of_small(NCOLS)
        w_ab = piece_of_small(K * 16).rearrange("p (k n) -> p k n", k=K)
        out_g = piece_of_small(P)
        rows1 = piece_of_small(P)
        rows2 = piece_of_small(P)
        rows3 = piece_of_small(P)
        alog = piece_of_small(8)
        dtb = piece_of_small(8)
        eps_c = piece_of_small(1)
        one_c = piece_of_small(1)
        sums = piece_of_small(2)
        devs = piece_of_small(2)
        rstd = piece_of_small(2)
        ab = piece_of_small(32).rearrange("p (t n) -> p t n", t=T)
        ga = piece_of_small(16).rearrange("p (t n) -> p t n", t=T)
        gtmp = piece_of_small(16).rearrange("p (t n) -> p t n", t=T)
        glog = piece_of_small(16).rearrange("p (t n) -> p t n", t=T)
        beta = piece_of_small(16).rearrange("p (t n) -> p t n", t=T)
        gdec = piece_of_small(16).rearrange("p (t n) -> p t n", t=T)
        gcum = piece_of_small(16).rearrange("p (t n) -> p t n", t=T)
        ealog = piece_of_small(8)
        osum = piece_of_small(16)
        orstd = piece_of_small(16)
        hd = piece_of_small(12).rearrange("p (b n) -> p b n", b=2)
        relb = rows1
        filt = piece_of_small(3)
        m8 = piece_of_small(8)

        x_in, const_in, gain_in, small_in = sem("x_in"), sem("const_in"), sem("gain_in"), sem("small_in")
        piece_in = [sem(f"piece_in{r}") for r in range(RING)]
        consts_set = sem("consts_set")
        squares = sem("squares")
        sd_ready = sem("sd_ready")
        rstd_ready = sem("rstd_ready")
        hn_ready = sem("hn_ready")
        turned = sem("turned")
        turned_dve, turned_act = sem("turned_dve"), sem("turned_act")
        rows_turned, cols_ready = sem("rows_turned"), sem("cols_ready")
        unit = sem("unit")
        ab_done, ab_copied, gate_act, gate_ready = sem("ab_done"), sem("ab_copied"), sem("gate_act"), sem("gate_ready")
        ga_ready = sem("ga_ready")
        dve_chain = sem("dve_chain")
        act_chain = sem("act_chain")
        pool_chain = sem("pool_chain")
        conv_done, silu_done, z_ready = sem("conv_done"), sem("silu_done"), sem("z_ready")
        cum_done, cum_copied = sem("cum_done"), sem("cum_copied")
        sq_ready, l2_summed, l2_sd, qk_ready = sem("sq_ready"), sem("l2_summed"), sem("l2_sd"), sem("qk_ready")
        bb_ready, b_turned, kb_ready = sem("bb_ready"), sem("b_turned"), sem("kb_ready")
        v_turned, v_ready = sem("v_turned"), sem("v_ready")
        gb_ready, g_turned = sem("gb_ready"), sem("g_turned")
        pair_a, pair_b = sem("pair_a"), sem("pair_b")
        diff_ready, decay_ready, prod_a, prod_b = sem("diff_ready"), sem("decay_ready"), sem("prod_a"), sem("prod_b")
        mask_ready, y_filled, y_ready = sem("mask_ready"), sem("y_filled"), sem("y_ready")
        inv_filled, x_upd, xt_upd = sem("inv_filled"), sem("x_upd"), sem("xt_upd")
        csilu_ready = sem("csilu_ready")
        bmod_in, mod_added, mod_out = sem("bmod_in"), sem("mod_added"), sem("mod_out")
        solve_filled, v0_ready, r1_ready, v1_ready, o_ready = (sem("solve_filled"), sem("v0_ready"), sem("r1_ready"),
                                                               sem("v1_ready"), sem("o_ready"))
        o_sq, o_ms, o_sd, zg_ready = sem("o_sq"), sem("o_ms"), sem("o_sd"), sem("zg_ready")
        x_added = sem("x_added")
        b_gain_in = sem("b_gain_in")
        t5_filled, t5_row, t5_moved, hot_in = sem("t5_filled"), sem("t5_row"), sem("t5_moved"), sem("hot_in")
        k_copied, v_copied, q_copied, zb_ready = sem("k_copied"), sem("v_copied"), sem("q_copied"), sem("zb_ready")
        scored, biased, maxed, exped, normed = sem("scored"), sem("biased"), sem("maxed"), sem("exped"), sem("normed")
        p_turned, pt_ready, head_out, yt_ready = sem("p_turned"), sem("pt_ready"), sem("head_out"), sem("yt_ready")
        c_load, ctx_in, fin_in = sem("c_load"), sem("ctx_in"), sem("fin_in")
        x3_ready, ctx_normed, cat_ready, zf_used = sem("x3_ready"), sem("ctx_normed"), sem("cat_ready"), sem("zf_used")
        rpb_out, rpb_in = sem("rpb_out"), sem("rpb_in")
        nabias_ready = sem("nabias_ready")
        w_read = sem("w_read")
        w_act = sem("w_act")
        hy_in_ready = sem("hy_in_ready")
        dft_in, filt_in, filt_filled, filt_arg, filt_sin = (sem("dft_in"), sem("filt_in"), sem("filt_filled"),
                                                            sem("filt_arg"), sem("filt_sin"))
        filt_dec, filt_mix, spec_filled, spec_ready = (sem("filt_dec"), sem("filt_mix"), sem("spec_filled"),
                                                       sem("spec_ready"))
        z_turned, zt_ready, zf_filled, yf_ready, hy_filled, hy_ready = (
            sem("z_turned"), sem("zt_ready"), sem("zf_filled"), sem("yf_ready"), sem("hy_filled"), sem("hy_ready"))
        cf_conv, cf_mean, cf_cent, cf_sq, cf_var, cf_sd, cf_n, cf_ready = (
            sem("cf_conv"), sem("cf_mean"), sem("cf_cent"), sem("cf_sq"), sem("cf_var"), sem("cf_sd"), sem("cf_n"),
            sem("cf_ready"))
        router_in, d_load, g1_in, g2_in = (sem("router_in"), sem("d_load"), sem("g1_in"), sem("g2_in"))
        route_filled, route_max, route_exp, aff_ready, aff_turned, top_ready, mask_copied = (
            sem("route_filled"), sem("route_max"), sem("route_exp"), sem("aff_ready"), sem("aff_turned"),
            sem("top_ready"), sem("mask_copied"))
        sel_ready, selg_ready, selg_turned, selgt_ready = (
            sem("sel_ready"), sem("selg_ready"), sem("selg_turned"), sem("selgt_ready"))
        xe_filled, xe_dve, xe_act = sem("xe_filled"), sem("xe_dve"), sem("xe_act")
        xe_static = sem("xe_static")
        xpiece = sem("xpiece")
        gate_silu, act_made, act_turned, actt_ready, y_copied = (sem("gate_silu"), sem("act_made"), sem("act_turned"),
                                                                 sem("actt_ready"), sem("y_copied"))
        comb_filled, final_ready, out_done = sem("comb_filled"), sem("final_ready"), sem("out_done")

        def rows128(w, c0, c1):
            return w[:, c0:c1].rearrange("(k p) n -> p k n", p=P)

        w_a, w_ao, w_kv = a["a_w_in"][0], a["a_w_out"][0], a["w_kv"]
        w_b, w_bo, w_i, w_o, w_m = a["b_w_in"][0], a["b_w_out"][0], a["w_in_2"][0], a["w_out_2"][0], a["w_mod_2"][0]
        pieces = [(rows128(w_a, c, c + 512), 2) for c in range(0, 4096, 512)]
        N_MOD = 12
        pieces += [(rows128(w_m, c, c + 512), 1) for c in range(0, 6 * D, 512)]
        for w, width in ((w_ao, D), (w_kv, 2 * D), (w_b, 2 * D), (w_bo, D)):
            pieces += [(rows128(w, c, c + 512), 2) for c in range(0, width, 512)]
        for c, n in ((0, 2), (512, 4), (1024, 4), (1536, 2), (2048, 2)):
            pieces.append((rows128(w_i, c, c + 512), n))
        pieces.append((rows128(w_i, 2560, 2816), 1))
        pieces += [(rows128(w_o, c, c + 512), 2) for c in (0, 512)]
        NPRE = len(pieces)
        freed_at = []
        for _, n in pieces:
            freed_at.append(n + (freed_at[-1] if freed_at else 0))
        ew1, ew3, ew2 = a["expert_w1_2"][0], a["expert_w3_2"][0], a["expert_w2_2"][0]

        def expert_piece(w, e, j):
            if w is ew2:
                return w[bass.ds(e, 1), 512 * j:512 * j + 512, :].rearrange("o (p b) n -> p (o b) n", p=P)
            return w[bass.ds(e, 1)].rearrange("o (p k) n -> p (o k) n", p=P)[:, 2 * j:2 * j + 2, :]

        NP_ROW = 12
        BODY = 4 * NP_ROW
        assert BODY % RING == 0

        X = slot(0).rearrange("p (n c) -> p n c", c=P)
        XT = slot(1).rearrange("p (n c) -> p n c", c=P)
        kT = chan(slot(2))
        kbq = slots[:, 3 * 2048:5 * 2048].rearrange("p (h r s) -> p h r s", h=H, r=2)
        vtok = slot(5).rearrange("p (t h d) -> p t h d", t=T, h=H)
        zsil = slot(6)
        raw = slots[:, 7 * 2048:10 * 2048]
        pairs = raw.rearrange("p (h n) -> p h n", h=H)
        masked = slot(2).rearrange("p (n c) -> p n c", c=P)
        ybuf = slot(3).rearrange("p (n c) -> p n c", c=P)
        osb = slot(3)
        decay = slots[:, 0:768].rearrange("p (b n) -> p b n", b=2)
        bb = slot(0).rearrange("p (t h c) -> p t h c", t=T, h=H)
        gb = slot(1).rearrange("p (t h c) -> p t h c", t=T, h=H)
        mkT, mv, mqT, mzT, myT = chan(slot(3)), slot(4).rearrange("p (t h d) -> p t h d", t=T, h=H), chan(slot(5)), \
            chan(slot(6)), chan(slot(7))
        t5 = slot(8).rearrange("p (h m) -> p h m", h=H)
        msc = slot(9, 0, 768).rearrange("p (b n) -> p b n", b=2)
        mpt = slot(9, 768, 1536).rearrange("p (b n) -> p b n", b=2)
        nq, nk = chan(slot(3, 0, 1024)), chan(slot(3, 1024))
        nv, nkc = slot(4, 0, 1024).rearrange("p (t n) -> p t n", t=T), chan(slot(4, 1024))
        nvc = slot(5, 0, 1024).rearrange("p (t n) -> p t n", t=T)
        cfa, cfg = chan(slot(5, 1024, 1536)), chan(slot(5, 1536))
        hyu, cfy = chan(slot(6, 0, 1536)), chan(slot(6, 1536))
        catT = chan(slot(7))
        nab = slots[:, 8 * 2048:8 * 2048 + 3072].rearrange("p (h r c) -> p h r c", h=H, r=6)
        dec = slot(9, 1024)
        dft = slot(2).rearrange("p (m t s) -> p m t s", m=4, t=T)
        spec = slot(1).rearrange("p (m f n) -> p m f n", m=2, f=T)
        nsc = slot(0, 0, 1024).rearrange("p (b n) -> p b n", b=2)
        npt = [slot(0, 1024).rearrange("p (k s) -> p k s", k=4), slot(7, 1024).rearrange("p (k s) -> p k s", k=4)]
        zt = slot(0, 0, 512).rearrange("p (t n) -> p t n", t=T)
        yf = slot(0, 512, 1536).rearrange("p (f m n) -> p f m n", f=T, m=2)
        tmp_a = slot(0, 1536).rearrange("p (m n) -> p m n", m=2)
        tmp_b = slot(5, 0, 512).rearrange("p (m n) -> p m n", m=2)
        cfsq, cfsd = slot(9, 1024, 1536), slot(9, 1536, 1792)
        filters = slot(0).rearrange("p (m t n) -> p m t n", m=2, t=T)
        mix = slot(7).rearrange("p (m t n) -> p m t n", m=2, t=T)
        sel = slot(2, 0, 1024).rearrange("p (t n) -> p t n", t=T)
        selgt = slot(2, 1024).rearrange("p (g s) -> p g s", g=GROUPS)
        xet = slots[:, 3 * 2048:5 * 2048].rearrange("p (k n) -> p k n", k=K)
        yexp = slots[:, 5 * 2048:7 * 2048].rearrange("p (g n) -> p g n", g=GROUPS)
        hs = slot(7, 0, 512)
        act = slot(7, 512, 1024)
        actt = slot(7, 1024, 1536).rearrange("p (b n) -> p b n", b=4)
        xe = slot(7, 1536).rearrange("p (b k n) -> p b k n", b=2, k=K)
        router = slot(9, 1024, 2048)
        aff, chosen, pos = (router[:, c:c + 32].rearrange("p (t n) -> p t n", t=T) for c in (0, 32, 64))
        chosen_t, left, aff_t = router[0:16, 96:352], router[0:16, 352:608], router[0:16, 608:864]
        rmax, rsum, rinv = router[:, 864:866], router[:, 866:868], router[:, 868:870]
        selg = slot(8).rearrange("p (t n) -> p t n", t=T)[:, :, 0:512]

        def done_a(s):
            return 4 if s == 0 else 12 * s

        def done_u(s):
            return 8 if s == 0 else 12 * s + 4

        def done_y(s):
            return 12 * s + 20 if s < NEXP - 1 else 12 * s + 12

        block = ctx.enter_context(nc.Block())

        @block.sync
        def _(sp):
            sp.dma_start(x[:], a["x"][0].rearrange("(t p) d -> p t d", p=P)).then_inc(x_in, 16)
            sp.dma_start(gain_a, a["a_norm_g"].to_broadcast([P, D])).then_inc(gain_in, 16)
            sp.dma_start(cst[:], a["t_const"]).then_inc(const_in, 16)
            for n, (src, _) in enumerate(pieces):
                if n >= RING:
                    sp.wait_ge(unit, freed_at[n - RING])
                dst = ring[n % RING][:, 0:src.shape[1] * src.shape[2]].rearrange("p (k n) -> p k n", k=K)
                sp.dma_start(dst, src).then_inc(piece_in[n % RING], 16)

            def expert_step(n, s, first, wait):
                for w, e in ((ew1, s), (ew3, s)) + (() if first else ((ew2, s - 1),)):
                    for j in range(4):
                        wait(n)
                        dst = ring[n % RING][:].rearrange("p (k n) -> p k n", k=4 if w is ew2 else 2)
                        sp.dma_start(dst, expert_piece(w, e, j)).then_inc(piece_in[n % RING], 16)
                        n += 1
                return n

            def wait_static(n):
                if n - RING < NPRE:
                    sp.wait_ge(unit, freed_at[n - RING])
                else:
                    sp.wait_ge(xpiece, n - RING - NPRE + 1)

            n = NPRE
            for s in range(4):
                n = expert_step(n, s, s == 0, wait_static)
            first = n
            with sp.Fori(1, GROUPS) as g:
                n = first
                for q in range(4):
                    n = expert_step(n, g * 4 + q, False,
                                    lambda m: sp.wait_ge(xpiece, (g - 1) * BODY + (m - RING - NPRE + 1)))
            n = first + (GROUPS - 1) * BODY
            for j in range(4):
                wait_static(n)
                sp.dma_start(ring[n % RING][:].rearrange("p (k n) -> p k n", k=4),
                             expert_piece(ew2, NEXP - 1, j)).then_inc(piece_in[n % RING], 16)
                n += 1
            sp.wait_ge(final_ready, T)
            sp.dma_start(out[0].rearrange("(t p) d -> p t d", p=P), x[:]).then_inc(out_done, 16)
            sp.wait_ge(out_done, 16)

        @block.gpsimd
        def _(pool):
            def load(dst, src, s):
                pool.dma_start(dst, src).then_inc(s, 16)

            load(w_ab, w_a[:, 4096:4112].rearrange("(k p) n -> p k n", p=P), small_in)
            load(rows1[0:96, :], a["a_conv_w"][0].rearrange("j (t p) -> (j t) p", p=P), small_in)
            r = 0
            for src in (a["cf_dw_w_2"][0].rearrange("j (t p) -> (j t) p", p=P),
                        a["cf_dw_b_2"][0].rearrange("(t p) -> t p", p=P),
                        a["cf_ln_g_2"][0].rearrange("(t p) -> t p", p=P),
                        a["cf_ln_b_2"][0].rearrange("(t p) -> t p", p=P),
                        a["hy_short_w_2"][0].rearrange("j (t p) -> (j t) p", p=P),
                        a["hy_short_b_2"][0].rearrange("(t p) -> t p", p=P),
                        a["hy_bias_d_2"][0].rearrange("o (t p) -> (o t) p", p=P)):
                load(rows2[r:r + src.shape[0], :], src, small_in)
                r += src.shape[0]
            load(rows3[0:8, :], a["c_2"][0].rearrange("(k p) -> k p", p=P), small_in)
            load(rows3[8:16, :], a["c_ctx_2"].rearrange("(k p) -> k p", p=P), small_in)
            load(alog, a["a_log"].to_broadcast([P, 8]), small_in)
            load(dtb, a["a_dt_bias"].to_broadcast([P, 8]), small_in)
            load(out_g, a["a_out_norm_g"].to_broadcast([P, P]), small_in)
            for i, name in enumerate(("hy_filt_b1_2", "hy_filt_freq_2", "hy_filt_b2_2")):
                load(filt[0:64, i:i + 1], a[name][0].rearrange("(p o) -> p o", o=1), small_in)

            def bmod(m):
                if m >= 2:
                    pool.wait_ge(mod_added, m - 1)
                load(gain_b[0:2, (m % 2) * 512:(m % 2) * 512 + 512],
                     a["b_mod_2"][:, m * 512:m * 512 + 512].to_broadcast([2, 512]), bmod_in)

            bmod(0)
            bmod(1)
            pool.wait_ge(cols_ready, 1)
            load(relb[0:32, 0:8], a["rel_bias"], hot_in)
            for lv in range(LEVELS):
                for g in range(4):
                    if lv == 0:
                        pool.wait_ge(prod_b, 2 * g + 2)
                        if g == 0:
                            pool.wait_ge(pair_b, H)
                    else:
                        pool.wait_ge(y_filled, 4 * (lv - 1) + g + 1)
                    if lv == 1:
                        pool.wait_ge(xt_upd, g + 1)
                    for hh in range(2):
                        src = pairs[:, 2 * g + hh, :].rearrange("p (c n) -> p c n", n=P)[:, 0:5:4, :]
                        m = nc.gpsimd.tensor_tensor(
                            masked[:, 4 * g + 2 * hh:4 * g + 2 * hh + 2, :], src,
                            cst[:, C_LEV + lv * P:C_LEV + (lv + 1) * P].unsqueeze(1).to_broadcast([P, 2, P]), ALU.mult)
                    m.then_inc(mask_ready, 1)
                if lv >= 1:
                    for m in (2 * lv - 2, 2 * lv - 1):
                        pool.wait_ge(mod_added, m + 1)
                        load(mod_dram[:, m * 512:m * 512 + 512], gain_a[0:2, (m % 2) * 512:(m % 2) * 512 + 512], mod_out)
                        if m + 2 < N_MOD:
                            bmod(m + 2)
            pool.wait_ge(small_in, 16 * 17)
            pool.wait_ge(z_ready, 4)
            z3 = zsil.rearrange("p (n d) -> p n d", d=P)
            nc.gpsimd.tensor_tensor(z3, z3, out_g.unsqueeze(1).to_broadcast([P, 16, P]), ALU.mult).then_inc(zg_ready, 1)
            pool.wait_ge(mod_out, 16 * N_MOD)
            load(gain_a, a["kv_norm_g"].rearrange("(o d) -> o d", o=1).to_broadcast([P, D]), b_gain_in)
            load(gain_b, a["b_norm_g"].to_broadcast([P, D]), b_gain_in)
            pool.wait_ge(o_ready, 4)
            load(slot(9, 0, 384)[0:32, :], a["t_hot"], hot_in)
            load(slot(9, 384, 768)[0:8, :], a["t_causal"], hot_in)
            pool.wait_ge(t5_row, 1)
            load(bias_dram, slot(9, 768, 1152)[0:8, :], t5_moved)
            pool.wait_ge(t5_moved, 16)
            load(t5, bass.AP(bias_dram.tensor, 0, [[1, P], [384, H], [1, 256]]), t5_moved)
            zeros = slot(9, 1536, 1664)[0:96, :]
            nc.gpsimd.memset(zeros, 0.0).then_inc(pool_chain, 1)
            pool.wait_ge(pool_chain, 1)
            load(rpb_dram.rearrange("a h r c -> (a h r) c"), zeros, rpb_out)
            pool.wait_ge(rpb_out, 16)
            for half in range(2):
                load(rpb_dram[half, :, :, 48:79], a["na_rpb_2"][0][:, 5 - half:11 - half, :], rpb_out)
            pool.wait_ge(hn_ready, 8)
            load(gain_a, a["final_norm_g"].rearrange("(o d) -> o d", o=1).to_broadcast([P, D]), fin_in)

            def mod_row(dst, who, part, s):
                load(dst, mod_dram[who:who + 1, part * D:(part + 1) * D].to_broadcast([P, D]), s)

            pool.wait_ge(head_out, H)
            pool.wait_ge(yt_ready, H)
            load(slot(5, 0, 1024), a["norm1_g_2"].to_broadcast([P, D]), c_load)
            mod_row(slot(5, 1024), 0, 1, c_load)
            mod_row(slot(6, 0, 1024), 0, 0, c_load)
            mod_row(slot(6, 1024), 1, 1, c_load)
            mod_row(slot(4, 0, 1024), 1, 0, c_load)
            load(tok(slot(3)), a["ctx_2"][0].rearrange("(t p) d -> p t d", p=P), ctx_in)
            pool.wait_ge(rpb_out, 48)
            for half in range(2):
                load(nab[64 * half:64 * half + 64].rearrange("p h r c -> p (h r) c"),
                     bass.AP(rpb_dram.tensor, half * 6 * H * P, [[1, 64], [P, 6 * H], [1, 64]]), rpb_in)
            load(dec, a["t_decay"], filt_in)
            pool.wait_ge(rpb_in, 32)
            n3 = nab.rearrange("p h r c -> p (h r) c")
            nc.gpsimd.tensor_tensor(n3, n3, cst[:, C_COLM:C_COLM + 64].unsqueeze(1).to_broadcast([P, 6 * H, 64]),
                                    ALU.add).then_inc(nabias_ready, 1)
            pool.wait_ge(x3_ready, T)
            load(gain_a[0:64, :], a["hy_filt_w3_2"][0], filt_in)
            load(gain_b[0:33, 0:64], a["hy_filt_w1_2"][0], filt_in)
            load(gain_b[0:64, 64:128], a["hy_filt_w2_2"][0], filt_in)
            load(gain_b[0:33, 128:384], a["t_feat"], filt_in)
            load(w_ab, a["router_w_2"][0].rearrange("(k p) n -> p k n", p=P), router_in)
            pool.wait_ge(unit, freed_at[NPRE - 6])
            load(slot(2), a["t_dft"], dft_in)
            pool.wait_ge(filt_filled, 6)
            mod_row(gain_a, 0, 2, g1_in)
            mod_row(gain_b, 0, 5, g2_in)
            pool.wait_ge(biased, H + 2 * H)
            load(slot(8, 0, 1024), a["norm2_g_2"].to_broadcast([P, D]), d_load)
            mod_row(slot(8, 1024), 0, 4, d_load)
            mod_row(slot(9, 0, 1024), 0, 3, d_load)
            pool.wait_ge(hn_ready, 12)
            load(slot(9, 0, 1024), a["final_norm_g_2"].rearrange("(o d) -> o d", o=1).to_broadcast([P, D]), g2_in)
            pool.wait_ge(xe_dve, 4)
            pool.wait_ge(xe_act, 4)
            for s in range(4):
                if s >= 2:
                    pool.wait_ge(xpiece, done_u(s - 2))
                nc.gpsimd.tensor_copy(xe[:, s % 2], xet[:, :, s * CAP:(s + 1) * CAP]).then_inc(xe_static, 1)
            with pool.Fori(1, GROUPS) as g:
                for q in range(4):
                    pool.wait_ge(xpiece, (g - 1) * BODY + done_u(4 + q - 2))
                    nc.gpsimd.tensor_copy(xe[:, q % 2], xet[:, :, bass.ds(g * 4 * CAP + q * CAP, CAP)]
                                          ).then_inc(xe_static, 1)
            pool.wait_ge(mod_out, 16 * N_MOD)


        @block.tensor
        def _(pe):
            reader = {}

            def fill(b, sem_, count):
                for s_, c_ in reader.get(b, ()):
                    pe.wait_ge(s_, c_)
                reader[b] = ((sem_, count),)
                return bank[b]

            def fill2(b, pairs_):
                bk = fill(b, *pairs_[0])
                reader[b] = tuple(pairs_)
                return bk

            turn_count = [0]

            def turn(src):
                n = turn_count[0]
                turn_count[0] += 1
                for g in range(4):
                    bk = fill(4 + g, (turned_dve, turned_act)[g % 2], 2 * n + g // 2 + 1)
                    for kk in range(2):
                        for t in range(T):
                            k = 2 * g + kk
                            m = pe.transpose(bk[:, kk * S + t * P:kk * S + (t + 1) * P], src[:, t, k * P:(k + 1) * P], ident)
                    m.then_inc(turned, 1)

            units = [0]
            piece = [0]

            def take():
                n = piece[0]
                pe.wait_ge(piece_in[n % RING], 16 * (n // RING + 1))
                piece[0] += 1
                return ring[n % RING]

            def chan_unit(w, c, act_t, sem_, count, ntile=2):
                bk = fill(units[0] % 4, sem_, count)
                for i in range(ntile):
                    for k in range(K):
                        m = pe.matmul(bk[:, i * S:(i + 1) * S], w[:, k, (c + i) * P:(c + i + 1) * P], act_t[:, k, :],
                                      start=(k == 0), stop=(k == K - 1))
                m.then_inc(unit, 1)
                units[0] += 1

            def tok_unit(w, t, act_t, sem_, count):
                bk = fill(units[0] % 4, sem_, count)
                for k in range(K):
                    m = pe.matmul(bk[:], act_t[:, k, t * P:(t + 1) * P], w[:, k, :], start=(k == 0), stop=(k == K - 1))
                m.then_inc(unit, 1)
                units[0] += 1

            def wide(r):
                return r[:].rearrange("p (k n) -> p k n", k=K)

            hT = chan(slot(1))
            pe.wait_ge(const_in, 16)
            pe.wait_ge(small_in, 16 * 17)
            bk = fill(0, cols_ready, 3)
            for rows, nr, c in ((rows1, 96, CW), (rows2, 96, R2), (rows3, 16, R3)):
                m = pe.transpose(bk[:, c:c + nr], rows[0:nr, :], ident[0:nr, 0:nr])
                m.then_inc(rows_turned, 1)
            pe.wait_ge(hn_ready, 2)
            turn(tok(slot(0)))
            pe.wait_ge(turned_dve, 2)
            pe.wait_ge(turned_act, 2)
            bk = fill(4, ab_copied, 1)
            for t in range(T):
                for k in range(K):
                    m = pe.matmul(bk[:, t * 16:(t + 1) * 16], hT[:, k, t * P:(t + 1) * P], w_ab[:, k, :],
                                  start=(k == 0), stop=(k == K - 1))
            m.then_inc(ab_done, 1)
            for n in range(6):
                w = wide(take())
                for c in (0, 2):
                    chan_unit(w, c, hT, conv_done, units[0] + 1)
            for n in range(2):
                w = wide(take())
                for t in range(T):
                    tok_unit(w, t, hT, z_ready, 2 * n + t + 1)
            pe.wait_ge(gate_ready, 1)
            bk = fill(5, cum_copied, 1)
            pe.matmul(bk[:, 0:8], incl, glog[:, 0, :], start=True, stop=True)
            pe.matmul(bk[:, 8:16], incl, glog[:, 1, :], start=True, stop=False)
            pe.matmul(bk[:, 8:16], ones, glog[:, 0, :], start=False, stop=True).then_inc(cum_done, 1)
            for j in range(8):
                pe.wait_ge(sq_ready, j + 1)
                bk = fill(4 + j % 4, l2_sd, j + 1)
                sq = slot(j // 4, (j % 4) * 512, (j % 4) * 512 + 512)
                pe.matmul(bk[:], ones, sq, start=True, stop=True).then_inc(l2_summed, 1)
            for t in range(T):
                for hb in range(2):
                    pe.wait_ge(silu_done, 12)
                    bk = fill(4 + 2 * t + hb, v_ready, 2 * t + hb + 1)
                    for i in range(4):
                        h = 4 * hb + i
                        m = pe.transpose(bk[:, i * P:(i + 1) * P], chan(slot(9))[:, h, t * P:(t + 1) * P], ident)
                    m.then_inc(v_turned, 1)
            pe.wait_ge(bb_ready, 1)
            for j in range(4):
                bk = fill(4 + j, kb_ready, j + 1)
                for hh in range(2):
                    for t in range(T):
                        m = pe.transpose(bk[:, hh * S + t * P:hh * S + (t + 1) * P], bb[:, t, 2 * j + hh, :], ident)
                m.then_inc(b_turned, 1)
            pe.wait_ge(kb_ready, 4)
            pe.wait_ge(gb_ready, 1)
            for h in range(H):
                if h % 2 == 0:
                    bk = fill(4 + (h // 2) % 2, diff_ready, h + 2)
                    for hh in range(2):
                        for t in range(T):
                            m = pe.transpose(bk[:, hh * S + t * P:hh * S + (t + 1) * P], gb[:, t, h + hh, :], ident)
                    m.then_inc(g_turned, 1)
                bk = fill(h % 2, prod_a, h + 1)
                pe.matmul(bk[:], kT[:, h, 0:P], kbq[:, h, :, :], start=True, stop=True).then_inc(pair_a, 1)
                bk = fill(2 + h % 2, prod_b, h + 1)
                pe.matmul(bk[:, 0:S].rearrange("p (r s) -> p r s", r=2), kT[:, h, P:S], kbq[:, h, :, P:S],
                          start=True, stop=True).then_inc(pair_b, 1)
            cT = cols[:, R3:R3 + 16].rearrange("p (w k) -> p w k", w=2)

            def modulation(m):
                w = wide(take())
                bk = fill(units[0] % 2, mod_added, m + 1)
                for k in range(K):
                    q = pe.matmul(bk[0:2, :], cT[:, :, k], w[:, k, :], start=(k == 0), stop=(k == K - 1))
                q.then_inc(unit, 1)
                units[0] += 1

            for lv in range(LEVELS):
                for g in range(4):
                    pe.wait_ge(mask_ready, 4 * lv + g + 1)
                    if lv == 0:
                        bk = fill(4 + g % 2, x_upd, g + 1)
                        for i in range(4):
                            m = pe.transpose(bk[:, i * P:(i + 1) * P], masked[:, 4 * g + i, :], ident)
                        m.then_inc(y_filled, 1)
                        continue
                    pe.wait_ge(x_upd, 4 * (lv - 1) + g + 1)
                    bk = fill(2 + g % 2, y_ready, 4 * (lv - 1) + g + 1)
                    for i in range(4):
                        m = pe.matmul(bk[:, i * P:(i + 1) * P], masked[:, 4 * g + i, :], X[:, 4 * g + i, :],
                                      start=True, stop=True)
                    m.then_inc(y_filled, 1)
                if lv == 0:
                    continue
                for g in range(4):
                    pe.wait_ge(y_ready, 4 * (lv - 1) + g + 1)
                    pe.wait_ge(xt_upd, 4 * (lv - 1) + g + 1)
                    if lv < LEVELS - 1:
                        bk = fill(4 + g % 2, x_upd, 4 * lv + g + 1)
                        for i in range(4):
                            pe.matmul(bk[:, i * P:(i + 1) * P], XT[:, 4 * g + i, :], ybuf[:, 4 * g + i, :],
                                      start=True, stop=True)
                    bk = fill(6 + g % 2, xt_upd, 4 * lv + g + 1)
                    for i in range(4):
                        m = pe.matmul(bk[:, i * P:(i + 1) * P], ybuf[:, 4 * g + i, :], XT[:, 4 * g + i, :],
                                      start=True, stop=True)
                    m.then_inc(inv_filled, 1)
                if lv == 1:
                    pe.wait_ge(csilu_ready, 1)
                modulation(2 * lv - 2)
                modulation(2 * lv - 1)
            pe.wait_ge(v_ready, 4)
            for hb in range(2):
                pe.wait_ge(xt_upd, 4 * (LEVELS - 1) + 2 * hb + 2)
                bk = fill(hb, v0_ready, hb + 1)
                for i in range(4):
                    h = 4 * hb + i
                    m = pe.matmul(bk[:, i * P:(i + 1) * P], XT[:, 2 * h, :], vtok[:, 0, h, :], start=True, stop=True)
                m.then_inc(solve_filled, 1)
            for hb in range(2):
                pe.wait_ge(v0_ready, hb + 1)
                bk = fill(2 + hb, r1_ready, hb + 1)
                for i in range(4):
                    h = 4 * hb + i
                    m = pe.matmul(bk[:, i * P:(i + 1) * P], pairs[:, h, P:2 * P], vtok[:, 0, h, :], start=True, stop=True)
                m.then_inc(solve_filled, 1)
                bk = fill(6 + hb, o_ready, hb + 1)
                for i in range(4):
                    h = 4 * hb + i
                    m = pe.matmul(bk[:, i * P:(i + 1) * P], pairs[:, h, 2 * P:3 * P], vtok[:, 0, h, :],
                                  start=True, stop=True)
                m.then_inc(solve_filled, 1)
            for hb in range(2):
                pe.wait_ge(r1_ready, hb + 1)
                bk = fill(4 + hb, v1_ready, hb + 1)
                for i in range(4):
                    h = 4 * hb + i
                    m = pe.matmul(bk[:, i * P:(i + 1) * P], XT[:, 2 * h + 1, :], vtok[:, 1, h, :], start=True, stop=True)
                m.then_inc(solve_filled, 1)
            for hb in range(2):
                pe.wait_ge(v1_ready, hb + 1)
                bk = fill(hb, o_ready, 3 + hb)
                for i in range(4):
                    h = 4 * hb + i
                    pe.matmul(bk[:, i * P:(i + 1) * P], pairs[:, h, 3 * P:4 * P], vtok[:, 0, h, :], start=True, stop=False)
                    m = pe.matmul(bk[:, i * P:(i + 1) * P], pairs[:, h, 5 * P:6 * P], vtok[:, 1, h, :],
                                  start=False, stop=True)
                m.then_inc(solve_filled, 1)
            pe.wait_ge(hn_ready, 4)
            turn(tok(slot(0)))
            pe.wait_ge(turned_dve, 4)
            pe.wait_ge(turned_act, 4)
            for c in range(2):
                w = wide(take())
                for t in range(T):
                    tok_unit(w, t, chan(slot(2)), x_added, 2 * c + t + 1)
            pe.wait_ge(hot_in, 48)
            bk = fill(5, t5_row, 1)
            pe.matmul(bk[0:8, 0:384], relb[0:32, 0:8], slot(9, 0, 384)[0:32, :], start=True, stop=True).then_inc(t5_filled, 1)
            pe.wait_ge(hn_ready, 6)
            turn(tok(slot(0)))
            kvT, bT = chan(slot(1)), chan(slot(2))
            pe.wait_ge(turned_dve, 6)
            pe.wait_ge(turned_act, 6)
            for n in range(2):
                w = wide(take())
                for c in (0, 2):
                    chan_unit(w, c, kvT, k_copied, 2 * n + c // 2 + 1)
            pe.wait_ge(hn_ready, 8)
            turn(tok(slot(7)))
            for n in range(2):
                w = wide(take())
                for t in range(T):
                    tok_unit(w, t, kvT, v_copied, 2 * n + t + 1)
            pe.wait_ge(turned_dve, 8)
            pe.wait_ge(turned_act, 8)
            for n in range(2):
                w = wide(take())
                for c in (0, 2):
                    chan_unit(w, c, bT, q_copied, 2 * n + c // 2 + 1)
            for n in range(2):
                w = wide(take())
                for c in (0, 2):
                    chan_unit(w, c, bT, zb_ready, 2 * n + c // 2 + 1)

            def m_scores(h):
                bk = fill(4 + h % 2, biased, h + 1)
                pe.matmul(bk[:, 0:S], mqT[:, h, P:S], mkT[:, h, :], start=True, stop=True)
                pe.matmul(bk[:, S:S + P], mqT[:, h, 0:P], mkT[:, h, 0:P], start=True, stop=True).then_inc(scored, 1)

            def m_out(h):
                pe.wait_ge(normed, h + 1)
                bk = fill(6 + h % 2, pt_ready, h + 1)
                p = msc[:, h % 2]
                pe.transpose(bk[:, 0:P], p[:, S:S + P], ident)
                pe.transpose(bk[:, P:S], p[:, 0:P], ident)
                pe.transpose(bk[:, S:S + P], p[:, P:S], ident).then_inc(p_turned, 1)

            def m_values(h):
                pe.wait_ge(pt_ready, h + 1)
                bk = fill(h % 4, yt_ready, h + 1)
                p = mpt[:, h % 2]
                pe.matmul(bk[:, 0:S], mv[:, 0, h, :], p[:, 0:S], start=True, stop=False)
                pe.matmul(bk[:, P:S], mv[:, 1, h, :], p[:, S:S + P], start=False, stop=True).then_inc(head_out, 1)

            pe.wait_ge(k_copied, 4)
            pe.wait_ge(q_copied, 4)
            pe.wait_ge(v_copied, 4)
            for h in range(H + 2):
                if h < H:
                    m_scores(h)
                if 1 <= h <= H:
                    m_out(h - 1)
                if h >= 2:
                    m_values(h - 2)
            pe.wait_ge(yt_ready, H)
            for c in range(2):
                w = wide(take())
                for t in range(T):
                    tok_unit(w, t, myT, x_added, 4 + 2 * c + t + 1)
            pe.wait_ge(ctx_normed, T)
            turn(tok(slot(3)))
            pe.wait_ge(hn_ready, 10 - 0)
            turn(tok(slot(0)))
            nT, cT2 = chan(slot(1)), chan(slot(2))
            pe.wait_ge(turned_dve, 12)
            pe.wait_ge(turned_act, 12)
            w = wide(take())
            for c in (0, 2):
                chan_unit(w, c, nT, w_read, c // 2 + 1)
            w = wide(take())
            for c in (0, 2):
                chan_unit(w, c, nT, w_read, 2 + c // 2 + 1)
            for c in (0, 2):
                chan_unit(w, c, cT2, w_read, 4 + c // 2 + 1)
            w = wide(take())
            for t in range(T):
                tok_unit(w, t, nT, w_act, t + 1)
            for t in range(T):
                tok_unit(w, t, cT2, w_act, 2 + t + 1)
            w = wide(take())
            chan_unit(w, 0, nT, hy_in_ready, 1)
            chan_unit(w, 2, nT, hy_in_ready, 2)
            w = wide(take())
            chan_unit(w, 0, nT, hy_in_ready, 3)
            chan_unit(w, 2, nT, w_act, 5)
            w = take()[:, 0:K * S].rearrange("p (k n) -> p k n", k=K)
            chan_unit(w, 0, nT, w_act, 6)
            w1s, w2s, feat = gain_b[0:33, 0:64], gain_b[0:64, 64:128], gain_b[0:33, 128:384]
            f1, f2 = gain_b[0:64, 384:640], gain_b[0:64, 640:896]
            pe.wait_ge(filt_in, 16 * 5)
            bk = fill(4, filt_arg, 1)
            pe.matmul(bk[0:64, 0:S], w1s, feat, start=True, stop=True).then_inc(filt_filled, 1)
            pe.wait_ge(filt_sin, 1)
            bk = fill(5, filt_arg, 2)
            pe.matmul(bk[0:64, 0:S], w2s, f1, start=True, stop=True).then_inc(filt_filled, 1)
            pe.wait_ge(filt_sin, 2)
            for j in range(T):
                for di in range(2):
                    bk = fill(4 + 2 * j + di, filt_dec, 2 * j + di + 1)
                    pe.matmul(bk[:], f2[:, j * P:(j + 1) * P], gain_a[0:64, di * 512:di * 512 + 512],
                              start=True, stop=True).then_inc(filt_filled, 1)
            pe.wait_ge(filt_mix, 2)
            pe.wait_ge(dft_in, 16)
            for m_ in range(2):
                for f in range(T):
                    bk = fill(4 + 2 * m_ + f, spec_ready, 2 * m_ + f + 1)
                    for j in range(T):
                        q = pe.matmul(bk[:], dft[:, m_, j, f * P:(f + 1) * P], mix[:, m_, j, :],
                                      start=(j == 0), stop=(j == T - 1))
                    q.then_inc(spec_filled, 1)

            def n_scores(i):
                h, t = i // 2, i % 2
                lo = 64 * (h % 2)
                bk = fill(4 + i % 2, biased, H + i + 1)
                q = nq[lo:lo + 64, h // 2, t * P:(t + 1) * P]
                pe.matmul(bk[:, 0:S], q, nk[lo:lo + 64, h // 2, :], start=True, stop=True)
                pe.matmul(bk[:, S:2 * S], q, nkc[lo:lo + 64, h // 2, :], start=True, stop=True).then_inc(scored, 1)

            def n_turn(i):
                pe.wait_ge(normed, H + i + 1)
                bk = fill(6 + i % 2, pt_ready, H + i + 1)
                for kt in range(4):
                    m = pe.transpose(bk[:, kt * P:(kt + 1) * P], nsc[:, i % 2, kt * P:(kt + 1) * P], ident)
                m.then_inc(p_turned, 1)

            def n_values(h):
                lo = 64 * (h % 2)
                pe.wait_ge(pt_ready, H + 2 * h + 2)
                bk = fill((h // 2) % 2 * 2 + h % 2, cat_ready, h + 1)
                for kt in range(4):
                    v = (nv if kt < 2 else nvc)[:, kt % 2, h * 64:h * 64 + 64]
                    m = pe.matmul(bk[lo:lo + 64, 0:S], v, npt[h % 2][:, kt, :], start=(kt == 0), stop=(kt == 3))
                m.then_inc(head_out, 1)

            pe.wait_ge(w_read, 6)
            pe.wait_ge(w_act, 4)
            for i in range(2 * H + 3):
                if i < 2 * H:
                    n_scores(i)
                if 1 <= i <= 2 * H:
                    n_turn(i - 1)
                if i >= 3 and i % 2 == 1:
                    n_values((i - 3) // 2)
            pe.wait_ge(cf_conv, 1)
            bk = fill(4, cf_cent, 1)
            for c in range(2):
                m = pe.matmul(bk[:, 0:S], ones, cfy[:, c, :], start=(c == 0), stop=(c == 1))
            m.then_inc(cf_mean, 1)
            pe.wait_ge(cf_sq, 1)
            bk = fill(4, cf_sd, 1)
            for c in range(2):
                m = pe.matmul(bk[:, 0:S], ones, chan(cfsq)[:, c, :], start=(c == 0), stop=(c == 1))
            m.then_inc(cf_var, 1)
            for o in range(2):
                if o == 0:
                    pe.wait_ge(hy_in_ready, 3)
                    pe.wait_ge(spec_ready, 4)
                else:
                    pe.wait_ge(hy_ready, 1)
                bk = fill(5, zt_ready, o + 1)
                for t in range(T):
                    for c in range(2):
                        m = pe.transpose(bk[:, t * S + c * P:t * S + (c + 1) * P], hyu[:, 4 + c, t * P:(t + 1) * P], ident)
                m.then_inc(z_turned, 1)
                pe.wait_ge(zt_ready, o + 1)
                for f in range(T):
                    bk = fill(6 + f, zf_used, 2 * o + f + 1)
                    for m_ in range(2):
                        for t in range(T):
                            q = pe.matmul(bk[:, m_ * S:(m_ + 1) * S], dft[:, m_, t, f * P:(f + 1) * P],
                                          zt[:, t, :], start=(t == 0), stop=(t == T - 1))
                    q.then_inc(zf_filled, 1)
                pe.wait_ge(yf_ready, 2 * o + 2)
                bk = fill(5, hy_ready, o + 1)
                for c in range(2):
                    n = 0
                    for f in range(T):
                        for m_ in range(2):
                            q = pe.matmul(bk[:, c * S:(c + 1) * S], yf[:, f, m_, c * P:(c + 1) * P],
                                          dft[:, 2 + m_, f, :], start=(n == 0), stop=(n == 3))
                            n += 1
                q.then_inc(hy_filled, 1)
            pe.wait_ge(cat_ready, H)
            pe.wait_ge(hy_ready, 2)
            pe.wait_ge(cf_ready, 2)
            for c in range(2):
                w = wide(take())
                for t in range(T):
                    tok_unit(w, t, catT, x_added, 8 + 2 * c + t + 1)
            pe.wait_ge(hn_ready, 12)
            turn(tok(slot(0)))
            pe.wait_ge(turned_dve, 14)
            pe.wait_ge(turned_act, 14)
            pe.wait_ge(router_in, 16)
            h2T = chan(slot(1))
            bk = fill(4, route_exp, 1)
            for t in range(T):
                for k in range(K):
                    m = pe.matmul(bk[:, t * 16:(t + 1) * 16], h2T[:, k, t * P:(t + 1) * P], w_ab[:, k, :],
                                  start=(k == 0), stop=(k == K - 1))
            m.then_inc(route_filled, 1)
            pe.wait_ge(aff_ready, 1)
            bk = fill(5, top_ready, 1)
            for t in range(T):
                m = pe.transpose(bk[0:16, t * P:(t + 1) * P], aff[:, t, :], ident)
            m.then_inc(aff_turned, 1)
            pe.wait_ge(top_ready, 2)
            bk = fill(6, mask_copied, 1)
            for t in range(T):
                m = pe.transpose(bk[:, t * 16:(t + 1) * 16], chosen_t[0:16, t * P:(t + 1) * P], ident[0:16, 0:16])
            m.then_inc(aff_turned, 1)
            pe.wait_ge(mask_copied, 1)
            bk = fill(7, sel_ready, 1)
            pe.matmul(bk[:, 0:16], strict, chosen[:, 0, :], start=True, stop=True)
            pe.matmul(bk[:, 16:32], strict, chosen[:, 1, :], start=True, stop=False)
            pe.matmul(bk[:, 16:32], ones, chosen[:, 0, :], start=False, stop=True).then_inc(route_filled, 1)
            pe.wait_ge(sel_ready, 2)
            h2 = tok(slot(0)).rearrange("p t (c k) -> p t k c", k=K)
            for k in range(K):
                bk = fill(k % 4, (xe_dve, xe_act)[k % 2], k // 2 + 1)
                for t in range(T):
                    m = pe.matmul(bk[:], h2[:, t, k, :], sel[:, t, :], start=(t == 0), stop=(t == 1))
                m.then_inc(xe_filled, 1)
            for g in range(GROUPS):
                if g == 0:
                    pe.wait_ge(selg_ready, 1)
                bk = fill(4 + g, selgt_ready, g + 1)
                for t in range(T):
                    m = pe.transpose(bk[:, t * P:(t + 1) * P], selg[:, t, g * P:(g + 1) * P], ident)
                m.then_inc(selg_turned, 1)
            for b in range(8):
                for s_, c_ in reader.get(b, ()):
                    pe.wait_ge(s_, c_)

            def wait_piece(n, g):
                c = 16 * (n // RING + 1)
                pe.wait_ge(piece_in[n % RING], c if g is None else (g - 1) * (16 * BODY // RING) + c)

            def at(base, step, g):
                return base if g is None else (g - 1) * step + base

            def wide_product(n, s, bk, g):
                for j in range(4):
                    wait_piece(n + j, g)
                    w = ring[(n + j) % RING][:].rearrange("p (k n) -> p k n", k=2)
                    for kk in range(2):
                        for q in range(4):
                            m = pe.matmul(bk[32 * q:32 * q + 32, :], xe[:, s % 2, 2 * j + kk, :],
                                          w[:, kk, q * 512:q * 512 + 512], start=(j + kk == 0), stop=(j + kk == 4))
                    m.then_inc(xpiece, 1)

            def turn_act(s, g):
                pe.wait_ge(act_made, at(s + 1, 4, g))
                for b in range(4):
                    m = pe.transpose(bank[4][:, b * P:(b + 1) * P],
                                     act.rearrange("p (c b) -> p b c", b=4)[:, b, :], ident)
                m.then_inc(act_turned, 1)

            def narrow_product(n, s, g):
                pe.wait_ge(actt_ready, at(s + 1, 4, g))
                if s >= 4 or g is not None:
                    pe.wait_ge(y_copied, at(s - 2, 4, g))
                q = s % 4
                for j in range(4):
                    wait_piece(n + j, g)
                    w = ring[(n + j) % RING][:].rearrange("p (k n) -> p k n", k=4)
                    for b in range(4):
                        for half in range(2):
                            m = pe.matmul(bank[5 + half][32 * q:32 * q + 32, :], actt[:, b, 32 * j:32 * j + 32],
                                          w[:, b, half * 512:half * 512 + 512],
                                          start=(j + b == 0), stop=(j + b == 6))
                    m.then_inc(xpiece, 1)

            def expert_step(n, s, g):
                pe.wait_ge(xe_static, at(s + 1, 4, g))
                if s >= 2:
                    pe.wait_ge(gate_silu, at(s - 1, 4, g))
                wide_product(n, s, bank[s % 2], g)
                if s >= 1:
                    turn_act(s - 1, g)
                if s >= 2:
                    pe.wait_ge(act_made, at(s - 1, 4, g))
                wide_product(n + 4, s, bank[2 + s % 2], g)
                if s >= 1:
                    narrow_product(n + 8, s - 1, g)
                return n + (8 if s == 0 else NP_ROW)

            n = NPRE
            for s in range(4):
                n = expert_step(n, s, None)
            with pe.Fori(1, GROUPS) as g:
                m_ = n
                for q in range(4):
                    m_ = expert_step(m_, 4 + q, g)
            n += (GROUPS - 1) * BODY
            turn_act(NEXP - 1, None)
            narrow_product(n, NEXP - 1, None)
            pe.wait_ge(y_copied, NEXP)
            for t in range(T):
                for half in range(2):
                    bk = bank[2 * t + half]
                    for g in range(GROUPS):
                        m = pe.matmul(bk[:], selgt[:, g, t * P:(t + 1) * P], yexp[:, g, half * 512:half * 512 + 512],
                                      start=(g == 0), stop=(g == GROUPS - 1))
                    m.then_inc(comb_filled, 1)

        @block.scalar
        def _(act_e):
            w_ = act_e.wait_ge

            def f(dst, src, func, **kw):
                return nc.scalar.activation(dst, src, func, **kw)

            def stats(n, src, junk):
                if n:
                    w_(rstd_ready, n)
                for t in range(T):
                    f(junk[:, t, :], src[:, t, :], ACT.Square, accum_out=sums[:, t:t + 1]).then_inc(squares, 1)
                w_(squares, T * (n + 1))
                f(devs, sums, ACT.Sqrt, bias=eps_c, scale=1.0 / D).then_inc(sd_ready, 1)

            def turned_copies(n, dst):
                for g in (1, 3):
                    w_(turned, 4 * n + g + 1)
                    f(dst[:, g * 512:(g + 1) * 512], bank[4 + g][:], ACT.Copy).then_inc(turned_act, 1)

            w_(consts_set, 1)
            w_(x_in, 16)
            stats(0, x, tok(slot(0)))
            turned_copies(0, slot(1))
            w_(small_in, 16 * 17)
            w_(ga_ready, 1)
            f(gtmp, ga, ACT.Abs).then_inc(act_chain, 1)
            w_(act_chain, 1)
            f(gtmp, gtmp, ACT.Exp, scale=-1.0).then_inc(act_chain, 1)
            f(ealog, alog, ACT.Exp)
            f(beta, ab[:, :, 8:16], ACT.Exp, scale=-1.0)
            w_(act_chain, 2)
            f(gtmp, gtmp, ACT.Ln, bias=one_c).then_inc(gate_act, 1)
            for u in range(12):
                w_(conv_done, u + 1)
                q = raw[:, u * 512:(u + 1) * 512]
                f(q, q, ACT.Silu).then_inc(silu_done, 1)
            for n in range(2):
                for t in range(T):
                    w_(unit, 12 + 2 * n + t + 1)
                    f(tok(zsil)[:, t, n * 512:(n + 1) * 512], bank[(2 * n + t) % 4][:], ACT.Silu).then_inc(z_ready, 1)
            w_(cols_ready, 3)
            f(cols[:, R3:R3 + 16], cols[:, R3:R3 + 16], ACT.Silu).then_inc(csilu_ready, 1)
            for j in range(8):
                w_(silu_done, j + 1)
                f(slot(j // 4, (j % 4) * 512, (j % 4) * 512 + 512), raw[:, j * 512:(j + 1) * 512],
                  ACT.Square).then_inc(sq_ready, 1)
            for j in range(8):
                w_(l2_summed, j + 1)
                f(slot(j // 4, (j % 4) * 512, (j % 4) * 512 + 512), bank[4 + j % 4][:], ACT.Sqrt,
                  bias=eps_c).then_inc(l2_sd, 1)
            for h in range(H):
                w_(diff_ready, h + 1)
                f(decay[:, h % 2], decay[:, h % 2], ACT.Exp).then_inc(decay_ready, 1)
            for lv in range(1, LEVELS):
                for g in range(4):
                    w_(y_filled, 4 * lv + g + 1)
                    f(slot(3, g * 512, (g + 1) * 512), bank[2 + g % 2][:], ACT.Copy).then_inc(y_ready, 1)
            v2, o2 = tok(slot(5)), tok(osb)
            for hb in range(2):
                w_(solve_filled, hb + 1)
                f(v2[:, 0, hb * 512:(hb + 1) * 512], bank[hb][:], ACT.Copy).then_inc(v0_ready, 1)
            for hb in range(2):
                w_(solve_filled, 4 + 2 * hb)
                f(o2[:, 0, hb * 512:(hb + 1) * 512], bank[6 + hb][:], ACT.Copy).then_inc(o_ready, 1)
            for hb in range(2):
                w_(solve_filled, 7 + hb)
                f(v2[:, 1, hb * 512:(hb + 1) * 512], bank[4 + hb][:], ACT.Copy).then_inc(v1_ready, 1)
            for hb in range(2):
                w_(solve_filled, 9 + hb)
                f(o2[:, 1, hb * 512:(hb + 1) * 512], bank[hb][:], ACT.Copy).then_inc(o_ready, 1)
            w_(o_ready, 4)
            f(slot(4), osb, ACT.Square).then_inc(o_sq, 1)
            w_(o_ms, 1)
            f(osum, osum, ACT.Sqrt, bias=eps_c, scale=1.0 / P).then_inc(o_sd, 1)
            turned_copies(1, slot(2))
            w_(x_added, 4)
            stats(1, x, tok(slot(0)))
            turned_copies(2, slot(1))

            def unit_copy(u, dst, sem_, func=ACT.Copy):
                w_(unit, u + 1)
                f(dst, bank[u % 4][:], func).then_inc(sem_, 1)

            def blocks(ap, n):
                return ap.rearrange("p (b n) -> p b n", n=n)

            for j in range(4):
                unit_copy(32 + j, slot(3, j * 512, (j + 1) * 512), k_copied)
            turned_copies(3, slot(2))
            for j in range(4):
                w_(unit, 40 + j + 1)
                f(blocks(slot(5, j * 512, (j + 1) * 512), P), flipped(bank[(40 + j) % 4][:], P),
                  ACT.Copy).then_inc(q_copied, 1)
            for j in range(4):
                unit_copy(44 + j, slot(6, j * 512, (j + 1) * 512), zb_ready, ACT.Silu)
            for h in range(H + 1):
                if h < H:
                    b = h % 2
                    w_(maxed, h + 1)
                    f(msc[:, b, 0:S], msc[:, b, 0:S], ACT.Exp, bias=hd[:, b, 0:1], accum_out=hd[:, b, 2:3])
                    f(msc[:, b, S:S + P], msc[:, b, S:S + P], ACT.Exp, bias=hd[:, b, 1:2],
                      accum_out=hd[:, b, 3:4]).then_inc(exped, 1)
                if h >= 1:
                    w_(p_turned, h)
                    if h >= 3:
                        w_(head_out, h - 2)
                    f(blocks(mpt[:, (h - 1) % 2], P), flipped(bank[6 + (h - 1) % 2][:, 0:384], P), ACT.Copy).then_inc(pt_ready, 1)
            w_(ctx_in, 16)
            stats(2, tok(slot(3)), tok(slot(0)))
            w_(x_added, 8)
            stats(3, x, tok(slot(0)))
            w_(x3_ready, T)
            stats(4, x, tok(slot(0)))
            turned_copies(4, slot(2))
            turned_copies(5, slot(1))
            for j in range(2):
                unit_copy(58 + j, slot(4, j * 512, (j + 1) * 512), w_act)
            for j in range(2):
                unit_copy(60 + j, slot(5, j * 512, (j + 1) * 512), w_act)
            unit_copy(65, slot(5, 1024, 1536), w_act)
            unit_copy(66, slot(5, 1536), w_act, ACT.Sigmoid)
            w1, w2 = gain_b[0:64, 384:640], gain_b[0:64, 640:896]
            for i, v in enumerate((w1, w2)):
                w_(filt_arg, i + 1)
                f(v, v, ACT.Sin).then_inc(filt_sin, 1)
            for i in range(4):
                w_(spec_filled, i + 1)
                f(spec[:, i // 2, i % 2, :], bank[4 + i][:], ACT.Copy).then_inc(spec_ready, 1)
            for i in range(2 * H + 1):
                if i < 2 * H:
                    b = i % 2
                    w_(maxed, H + i + 1)
                    f(nsc[:, b], nsc[:, b], ACT.Exp, bias=hd[:, b, 0:1], accum_out=hd[:, b, 2:3]).then_inc(exped, 1)
                if i >= 1:
                    h, t = (i - 1) // 2, (i - 1) % 2
                    w_(p_turned, H + i)
                    if h >= 2:
                        w_(head_out, H + h - 1)
                    f(npt[h % 2][:, :, t * P:(t + 1) * P].rearrange("p k (b n) -> p k b n", n=64),
                      flipped(bank[6 + t][:], 64).rearrange("p (k b) n -> p k b n", k=4),
                      ACT.Copy).then_inc(pt_ready, 1)
            w_(cf_cent, 2)
            f(cfsq, slot(6, 1536), ACT.Square).then_inc(cf_sq, 1)
            w_(cf_var, 1)
            f(cfsd, bank[4][:, 0:S], ACT.Sqrt, bias=eps_c, scale=1.0 / S).then_inc(cf_sd, 1)
            w_(head_out, 2 * H)
            for o in range(2):
                w_(z_turned, o + 1)
                f(slot(0, 0, 512), bank[5][:], ACT.Copy).then_inc(zt_ready, 1)
            w_(cf_n, 1)
            for c in range(2):
                f(catT[:, 6 + c, :], cfy[:, c, :], ACT.Silu, scale=cols[:, LNG + c:LNG + c + 1],
                  bias=cols[:, LNB + c:LNB + c + 1]).then_inc(cf_ready, 1)
            w_(x_added, 12)
            stats(5, x, tok(slot(0)))
            turned_copies(6, slot(1))
            w_(route_max, 1)
            for t in range(T):
                m = f(aff[:, t, :], bank[4][:, t * 16:(t + 1) * 16], ACT.Exp, bias=rmax[:, t:t + 1],
                      accum_out=rsum[:, t:t + 1])
            m.then_inc(route_exp, 1)
            for k in (1, 3, 5, 7):
                w_(xe_filled, k + 1)
                f(xet[:, k, :], bank[k % 4][:], ACT.Copy).then_inc(xe_act, 1)
            for g in range(GROUPS):
                w_(selg_turned, g + 1)
                f(selgt[:, g, :], bank[4 + g][:, 0:S], ACT.Copy).then_inc(selgt_ready, 1)

            def step(s, g):
                def at(base, stride):
                    return base if g is None else (g - 1) * stride + base
                w_(xpiece, at(done_a(s), BODY))
                if s >= 1:
                    w_(act_made, at(s, 4))
                f(hs, bank[s % 2][:], ACT.Silu).then_inc(gate_silu, 1)
                if s >= 1:
                    w_(act_turned, at(s, 4))
                    if s >= 2:
                        w_(xpiece, at(done_y(s - 2), BODY))
                    f(slot(7, 1024, 1536), bank[4][:], ACT.Copy).then_inc(actt_ready, 1)

            for s in range(4):
                step(s, None)
            with act_e.Fori(1, GROUPS) as g:
                for q in range(4):
                    step(4 + q, g)
            w_(act_turned, NEXP)
            w_(xpiece, done_y(NEXP - 2))
            f(slot(7, 1024, 1536), bank[4][:], ACT.Copy).then_inc(actt_ready, 1)
            w_(x_added, 16)
            stats(6, x, tok(slot(0)))

        @block.vector
        def _(dve):
            v = nc.vector
            w_ = dve.wait_ge
            steps = [0]

            def link(ins):
                ins.then_inc(dve_chain, 1)
                steps[0] += 1
                w_(dve_chain, steps[0])

            def stt(dst, a_, s_, b_, op0=ALU.mult, op1=ALU.mult):
                return v.scalar_tensor_tensor(dst, a_, s_, b_, op0, op1)

            def invert(n):
                w_(sd_ready, n + 1)
                v.reciprocal(rstd, devs).then_inc(rstd_ready, 1)
                w_(rstd_ready, n + 1)

            def turned_copies(n, dst):
                for g in (0, 2):
                    w_(turned, 4 * n + g + 1)
                    v.tensor_copy(dst[:, g * 512:(g + 1) * 512], bank[4 + g][:]).then_inc(turned_dve, 1)

            v.memset(eps_c, EPS)
            v.memset(one_c, 1.0).then_inc(consts_set, 1)
            h0 = tok(slot(0))
            invert(0)
            w_(gain_in, 16)
            for t in range(T):
                stt(h0[:, t, :], x[:, t, :], rstd[:, t:t + 1], gain_a).then_inc(hn_ready, 1)
            for i, (c, n) in enumerate(((CW, 96), (R2, 96), (R3, 16))):
                w_(rows_turned, 3)
                v.tensor_copy(cols[:, c:c + n], bank[0][:, c:c + n]).then_inc(cols_ready, 1)
            turned_copies(0, slot(1))
            w_(ab_done, 1)
            v.tensor_copy(ab, bank[4][:, 0:32].rearrange("p (t n) -> p t n", t=T)).then_inc(ab_copied, 1)
            w_(ab_copied, 1)
            w_(small_in, 16 * 17)
            v.tensor_tensor(ga, ab[:, :, 0:8], dtb.unsqueeze(1).to_broadcast([P, T, 8]), ALU.add).then_inc(ga_ready, 1)
            w_(ga_ready, 1)
            w_(cols_ready, 1)

            def taps(u):
                w_(unit, u + 1)
                src = chan(bank[u % 4][:])
                dst = chan(raw[:, u * 512:(u + 1) * 512])
                for j in (3, 2, 1, 0):
                    sh = 3 - j
                    for i in range(2):
                        wt = cols[:, CW + 24 * j + 2 * u + i:CW + 24 * j + 2 * u + i + 1]
                        if j == 3:
                            m = v.tensor_scalar(dst[:, i, :], src[:, i, :], wt, None, ALU.mult)
                        else:
                            m = stt(dst[:, i, sh:], src[:, i, 0:S - sh], wt, dst[:, i, sh:], op1=ALU.add)
                    if j:
                        link(m)
                m.then_inc(conv_done, 1)

            taps(0)
            w_(gate_act, 1)
            link(stt(gtmp, ga, 0.0, gtmp, ALU.max, ALU.add))
            stt(glog, gtmp, -1.0, ealog.unsqueeze(1).to_broadcast([P, T, 8])).then_inc(gate_ready, 1)
            link(v.tensor_scalar(beta, beta, 1.0, None, ALU.add))
            link(v.reciprocal(beta, beta))
            for u in range(1, 12):
                taps(u)
            w_(cum_done, 1)
            v.tensor_copy(gcum, bank[5][:, 0:16].rearrange("p (t n) -> p t n", t=T)).then_inc(cum_copied, 1)
            w_(cum_copied, 1)
            for j in range(8):
                w_(l2_sd, j + 1)
                r = slot(j // 4, (j % 4) * 512, (j % 4) * 512 + 512)
                link(v.reciprocal(r, r))
                q = raw[:, j * 512:(j + 1) * 512]
                if j < 4:
                    stt(kbq[:, 2 * j:2 * j + 2, 1, :], chan(q), float(P) ** -0.5, chan(r)).then_inc(qk_ready, 1)
                else:
                    v.tensor_tensor(slot(2, (j - 4) * 512, (j - 3) * 512), q, r, ALU.mult).then_inc(qk_ready, 1)
            w_(qk_ready, 8)
            v.tensor_copy(slot(0).rearrange("p (n c) -> p n c", c=P),
                          beta.rearrange("p t n -> p (t n)").unsqueeze(2).to_broadcast([P, 16, P])).then_inc(bb_ready, 1)
            for t in range(T):
                for hb in range(2):
                    w_(v_turned, 2 * t + hb + 1)
                    v.tensor_tensor(vtok[:, t, 4 * hb:4 * hb + 4, :],
                                    bank[4 + 2 * t + hb][:].rearrange("p (h d) -> p h d", h=4),
                                    beta[:, t, 4 * hb:4 * hb + 4].unsqueeze(2).to_broadcast([P, 4, P]),
                                    ALU.mult).then_inc(v_ready, 1)
            v.tensor_copy(slot(1).rearrange("p (n c) -> p n c", c=P),
                          gcum.rearrange("p t n -> p (t n)").unsqueeze(2).to_broadcast([P, 16, P])).then_inc(gb_ready, 1)
            for j in range(4):
                w_(b_turned, j + 1)
                v.tensor_tensor(kbq[:, 2 * j:2 * j + 2, 0, :], kT[:, 2 * j:2 * j + 2, :], chan(bank[4 + j][:]),
                                ALU.mult).then_inc(kb_ready, 1)

            def differences(h):
                w_(g_turned, h // 2 + 1)
                if h >= 2:
                    w_(prod_b, h - 1)
                row = bank[4 + (h // 2) % 2][:, (h % 2) * S:(h % 2) * S + S]
                v.tensor_scalar(decay[:, h % 2, 0:S], row, gcum[:, 0, h:h + 1], 0.0, ALU.subtract, ALU.min)
                v.tensor_scalar(decay[:, h % 2, S:S + P], row[:, P:S], gcum[:, 1, h:h + 1], 0.0, ALU.subtract,
                                ALU.min).then_inc(diff_ready, 1)

            differences(0)
            for h in range(H):
                if h + 1 < H:
                    differences(h + 1)
                w_(decay_ready, h + 1)
                e = decay[:, h % 2]
                v.tensor_tensor(e[:, 0:P], e[:, 0:P], incl, ALU.mult)
                link(v.tensor_tensor(e[:, S:S + P], e[:, S:S + P], incl, ALU.mult))
                w_(pair_a, h + 1)
                v.tensor_tensor(chan(pairs[:, h, 0:512]), chan(bank[h % 2][:]), e[:, 0:S].unsqueeze(1).to_broadcast(
                    [P, 2, S]), ALU.mult).then_inc(prod_a, 1)
                w_(pair_b, h + 1)
                v.tensor_tensor(pairs[:, h, 512:768].rearrange("p (m n) -> p m n", m=2),
                                bank[2 + h % 2][:, 0:S].rearrange("p (m n) -> p m n", m=2),
                                e[:, S:S + P].unsqueeze(1).to_broadcast([P, 2, P]), ALU.mult).then_inc(prod_b, 1)
            w_(prod_b, H)
            idb = ident.unsqueeze(1).to_broadcast([P, 4, P])
            for lv in range(LEVELS):
                for g in range(4):
                    sl = slice(4 * g, 4 * g + 4)
                    bk = bank[4 + g % 2][:].rearrange("p (n c) -> p n c", n=4)
                    if lv == 0:
                        w_(mask_ready, g + 1)
                        v.tensor_tensor(XT[:, sl, :], idb, masked[:, sl, :], ALU.subtract).then_inc(xt_upd, 1)
                        w_(y_filled, g + 1)
                        v.tensor_tensor(X[:, sl, :], idb, bk, ALU.subtract).then_inc(x_upd, 1)
                        continue
                    w_(inv_filled, 4 * (lv - 1) + g + 1)
                    w_(x_upd, 4 * (lv - 1) + g + 1 if lv < LEVELS - 1 else 4 * (LEVELS - 1))
                    w_(xt_upd, 4 * (lv - 1) + g + 1)
                    if lv < LEVELS - 1:
                        v.tensor_tensor(X[:, sl, :], X[:, sl, :], bk, ALU.subtract).then_inc(x_upd, 1)
                    bk = bank[6 + g % 2][:].rearrange("p (n c) -> p n c", n=4)
                    v.tensor_tensor(XT[:, sl, :], XT[:, sl, :], bk, ALU.subtract).then_inc(xt_upd, 1)
                if lv:
                    for m in (2 * lv - 2, 2 * lv - 1):
                        w_(unit, 16 + m + 1)
                        w_(bmod_in, 16 * min(m + 2, N_MOD))
                        if m >= 2:
                            w_(mod_out, 16 * m if m < N_MOD else 0)
                        b = m % 2
                        v.tensor_tensor(gain_a[0:2, b * 512:b * 512 + 512], bank[b][0:2, :],
                                        gain_b[0:2, b * 512:b * 512 + 512], ALU.add).then_inc(mod_added, 1)
            for hb in range(2):
                w_(solve_filled, 3 + 2 * hb)
                r = tok(slot(5))[:, 1, hb * 512:(hb + 1) * 512]
                v.tensor_tensor(r, r, bank[2 + hb][:], ALU.subtract).then_inc(r1_ready, 1)
            w_(o_sq, 1)
            v.tensor_reduce(osum, slot(4).rearrange("p (n d) -> p n d", d=P), AX.X, ALU.add).then_inc(o_ms, 1)
            w_(o_sd, 1)
            link(v.reciprocal(orstd, osum))
            o3 = osb.rearrange("p (n d) -> p n d", d=P)
            link(v.tensor_tensor(o3, o3, orstd.unsqueeze(2).to_broadcast([P, 16, P]), ALU.mult))
            w_(zg_ready, 1)
            for t in range(T):
                v.tensor_tensor(h0[:, t, :], tok(osb)[:, t, :], tok(zsil)[:, t, :], ALU.mult).then_inc(hn_ready, 1)
            turned_copies(1, slot(2))

            def add_units(u0):
                for c in range(2):
                    for t in range(T):
                        u = u0 + 2 * c + t
                        w_(unit, u + 1)
                        q = x[:, t, c * 512:(c + 1) * 512]
                        v.tensor_tensor(q, q, bank[u % 4][:], ALU.add).then_inc(x_added, 1)

            add_units(28)
            w_(t5_filled, 1)
            w_(hot_in, 48)
            v.tensor_tensor(slot(9, 768, 1152)[0:8, :], bank[5][0:8, 0:384], slot(9, 384, 768)[0:8, :],
                            ALU.add).then_inc(t5_row, 1)
            invert(1)
            w_(b_gain_in, 32)
            w_(x_added, 4)
            for t in range(T):
                stt(h0[:, t, :], x[:, t, :], rstd[:, t:t + 1], gain_a).then_inc(hn_ready, 1)
            for t in range(T):
                stt(tok(slot(7))[:, t, :], x[:, t, :], rstd[:, t:t + 1], gain_b).then_inc(hn_ready, 1)
            turned_copies(2, slot(1))
            turned_copies(3, slot(2))
            for j in range(4):
                w_(unit, 36 + j + 1)
                v.tensor_copy(tok(slot(4))[:, j % 2, (j // 2) * 512:(j // 2) * 512 + 512], bank[(36 + j) % 4][:]
                              ).then_inc(v_copied, 1)
            w_(t5_moved, 32)
            w_(zb_ready, 4)
            sc = float(P) ** -0.5
            for h in range(H + 2):
                if h < H:
                    b = h % 2
                    w_(scored, h + 1)
                    if h >= 2:
                        w_(p_turned, h - 1)
                        w_(normed, h - 1)
                    bk = bank[4 + b]
                    stt(msc[:, b, 0:S], bk[:, 0:S], sc, t5[:, h, :], op1=ALU.add)
                    stt(msc[:, b, S:S + P], bk[:, S:S + P], sc, t5[:, h, P:S], op1=ALU.add).then_inc(biased, 1)
                    w_(biased, h + 1)
                    v.tensor_reduce(hd[:, b, 0:1], msc[:, b, 0:S], AX.X, ALU.max, negate=True)
                    v.tensor_reduce(hd[:, b, 1:2], msc[:, b, S:S + P], AX.X, ALU.max, negate=True).then_inc(maxed, 1)
                if 1 <= h <= H:
                    b = (h - 1) % 2
                    w_(exped, h)
                    link(v.reciprocal(hd[:, b, 4:6], hd[:, b, 2:4]))
                    v.tensor_scalar(msc[:, b, 0:S], msc[:, b, 0:S], hd[:, b, 4:5], None, ALU.mult)
                    v.tensor_scalar(msc[:, b, S:S + P], msc[:, b, S:S + P], hd[:, b, 5:6], None,
                                    ALU.mult).then_inc(normed, 1)
                if h >= 2:
                    w_(head_out, h - 1)
                    v.tensor_tensor(myT[:, h - 2, :], bank[(h - 2) % 4][:, 0:S], mzT[:, h - 2, :],
                                    ALU.mult).then_inc(yt_ready, 1)
            w_(c_load, 16 * 5)
            stt(slot(6, 1024), slot(6, 1024), 1.0, slot(5, 0, 1024), ALU.add)
            link(stt(slot(5, 1024), slot(5, 1024), 1.0, slot(5, 0, 1024), ALU.add))
            invert(2)
            c3 = tok(slot(3))
            for t in range(T):
                link(stt(c3[:, t, :], c3[:, t, :], rstd[:, t:t + 1], slot(6, 1024)))
                v.tensor_tensor(c3[:, t, :], c3[:, t, :], slot(4, 0, 1024), ALU.add).then_inc(ctx_normed, 1)
            add_units(48)
            invert(3)
            w_(fin_in, 16)
            w_(x_added, 8)
            for t in range(T):
                stt(x[:, t, :], x[:, t, :], rstd[:, t:t + 1], gain_a).then_inc(x3_ready, 1)
            invert(4)
            w_(x3_ready, T)
            for t in range(T):
                link(stt(h0[:, t, :], x[:, t, :], rstd[:, t:t + 1], slot(5, 1024)))
                v.tensor_tensor(h0[:, t, :], h0[:, t, :], slot(6, 0, 1024), ALU.add).then_inc(hn_ready, 1)
            turned_copies(4, slot(2))
            turned_copies(5, slot(1))
            for j, dst in enumerate((slot(3, 0, 512), slot(3, 512, 1024), slot(3, 1024, 1536), slot(3, 1536),
                                     slot(4, 1024, 1536), slot(4, 1536))):
                w_(unit, 52 + j + 1)
                src = bank[(52 + j) % 4][:]
                if j < 2:
                    dst, src = dst.rearrange("p (b n) -> p b n", n=64), flipped(src, 64)
                v.tensor_copy(dst, src).then_inc(w_read, 1)
            for n, u in enumerate((62, 63, 64)):
                w_(unit, u + 1)
                src, dst = chan(bank[u % 4][:]), hyu[:, 2 * n:2 * n + 2, :]
                for j in (1, 0, 2):
                    for i in range(2):
                        c = 2 * n + i
                        wt = cols[:, HYW + 6 * j + c:HYW + 6 * j + c + 1]
                        if j == 1:
                            m = v.tensor_scalar(dst[:, i, :], src[:, i, :], wt, cols[:, HYB + c:HYB + c + 1],
                                                ALU.mult, ALU.add)
                        elif j == 0:
                            m = stt(dst[:, i, 1:], src[:, i, 0:S - 1], wt, dst[:, i, 1:], op1=ALU.add)
                        else:
                            m = stt(dst[:, i, 0:S - 1], src[:, i, 1:], wt, dst[:, i, 0:S - 1], op1=ALU.add)
                    if j != 2:
                        link(m)
                m.then_inc(hy_in_ready, 1)
            import math
            two_pi = 2 * math.pi
            p1 = 6.28125
            p2 = float(int((two_pi - p1) * 2 ** 22)) / 2 ** 22
            p3 = two_pi - p1 - p2
            magic = 1.5 * 2 ** 23
            turns = slot(7, 0, S)[0:64, :]
            w_(filt_in, 16 * 5)
            for i, (dst, bias) in enumerate(((gain_b[0:64, 384:640], 0), (gain_b[0:64, 640:896], 2))):
                w_(filt_filled, i + 1)
                link(v.tensor_scalar(dst, bank[4 + i][0:64, 0:S], filt[0:64, bias:bias + 1], filt[0:64, 1:2],
                                     ALU.add, ALU.mult))
                link(v.tensor_scalar(turns, dst, 1 / two_pi, magic, ALU.mult, ALU.add))
                link(v.tensor_scalar(turns, turns, magic, None, ALU.subtract))
                for p in (p1, p2, p3):
                    link(stt(dst, turns, -p, dst, op1=ALU.add))
                v.tensor_scalar(dst, dst, 3.1415925, -3.1415925, ALU.min, ALU.max).then_inc(filt_arg, 1)
            dec4 = dec.rearrange("p (m t n) -> p m t n", m=2, t=T)
            for j in range(T):
                for di in range(2):
                    w_(filt_filled, 2 + 2 * j + di + 1)
                    v.tensor_tensor(chan(filters[:, di, j, :]), chan(bank[4 + 2 * j + di][:]),
                                    dec4[:, di, j, :].unsqueeze(1).to_broadcast([P, 2, S]), ALU.mult
                                    ).then_inc(filt_dec, 1)
            w_(filt_dec, 4)
            v.tensor_tensor(slot(7, 0, 1024), slot(0, 0, 1024), slot(0, 1024), ALU.add).then_inc(filt_mix, 1)
            v.tensor_tensor(slot(7, 1024), slot(0, 0, 1024), slot(0, 1024), ALU.subtract).then_inc(filt_mix, 1)
            w_(filt_mix, 2)
            w_(nabias_ready, 1)
            w_(w_act, 6)
            link(v.tensor_tensor(cfa, cfa, cfg, ALU.mult))

            def cf_tap(j):
                for c in range(2):
                    wt = cols[:, CFW + 2 * j + c:CFW + 2 * j + c + 1]
                    sh = j - 15
                    if sh == 0:
                        m = v.tensor_scalar(cfy[:, c, :], cfa[:, c, :], wt, cols[:, CFB + c:CFB + c + 1],
                                            ALU.mult, ALU.add)
                    else:
                        o0, o1 = max(0, -sh), S - max(0, sh)
                        m = stt(cfy[:, c, o0:o1], cfa[:, c, o0 + sh:o1 + sh], wt, cfy[:, c, o0:o1], op1=ALU.add)
                return m

            order = [15] + [j for j in range(31) if j != 15]
            for i in range(2 * H + 3):
                if i < 2 * H:
                    h, t, b = i // 2, i % 2, i % 2
                    w_(scored, H + i + 1)
                    if i >= 2:
                        w_(p_turned, H + i - 1)
                        w_(normed, H + i - 1)
                    bk = bank[4 + b]
                    bias = nab[:, h, 2 - 2 * t:6 - 2 * t, :].rearrange("p r c -> p (r c)")
                    stt(nsc[:, b, 0:S], bk[:, 0:S], 0.125, bias, op1=ALU.add)
                    v.tensor_scalar(nsc[:, b, S:2 * S], bk[:, S:2 * S], 0.125, None, ALU.mult).then_inc(biased, 1)
                    w_(biased, H + i + 1)
                    v.tensor_reduce(hd[:, b, 0:1], nsc[:, b, :], AX.X, ALU.max, negate=True).then_inc(maxed, 1)
                for j in order[2 * i:2 * i + 2]:
                    link(cf_tap(j))
                if 1 <= i <= 2 * H:
                    b = (i - 1) % 2
                    w_(exped, H + i)
                    link(v.reciprocal(hd[:, b, 4:5], hd[:, b, 2:3]))
                    v.tensor_scalar(nsc[:, b, :], nsc[:, b, :], hd[:, b, 4:5], None, ALU.mult).then_inc(normed, 1)
                if i >= 3 and i % 2 == 1:
                    h = (i - 3) // 2
                    lo = 64 * (h % 2)
                    w_(head_out, H + h + 1)
                    v.tensor_copy(catT[lo:lo + 64, h // 2, :], bank[(h // 2) % 2 * 2 + h % 2][lo:lo + 64, 0:S]
                                  ).then_inc(cat_ready, 1)
            v.tensor_copy(hd[:, 0, 0:1], hd[:, 1, 0:1]).then_inc(cf_conv, 1)
            w_(cf_mean, 1)
            for c in range(2):
                stt(cfy[:, c, :], bank[4][:, 0:S], -1.0 / S, cfy[:, c, :], op1=ALU.add).then_inc(cf_cent, 1)
            w_(cf_cent, 2)
            w_(cf_sd, 1)
            link(v.reciprocal(cfsd, cfsd))
            v.tensor_tensor(cfy, cfy, cfsd.unsqueeze(1).to_broadcast([P, 2, S]), ALU.mult).then_inc(cf_n, 1)
            for o in range(2):
                for fq in range(T):
                    w_(zf_filled, 2 * o + fq + 1)
                    z = chan(bank[6 + fq][:])
                    kre, ks = (spec[:, m, fq, o * S:(o + 1) * S] for m in range(2))
                    v.tensor_tensor(tmp_a[:, 0], z[:, 0], kre, ALU.mult)
                    v.tensor_tensor(tmp_a[:, 1], z[:, 1], ks, ALU.mult)
                    v.tensor_tensor(tmp_b[:, 0], z[:, 0], ks, ALU.mult)
                    v.tensor_tensor(tmp_b[:, 1], z[:, 1], kre, ALU.mult).then_inc(zf_used, 1)
                    w_(zf_used, 2 * o + fq + 1)
                    v.tensor_tensor(yf[:, fq, 0, :], tmp_a[:, 0], tmp_a[:, 1], ALU.subtract)
                    v.tensor_tensor(yf[:, fq, 1, :], tmp_b[:, 0], tmp_b[:, 1], ALU.add).then_inc(yf_ready, 1)
                    w_(yf_ready, 2 * o + fq + 1)
                w_(hy_filled, o + 1)
                for c in range(2):
                    m = stt(tmp_a[:, c], hyu[:, 4 + c, :], cols[:, HYD + 2 * o + c:HYD + 2 * o + c + 1],
                            chan(bank[5][:])[:, c], op1=ALU.add)
                link(m)
                dst = hyu[:, 4:6, :] if o == 0 else catT[:, 4:6, :]
                v.tensor_tensor(dst, tmp_a, hyu[:, 2 * o:2 * o + 2, :], ALU.mult).then_inc(hy_ready, 1)
                w_(hy_ready, o + 1)

            def add_gated(banks, gain, scratch):
                for i, (c, t, wait) in enumerate(banks):
                    w_(*wait[0:2])
                    q = x[:, t, c * 512:(c + 1) * 512]
                    tm = slot(0, i * 512, (i + 1) * 512)
                    link(v.tensor_tensor(tm, wait[2][:], gain[:, c * 512:(c + 1) * 512], ALU.mult))
                    v.tensor_tensor(q, q, tm, ALU.add).then_inc(x_added, 1)

            w_(g1_in, 16)
            add_gated([(c, t, (unit, 67 + 2 * c + t + 1, bank[(67 + 2 * c + t) % 4])) for c in range(2) for t in range(T)],
                      gain_a, 0)
            w_(d_load, 16 * 3)
            link(stt(slot(8, 1024), slot(8, 1024), 1.0, slot(8, 0, 1024), ALU.add))
            invert(5)
            w_(x_added, 12)
            for t in range(T):
                link(stt(h0[:, t, :], x[:, t, :], rstd[:, t:t + 1], slot(8, 1024)))
                v.tensor_tensor(h0[:, t, :], h0[:, t, :], slot(9, 0, 1024), ALU.add).then_inc(hn_ready, 1)
            turned_copies(6, slot(1))
            w_(route_filled, 1)
            v.tensor_reduce(rmax, bank[4][:, 0:32].rearrange("p (t n) -> p t n", t=T), AX.X, ALU.max,
                            negate=True).then_inc(route_max, 1)
            w_(route_exp, 1)
            link(v.reciprocal(rinv, rsum))
            v.tensor_tensor(aff, aff, rinv.unsqueeze(2).to_broadcast([P, T, 16]), ALU.mult).then_inc(aff_ready, 1)
            w_(aff_turned, 1)
            v.tensor_copy(aff_t, bank[5][0:16, 0:S]).then_inc(top_ready, 1)
            w_(top_ready, 1)
            src = aff_t
            for r in range(CAP // 8):
                link(v.max(m8[0:16, :], src))
                link(v.match_replace(left, m8[0:16, :], src, -1.0))
                src = left
            v.tensor_tensor(chosen_t, left, aff_t, ALU.not_equal).then_inc(top_ready, 1)
            w_(aff_turned, 2)
            v.tensor_copy(chosen, bank[6][:, 0:32].rearrange("p (t n) -> p t n", t=T)).then_inc(mask_copied, 1)
            w_(mask_copied, 1)
            w_(route_filled, 2)
            v.tensor_copy(pos, bank[7][:, 0:32].rearrange("p (t n) -> p t n", t=T)).then_inc(sel_ready, 1)
            w_(sel_ready, 1)
            iota = cst[:, C_IOTA:C_IOTA + CAP].unsqueeze(1).to_broadcast([P, NEXP, CAP])

            def over_slots(q, t):
                return q[:, t, :].unsqueeze(2).to_broadcast([P, NEXP, CAP])

            def per_slot(q, t):
                return q[:, t, :].rearrange("p (e s) -> p e s", e=NEXP)

            for t in range(T):
                m = v.tensor_tensor(per_slot(sel, t), over_slots(pos, t), iota, ALU.is_equal)
            link(m)
            for t in range(T):
                m = v.tensor_tensor(per_slot(sel, t), per_slot(sel, t), over_slots(chosen, t), ALU.mult)
            m.then_inc(sel_ready, 1)
            w_(sel_ready, 2)
            for t in range(T):
                m = v.tensor_tensor(per_slot(selg, t), per_slot(sel, t), over_slots(aff, t), ALU.mult)
            m.then_inc(selg_ready, 1)
            for k in (0, 2, 4, 6):
                w_(xe_filled, k + 1)
                v.tensor_copy(xet[:, k, :], bank[k % 4][:]).then_inc(xe_dve, 1)

            def rows_out(s, at, grp):
                q = s % 4
                for half in range(2):
                    m = v.tensor_copy(yexp[32 * q:32 * q + 32, grp, half * 512:half * 512 + 512],
                                      bank[5 + half][32 * q:32 * q + 32, :])
                m.then_inc(y_copied, 1)

            def step(s, g):
                def at(base, stride):
                    return base if g is None else (g - 1) * stride + base
                w_(xpiece, at(done_u(s), BODY))
                w_(gate_silu, at(s + 1, 4))
                if s >= 1:
                    w_(act_turned, at(s, 4))
                v.tensor_tensor(act, hs, bank[2 + s % 2][:], ALU.mult).then_inc(act_made, 1)
                if s >= 1:
                    w_(xpiece, at(done_y(s - 1), BODY))
                    if g is None:
                        rows_out(s - 1, at, 0)
                    else:
                        q = (s - 1) % 4
                        base = g if q < 3 else g - 1
                        for half in range(2):
                            m = v.tensor_copy(
                                slots[32 * q:32 * q + 32, bass.ds(5 * 2048 + base * D + half * 512, 512)],
                                bank[5 + half][32 * q:32 * q + 32, :])
                        m.then_inc(y_copied, 1)

            for s in range(4):
                step(s, None)
            with dve.Fori(1, GROUPS) as g:
                for q in range(4):
                    step(4 + q, g)
            w_(xpiece, done_y(NEXP - 1))
            rows_out(NEXP - 1, None, GROUPS - 1)
            w_(g2_in, 32)
            add_gated([(c, t, (comb_filled, 2 * t + c + 1, bank[2 * t + c])) for t in range(T) for c in range(2)],
                      gain_b, 0)
            invert(6)
            w_(g2_in, 32)
            w_(x_added, 16)
            for t in range(T):
                stt(x[:, t, :], x[:, t, :], rstd[:, t:t + 1], slot(9, 0, 1024)).then_inc(final_ready, 1)


_INS = ["x", "a_norm_g", "a_w_in", "a_conv_w", "a_log", "a_dt_bias", "a_out_norm_g", "a_w_out", "kv_norm_g", "w_kv",
        "b_norm_g", "b_w_in", "b_w_out", "rel_bias", "final_norm_g", "c_2", "ctx_2", "c_ctx_2", "w_mod_2", "b_mod_2",
        "norm1_g_2", "norm2_g_2", "w_in_2", "na_rpb_2", "hy_short_w_2", "hy_short_b_2", "hy_filt_w1_2",
        "hy_filt_b1_2", "hy_filt_freq_2", "hy_filt_w2_2", "hy_filt_b2_2", "hy_filt_w3_2", "hy_bias_d_2", "cf_dw_w_2",
        "cf_dw_b_2", "cf_ln_g_2", "cf_ln_b_2", "w_out_2", "router_w_2", "expert_w1_2", "expert_w3_2", "expert_w2_2",
        "final_norm_g_2"]


def kernel(**inputs):
    import numpy as _np
    import concourse.bacc as _bacc
    from concourse import mybir as _mybir
    from concourse.bass_utils import run_bass_kernel_spmd as _run

    nc = _bacc.Bacc("TRN2", target_bir_lowering=False, num_devices=1)
    arrays, aps = {}, {}
    tables = arrays_of_shapes()
    for name in _INS + list(tables):
        v = tables[name] if name in tables else _np.ascontiguousarray(inputs[name])
        arrays[f"in_{name}_dram"] = v
        aps[name] = nc.dram_tensor(f"in_{name}_dram", v.shape, _mybir.dt.from_np(v.dtype), kind="ExternalInput").ap()
    out = nc.dram_tensor("out_0_dram", (1, S, D), F32, kind="ExternalOutput").ap()
    program(nc, aps, out)
    r = _run(nc, [arrays], core_ids=[0])
    return r.results[0]["out_0_dram"]
```

```python
from contextlib import ExitStack

import concourse.bass as bass
from concourse import mybir
from concourse.alu_op_type import AluOpType as ALU

F32 = mybir.dt.float32
ACT = mybir.ActivationFunctionType
AX = mybir.AxisListType

P = 128
S = 256
T = S // P
D = 1024
K = D // P
H = 8
EPS = 1e-6
RING = 6
PIECE = 4096
NEXP, CAP = 16, 32
GROUPS = NEXP // 4
BIG = -1e30

C_ID, C_INC, C_STR, C_ONE, C_LEV = 0, 128, 256, 384, 512
LEVELS = 7
C_IOTA = C_LEV + LEVELS * P
C_COLM = C_IOTA + CAP
C_CLIP = C_COLM + 64
C_END = C_CLIP + 2 * P

CW = 0
R2 = 96
CFW, CFB, LNG, LNB, HYW, HYB, HYD = R2, R2 + 62, R2 + 64, R2 + 66, R2 + 68, R2 + 86, R2 + 92
R3 = R2 + 96
NCOLS = R3 + 16


def arrays_of_shapes():
    import numpy as np
    import math
    i = np.arange(P)
    c = np.zeros((P, C_END), np.float32)
    c[:, C_ID:C_ID + P] = np.eye(P)
    c[:, C_INC:C_INC + P] = i[:, None] <= i[None, :]
    c[:, C_STR:C_STR + P] = i[:, None] < i[None, :]
    c[:, C_ONE:C_ONE + P] = 1
    for lv in range(LEVELS):
        m = 1 << lv
        c[:, C_LEV + lv * P:C_LEV + (lv + 1) * P] = ((i[:, None] // (2 * m) == i[None, :] // (2 * m))
                                                    & (i[:, None] % (2 * m) < m) & (i[None, :] % (2 * m) >= m))
    c[:, C_IOTA:C_IOTA + CAP] = np.arange(CAP)
    col = np.arange(64)
    c0 = np.clip(col - 8, 0, 48)
    ok = (col[None, :] >= c0[:, None]) & (col[None, :] < c0[:, None] + 16)
    c[:, C_COLM:C_COLM + 64] = np.tile(np.where(ok, 0, BIG)[::-1], (2, 1))
    c[:, C_CLIP:C_CLIP + P] = np.where(i[:, None] <= i[None, :], 0, BIG)
    n = np.arange(256)
    nf = np.maximum(n, 1).astype(np.float32)
    large = 16 + (np.log(nf / np.float32(16)) / np.float32(math.log(2048 / 16)) * np.float32(16)).astype(np.int32)
    bucket = np.where(n < 16, n, np.minimum(large, 31))
    hot = np.zeros((32, 384), np.float32)
    hot[bucket, 255 - n] = 1
    caus = np.zeros((H, 384), np.float32)
    caus[:, 256:] = BIG
    tt, ff = np.arange(S, dtype=np.float64), np.arange(S, dtype=np.float64)
    th = np.pi * (2 * ff[None, :] + 1) * tt[:, None] / 512
    fold = lambda a: a.reshape(T, P, S).transpose(1, 0, 2).reshape(P, T * S)
    dft = np.concatenate([fold(np.cos(th)), fold(np.sin(th)), fold(np.cos(th).T / 256), fold(np.sin(th).T / 256)],
                         axis=1).astype(np.float32)
    pos = np.arange(S, dtype=np.float32)[:, None]
    t = pos / np.float32(255)
    rate = np.abs(np.linspace(math.log(1e-2) / 1.5, math.log(1e-2) / 0.3, 256, dtype=np.float32))
    dec = np.exp(-t * rate)
    decb = dec.copy()
    decb[0] = 0
    dec = np.concatenate([fold(dec), fold(decb)], axis=1).astype(np.float32)
    fb = np.linspace(1e-4, 15, 16, dtype=np.float32)[None, :]
    ang = fb * np.float32(2 * math.pi) * pos / np.float32(256)
    feat = np.concatenate([t, np.cos(ang), -np.sin(ang)], axis=-1).astype(np.float32).T.copy()
    return {"t_const": c, "t_hot": hot, "t_causal": caus, "t_dft": dft, "t_decay": dec, "t_feat": feat}


def program(nc, a, out, dbg=None):
    ctx = ExitStack()
    with ctx:
        def sb(name, shape):
            return ctx.enter_context(nc.sbuf_tensor(name, shape, F32))

        def sem(name):
            return ctx.enter_context(nc.semaphore(name))

        ring = [sb(f"ring{r}", [P, PIECE]) for r in range(RING)]
        slots = sb("slots", [P, 10 * 2048])
        x = sb("x_state", [P, T, D])
        cst = sb("cst", [P, C_END])
        gains = sb("gains", [P, 2 * D])
        small = sb("small", [P, 1200])
        spare = sb("spare", [P, 1024])
        bank = [ctx.enter_context(nc.psum_tensor(f"bank{b}", [P, 512], F32)) for b in range(8)]
        bias_dram = nc.dram_tensor("t5_by_distance", [H, 384], F32, kind="Internal").ap()
        rpb_dram = nc.dram_tensor("rpb_extended", [2, H, 6, P], F32, kind="Internal").ap()
        mod_dram = nc.dram_tensor("modulation", [2, 6 * D], F32, kind="Internal").ap()

        def slot(i, c0=0, c1=2048):
            return slots[:, i * 2048 + c0:i * 2048 + c1]

        def tok(ap):
            return ap.rearrange("p (t d) -> p t d", t=T)

        def chan(ap):
            return ap.rearrange("p (c s) -> p c s", s=S)

        def flipped(ap, n):
            (step, parts), cols_ = ap.ap[0], ap.ap[-1][1]
            assert len(ap.ap) == 2 and ap.ap[-1][0] == 1
            return bass.AP(ap.tensor, ap.offset + n - 1, [[step, parts], [n, cols_ // n], [-1, n]])

        gain_a, gain_b = gains[:, 0:D], gains[:, D:2 * D]
        ident = cst[:, C_ID:C_ID + P]
        incl = cst[:, C_INC:C_INC + P]
        strict = cst[:, C_STR:C_STR + P]
        ones = cst[:, C_ONE:C_ONE + P]
        off = [0]

        def piece_of_small(n):
            off[0] += n
            assert off[0] <= 1200
            return small[:, off[0] - n:off[0]]

        cols = piece_of_small(NCOLS)
        w_ab = piece_of_small(K * 16).rearrange("p (k n) -> p k n", k=K)
        out_g = piece_of_small(P)
        rows1 = piece_of_small(P)
        rows2 = piece_of_small(P)
        rows3 = piece_of_small(P)
        alog = piece_of_small(8)
        dtb = piece_of_small(8)
        eps_c = piece_of_small(1)
        one_c = piece_of_small(1)
        sums = piece_of_small(2)
        devs = piece_of_small(2)
        rstd = piece_of_small(2)
        ab = piece_of_small(32).rearrange("p (t n) -> p t n", t=T)
        ga = piece_of_small(16).rearrange("p (t n) -> p t n", t=T)
        gtmp = piece_of_small(16).rearrange("p (t n) -> p t n", t=T)
        glog = piece_of_small(16).rearrange("p (t n) -> p t n", t=T)
        beta = piece_of_small(16).rearrange("p (t n) -> p t n", t=T)
        gcum = piece_of_small(16).rearrange("p (t n) -> p t n", t=T)
        ealog = piece_of_small(8)
        osum = piece_of_small(16)
        orstd = piece_of_small(16)
        hd = piece_of_small(12).rearrange("p (b n) -> p b n", b=2)
        relb = rows1
        filt = piece_of_small(3)
        m8 = piece_of_small(8)
        l2sd = piece_of_small(32)
        l2r = piece_of_small(32)
        l2kb = piece_of_small(16)

        x_in, const_in, gain_in, small_in = sem("x_in"), sem("const_in"), sem("gain_in"), sem("small_in")
        conv_in = sem("conv_in")
        piece_in = [sem(f"piece_in{r}") for r in range(RING)]
        consts_set = sem("consts_set")
        squares = sem("squares")
        sd_ready = sem("sd_ready")
        rstd_ready = sem("rstd_ready")
        hn_ready = sem("hn_ready")
        turned = sem("turned")
        turned_dve, turned_act = sem("turned_dve"), sem("turned_act")
        rows_turned, cols_ready = sem("rows_turned"), sem("cols_ready")
        unit = sem("unit")
        ab_done, ab_copied, gate_act, gate_ready = sem("ab_done"), sem("ab_copied"), sem("gate_act"), sem("gate_ready")
        ga_ready = sem("ga_ready")
        dve_chain = sem("dve_chain")
        act_chain = sem("act_chain")
        pool_chain = sem("pool_chain")
        conv_done, silu_done, z_ready = sem("conv_done"), sem("silu_done"), sem("z_ready")
        cum_done, cum_copied = sem("cum_done"), sem("cum_copied")
        sq_ready, l2_summed, l2_sd, l2r_ready, qk_ready = (sem("sq_ready"), sem("l2_summed"), sem("l2_sd"),
                                                           sem("l2r_ready"), sem("qk_ready"))
        fk_ready, fkb_ready, fq_ready, f_turned = sem("fk_ready"), sem("fkb_ready"), sem("fq_ready"), sem("f_turned")
        v_turned, v_ready = sem("v_turned"), sem("v_ready")
        gb_ready, g_turned = sem("gb_ready"), sem("g_turned")
        pair_a, pair_b = sem("pair_a"), sem("pair_b")
        diff_ready, decay_ready, prod_a, prod_b = sem("diff_ready"), sem("decay_ready"), sem("prod_a"), sem("prod_b")
        mask_ready, y_filled, y_ready = sem("mask_ready"), sem("y_filled"), sem("y_ready")
        inv_filled, x_upd, xt_upd = sem("inv_filled"), sem("x_upd"), sem("xt_upd")
        csilu_ready = sem("csilu_ready")
        mod_added = sem("mod_added")
        bmod_in = [sem("bmod_in_even"), sem("bmod_in_odd")]
        mod_out = [sem("mod_out_even"), sem("mod_out_odd")]
        solve_filled, v0_ready, r1_ready, v1_ready, o_ready = (sem("solve_filled"), sem("v0_ready"), sem("r1_ready"),
                                                               sem("v1_ready"), sem("o_ready"))
        o_sq, o_ms, o_sd, zg_ready = sem("o_sq"), sem("o_ms"), sem("o_sd"), sem("zg_ready")
        x_added = sem("x_added")
        b_gain_in = sem("b_gain_in")
        t5_filled, t5_row, t5_moved, hot_in = sem("t5_filled"), sem("t5_row"), sem("t5_moved"), sem("hot_in")
        k_copied, v_copied, q_copied, zb_copied = sem("k_copied"), sem("v_copied"), sem("q_copied"), sem("zb_copied")
        scored, biased, maxed, exped, normed = sem("scored"), sem("biased"), sem("maxed"), sem("exped"), sem("normed")
        p_turned, pt_ready, head_out, yt_ready = sem("p_turned"), sem("pt_ready"), sem("head_out"), sem("yt_ready")
        o_copied, zb_silu = sem("o_copied"), sem("zb_silu")
        c_load, ctx_in, fin_in = sem("c_load"), sem("ctx_in"), sem("fin_in")
        x3_ready, ctx_normed, cat_ready, zf_used = sem("x3_ready"), sem("ctx_normed"), sem("cat_ready"), sem("zf_used")
        rpb_out, rpb_in = sem("rpb_out"), sem("rpb_in")
        nabias_ready = sem("nabias_ready")
        w_read = sem("w_read")
        w_act = sem("w_act")
        hy_in_ready = sem("hy_in_ready")
        dft_in, filt_in, filt_filled, filt_arg, filt_sin = (sem("dft_in"), sem("filt_in"), sem("filt_filled"),
                                                            sem("filt_arg"), sem("filt_sin"))
        filt_dec, filt_mix, spec_filled, spec_ready = (sem("filt_dec"), sem("filt_mix"), sem("spec_filled"),
                                                       sem("spec_ready"))
        z_turned, zt_ready, zf_filled, yf_ready, hy_filled, hy_ready = (
            sem("z_turned"), sem("zt_ready"), sem("zf_filled"), sem("yf_ready"), sem("hy_filled"), sem("hy_ready"))
        cf_conv, cf_cent, cf_sum, cf_act, cf_n, cf_ready = (
            sem("cf_conv"), sem("cf_cent"), sem("cf_sum"), sem("cf_act"), sem("cf_n"),
            sem("cf_ready"))
        router_in, d_load, g1_in, g2_in = (sem("router_in"), sem("d_load"), sem("g1_in"), sem("g2_in"))
        route_filled, route_max, route_exp, aff_ready, aff_turned, top_ready = (
            sem("route_filled"), sem("route_max"), sem("route_exp"), sem("aff_ready"), sem("aff_turned"),
            sem("top_ready"))
        sel_ready, selg_ready, selg_turned, selgt_ready = (
            sem("sel_ready"), sem("selg_ready"), sem("selg_turned"), sem("selgt_ready"))
        xe_filled, xe_dve, xe_act = sem("xe_filled"), sem("xe_dve"), sem("xe_act")
        xe_static = sem("xe_static")
        xpiece = sem("xpiece")
        gate_silu, act_made, act_turned, actt_ready, y_copied = (sem("gate_silu"), sem("act_made"), sem("act_turned"),
                                                                 sem("actt_ready"), sem("y_copied"))
        comb_filled, final_ready, out_done = sem("comb_filled"), sem("final_ready"), sem("out_done")

        def rows128(w, c0, c1):
            return w[:, c0:c1].rearrange("(k p) n -> p k n", p=P)

        w_a, w_ao, w_kv = a["a_w_in"][0], a["a_w_out"][0], a["w_kv"]
        w_b, w_bo, w_i, w_o, w_m = a["b_w_in"][0], a["b_w_out"][0], a["w_in_2"][0], a["w_out_2"][0], a["w_mod_2"][0]
        N_MOD = 12

        def chunks(w, width, units_):
            return [(rows128(w, c, c + 512), units_) for c in range(0, width, 512)]

        mods = chunks(w_m, 6 * D, 1)
        pieces = chunks(w_a, 4096, 2) + mods[0:9] + chunks(w_ao, D, 2) + mods[9:10] + chunks(w_kv, 2 * D, 2)
        pieces += chunks(w_b, 2 * D, 2) + chunks(w_bo, D, 2)
        pieces += [(rows128(w_i, 512, 1024), 6), (rows128(w_i, 1024, 1536), 2), (rows128(w_i, 0, 512), 2)]
        pieces += [(rows128(w_i, 2304, 2816), 2), (rows128(w_i, 1536, 2048), 2), (rows128(w_i, 2048, 2304), 1)]
        pieces += chunks(w_o, D, 2) + mods[10:12]
        U_MOD = list(range(16, 25)) + [29, 69, 70]
        U_AOUT, U_K, U_V, U_Q, U_Z, U_BOUT, U_CTX, U_NK, U_NV, U_NQ, U_CF, U_HY, U_OUT = (
            25, 30, 34, 38, 42, 46, 50, 54, 56, 58, 60, 62, 65)
        bank_of = [u % 4 for u in range(71)]
        for m, b in enumerate((0, 1, 6, 7, 6, 0, 1, 2, 3, 3, 2, 3)):
            bank_of[U_MOD[m]] = b
        for j, b in enumerate((0, 1, 0, 1)):
            bank_of[U_Z + j] = b
        for j, b in enumerate((2, 3, 2)):
            bank_of[U_HY + j] = b
        mod_piece = {8 + m: m for m in range(9)}
        mod_piece[19] = 9
        LAST_TURN = 4
        NPRE = len(pieces)
        freed_at = []
        for _, n in pieces:
            freed_at.append(n + (freed_at[-1] if freed_at else 0))
        ew1, ew3, ew2 = a["expert_w1_2"][0], a["expert_w3_2"][0], a["expert_w2_2"][0]

        def expert_piece(w, e, j):
            if w is ew2:
                return w[bass.ds(e, 1), 512 * j:512 * j + 512, :].rearrange("o (p b) n -> p (o b) n", p=P)
            return w[bass.ds(e, 1)].rearrange("o (p k) n -> p (o k) n", p=P)[:, 2 * j:2 * j + 2, :]

        NP_ROW = 12
        BODY = 4 * NP_ROW
        assert BODY % RING == 0

        X = slot(0).rearrange("p (n c) -> p n c", c=P)
        XT = slot(1).rearrange("p (n c) -> p n c", c=P)
        kT = chan(slot(2))
        kbq = slots[:, 3 * 2048:5 * 2048].rearrange("p (h r s) -> p h r s", h=H, r=2)
        vtok = slot(5).rearrange("p (t h d) -> p t h d", t=T, h=H)
        zsil = slot(6)
        raw = slots[:, 7 * 2048:10 * 2048]
        pairs = raw.rearrange("p (h n) -> p h n", h=H)
        masked = slot(2).rearrange("p (n c) -> p n c", c=P)
        ybuf = slot(3).rearrange("p (n c) -> p n c", c=P)
        osb = slot(3)
        decay = slots[:, 0:768].rearrange("p (b n) -> p b n", b=2)
        fac0 = slot(0).rearrange("p (t h c) -> p t h c", t=T, h=H)
        fac1 = slot(1).rearrange("p (t h c) -> p t h c", t=T, h=H)
        gb = slot(1).rearrange("p (t h c) -> p t h c", t=T, h=H)
        mkT, mv, mqT, myT = chan(slot(3)), slot(4).rearrange("p (t h d) -> p t h d", t=T, h=H), chan(slot(5)), \
            chan(slot(7))
        t5 = slot(8).rearrange("p (h m) -> p h m", h=H)
        msc = slot(9, 0, 768).rearrange("p (b n) -> p b n", b=2)
        mpt = slot(9, 768, 1536).rearrange("p (b n) -> p b n", b=2)
        nq, nk = chan(slot(3, 0, 1024)), chan(slot(3, 1024))
        nv, nkc = slot(4, 0, 1024).rearrange("p (t n) -> p t n", t=T), chan(slot(4, 1024))
        nvc = slot(5, 0, 1024).rearrange("p (t n) -> p t n", t=T)
        cfa, cfg = chan(slot(5, 1024, 1536)), chan(slot(5, 1536))
        hyu, cfy = chan(slot(6, 0, 1536)), chan(slot(6, 1536))
        catT = chan(slot(7))
        nab = slots[:, 8 * 2048:8 * 2048 + 3072].rearrange("p (h r c) -> p h r c", h=H, r=6)
        dec = slot(9, 1024)
        dft = slot(2).rearrange("p (m t s) -> p m t s", m=4, t=T)
        cf_tap_b, cf_sum_b = chan(slot(7, 1536)), chan(slot(7, 1024, 1536))
        POOL_TAPS, DVE_TAPS = list(range(15)) + list(range(16, 20)), [15] + list(range(20, 31))
        spec = [spare[:].rearrange("p (f n) -> p f n", f=T), slot(9, 1024).rearrange("p (f n) -> p f n", f=T)]
        nsc = slot(0, 0, 1024).rearrange("p (b n) -> p b n", b=2)
        npt = [slot(0, 1024).rearrange("p (k s) -> p k s", k=4), gain_b.rearrange("p (k s) -> p k s", k=4)]
        zt = slot(1, 0, 512).rearrange("p (t n) -> p t n", t=T)
        yf = slot(1, 512, 1536).rearrange("p (f m n) -> p f m n", f=T, m=2)
        tmp_a = slot(1, 1536).rearrange("p (m n) -> p m n", m=2)
        tmp_b = slot(5, 1536).rearrange("p (m n) -> p m n", m=2)
        cfsq, cfsd = slot(8, 0, 512), slot(8, 512, 768)
        filters = slot(0).rearrange("p (m t n) -> p m t n", m=2, t=T)
        mix = slot(7).rearrange("p (m t n) -> p m t n", m=2, t=T)
        sel = slot(2, 0, 1024).rearrange("p (t n) -> p t n", t=T)
        selgt = slot(2, 1024).rearrange("p (g s) -> p g s", g=GROUPS)
        xet = slots[:, 3 * 2048:5 * 2048].rearrange("p (k n) -> p k n", k=K)
        yexp = slots[:, 5 * 2048:7 * 2048].rearrange("p (g n) -> p g n", g=GROUPS)
        hs = slot(7, 0, 512)
        act = slot(7, 512, 1024)
        actt = slot(7, 1024, 1536).rearrange("p (b n) -> p b n", b=4)
        xe = slot(7, 1536).rearrange("p (b k n) -> p b k n", b=2, k=K)
        router = slot(9, 1024, 2048)
        aff, chosen, pos = (router[:, c:c + 32].rearrange("p (t n) -> p t n", t=T) for c in (0, 32, 64))
        chosen_t, left, aff_t = router[0:16, 96:352], router[0:16, 352:608], router[0:16, 608:864]
        rmax, rsum, rinv = router[:, 864:866], router[:, 866:868], router[:, 868:870]
        selg = slot(8).rearrange("p (t n) -> p t n", t=T)[:, :, 0:512]

        def coupled(lv, g):
            if lv == 0 and g < 2:
                return X[:, 8 + 4 * g:12 + 4 * g, :]
            return masked[:, 4 * g:4 * g + 4, :]

        def block_half(q, lv, half):
            return q.rearrange("p (n two b) -> p n two b", two=2, b=2 ** lv)[:, :, half, :]

        def done_a(s):
            return 4 if s == 0 else 12 * s

        def done_u(s):
            return 8 if s == 0 else 12 * s + 4

        def done_y(s):
            return 12 * s + 20 if s < NEXP - 1 else 12 * s + 12

        block = ctx.enter_context(nc.Block())

        def bmod(eng, m):
            eng.dma_start(spare[0:2, (m % 2) * 512:(m % 2) * 512 + 512],
                          a["b_mod_2"][:, m * 512:m * 512 + 512].to_broadcast([2, 512])).then_inc(bmod_in[m % 2], 16)

        def mod_send(eng, m):
            eng.dma_start(mod_dram[:, m * 512:m * 512 + 512],
                          spare[0:2, (m % 2) * 512:(m % 2) * 512 + 512]).then_inc(mod_out[m % 2], 16)

        @block.sync
        def _(sp):
            sp.dma_start(x[:], a["x"][0].rearrange("(t p) d -> p t d", p=P)).then_inc(x_in, 16)
            sp.dma_start(gain_a, a["a_norm_g"].to_broadcast([P, D])).then_inc(gain_in, 16)
            sp.dma_start(cst[:], a["t_const"]).then_inc(const_in, 16)
            sp.dma_start(rows1[0:96, :], a["a_conv_w"][0].rearrange("j (t p) -> (j t) p", p=P)).then_inc(conv_in, 16)
            sp.dma_start(w_ab, w_a[:, 4096:4112].rearrange("(k p) n -> p k n", p=P)).then_inc(conv_in, 16)

            def mod_rows(n):
                if n in mod_piece:
                    m = mod_piece[n]
                    sp.wait_ge(mod_added, m + 1)
                    mod_send(sp, m)
                if n - 1 in mod_piece and mod_piece[n - 1] + 2 < 10:
                    m = mod_piece[n - 1]
                    sp.wait_ge(mod_out[m % 2], 16 * (m // 2 + 1))
                    bmod(sp, m + 2)

            for n, (src, _) in enumerate(pieces):
                if n >= RING:
                    sp.wait_ge(unit, freed_at[n - RING])
                dst = ring[n % RING][:, 0:src.shape[1] * src.shape[2]].rearrange("p (k n) -> p k n", k=K)
                sp.dma_start(dst, src).then_inc(piece_in[n % RING], 16)
                if n >= RING:
                    mod_rows(n - RING)

            def expert_step(n, s, first, wait):
                for w, e in ((ew1, s), (ew3, s)) + (() if first else ((ew2, s - 1),)):
                    for j in range(4):
                        wait(n)
                        dst = ring[n % RING][:].rearrange("p (k n) -> p k n", k=4 if w is ew2 else 2)
                        sp.dma_start(dst, expert_piece(w, e, j)).then_inc(piece_in[n % RING], 16)
                        n += 1
                return n

            def wait_static(n):
                if n - RING < NPRE:
                    sp.wait_ge(unit, freed_at[n - RING])
                else:
                    sp.wait_ge(xpiece, n - RING - NPRE + 1)

            n = NPRE
            for s in range(4):
                n = expert_step(n, s, s == 0, wait_static)
            first = n
            with sp.Fori(0, GROUPS - 1) as g:
                n = first
                for q in range(4):
                    n = expert_step(n, g * 4 + (4 + q), False,
                                    lambda m: sp.wait_ge(xpiece, g * BODY + (m - RING - NPRE + 1)))
            n = first + (GROUPS - 1) * BODY
            for j in range(4):
                wait_static(n)
                sp.dma_start(ring[n % RING][:].rearrange("p (k n) -> p k n", k=4),
                             expert_piece(ew2, NEXP - 1, j)).then_inc(piece_in[n % RING], 16)
                n += 1
            for t in range(T):
                sp.wait_ge(final_ready, t + 1)
                sp.dma_start(out[0, t * P:(t + 1) * P, :], x[:, t, :]).then_inc(out_done, 16)
            sp.wait_ge(out_done, 16 * T)

        @block.gpsimd
        def _(pool):
            def load(dst, src, s):
                pool.dma_start(dst, src).then_inc(s, 16)

            pool.wait_ge(hn_ready, T)
            load(gain_a, a["kv_norm_g"].rearrange("(o d) -> o d", o=1).to_broadcast([P, D]), b_gain_in)
            load(gain_b, a["b_norm_g"].to_broadcast([P, D]), b_gain_in)
            pool.wait_ge(cols_ready, 1)
            load(relb[0:32, 0:8], a["rel_bias"], hot_in)
            pool.wait_ge(l2r_ready, 2)
            pool.wait_ge(unit, 16)
            nc.gpsimd.tensor_copy(slot(1).rearrange("p (n c) -> p n c", c=P),
                                  l2kb.unsqueeze(2).to_broadcast([P, 16, P])).then_inc(fkb_ready, 1)
            pool.wait_ge(small_in, 16 * 15)
            pool.wait_ge(z_ready, 4)
            z3 = zsil.rearrange("p (n d) -> p n d", d=P)
            nc.gpsimd.tensor_tensor(z3, z3, out_g.unsqueeze(1).to_broadcast([P, 16, P]), ALU.mult).then_inc(zg_ready, 1)
            for lv in range(LEVELS):
                for g in range(4):
                    if lv == 0:
                        pool.wait_ge(prod_b, 2 * g + 2)
                        if g == 2:
                            pool.wait_ge(pair_b, H)
                    elif lv == 1:
                        if g >= 2:
                            pool.wait_ge(xt_upd, g + 1)
                    else:
                        pool.wait_ge(y_filled, 4 * (lv - 2) + g + 1)
                    for hh in range(2):
                        src = pairs[:, 2 * g + hh, :].rearrange("p (c n) -> p c n", n=P)[:, 0:5:4, :]
                        m = nc.gpsimd.tensor_tensor(
                            coupled(lv, g)[:, 2 * hh:2 * hh + 2, :], src,
                            cst[:, C_LEV + lv * P:C_LEV + (lv + 1) * P].unsqueeze(1).to_broadcast([P, 2, P]), ALU.mult)
                    m.then_inc(mask_ready, 1)
            pool.wait_ge(o_ready, 4)
            load(slot(9, 0, 384)[0:32, :], a["t_hot"], hot_in)
            load(slot(9, 384, 768)[0:8, :], a["t_causal"], hot_in)
            pool.wait_ge(t5_row, 1)
            load(bias_dram, slot(9, 768, 1152)[0:8, :], t5_moved)
            pool.wait_ge(t5_moved, 16)
            load(t5, bass.AP(bias_dram.tensor, 0, [[1, P], [384, H], [1, 256]]), t5_moved)
            zeros = slot(9, 1536, 1664)[0:96, :]
            nc.gpsimd.memset(zeros, 0.0).then_inc(pool_chain, 1)
            pool.wait_ge(pool_chain, 1)
            load(rpb_dram.rearrange("a h r c -> (a h r) c"), zeros, rpb_out)
            pool.wait_ge(rpb_out, 16)
            for half in range(2):
                load(rpb_dram[half, :, :, 48:79], a["na_rpb_2"][0][:, 5 - half:11 - half, :], rpb_out)
            pool.wait_ge(hn_ready, 8)
            load(gain_a, a["final_norm_g"].rearrange("(o d) -> o d", o=1).to_broadcast([P, D]), fin_in)

            def mod_row(dst, who, part, s):
                load(dst, mod_dram[who:who + 1, part * D:(part + 1) * D].to_broadcast([P, D]), s)

            for s in mod_out:
                pool.wait_ge(s, 16 * 5)
            pool.wait_ge(head_out, H)
            pool.wait_ge(yt_ready, 2)
            load(slot(5, 0, 1024), a["norm1_g_2"].to_broadcast([P, D]), c_load)
            mod_row(slot(5, 1024), 0, 1, c_load)
            mod_row(slot(6, 0, 1024), 0, 0, c_load)
            mod_row(slot(6, 1024), 1, 1, c_load)
            mod_row(slot(4, 0, 1024), 1, 0, c_load)
            load(tok(slot(3)), a["ctx_2"][0].rearrange("(t p) d -> p t d", p=P), ctx_in)
            pool.wait_ge(rpb_out, 48)
            for half in range(2):
                load(nab[64 * half:64 * half + 64].rearrange("p h r c -> p (h r) c"),
                     bass.AP(rpb_dram.tensor, half * 6 * H * P, [[1, 64], [P, 6 * H], [1, 64]]), rpb_in)
            load(dec, a["t_decay"], filt_in)
            pool.wait_ge(rpb_in, 32)
            n3 = nab.rearrange("p h r c -> p (h r) c")
            nc.gpsimd.tensor_tensor(n3, n3, cst[:, C_COLM:C_COLM + 64].unsqueeze(1).to_broadcast([P, 6 * H, 64]),
                                    ALU.add).then_inc(nabias_ready, 1)
            load(gain_b[0:33, 0:64], a["hy_filt_w1_2"][0], filt_in)
            load(gain_b[0:64, 64:128], a["hy_filt_w2_2"][0], filt_in)
            load(gain_b[0:33, 128:384], a["t_feat"], filt_in)
            pool.wait_ge(x3_ready, T)
            load(gain_a[0:64, :], a["hy_filt_w3_2"][0], filt_in)
            load(w_ab, a["router_w_2"][0].rearrange("(k p) n -> p k n", p=P), router_in)
            pool.wait_ge(unit, U_NK)
            load(slot(2), a["t_dft"], dft_in)
            pool.wait_ge(filt_filled, 6)
            mod_row(gain_a, 0, 2, g1_in)
            pool.wait_ge(w_act, 6)
            nc.gpsimd.tensor_tensor(cfa, cfa, cfg, ALU.mult).then_inc(cf_conv, 1)

            pool.wait_ge(cf_conv, 1)
            pool.wait_ge(spec_filled, 4)
            nc.gpsimd.memset(cf_sum_b, 0.0).then_inc(cf_conv, 1)
            pool.wait_ge(cf_conv, 2)
            for n, j in enumerate(POOL_TAPS):
                sh = j - 15
                o0, o1 = max(0, -sh), S - max(0, sh)
                wt = cols[:, CFW + 2 * j:CFW + 2 * j + 2].unsqueeze(2).to_broadcast([P, 2, o1 - o0])
                product, q = cf_tap_b[:, :, o0:o1], cf_sum_b[:, :, o0:o1]
                nc.gpsimd.tensor_tensor(product, cfa[:, :, o0 + sh:o1 + sh], wt, ALU.mult).then_inc(cf_conv, 1)
                pool.wait_ge(cf_conv, 3 + 2 * n)
                nc.gpsimd.tensor_tensor(q, q, product, ALU.add).then_inc(cf_conv, 1)
                pool.wait_ge(cf_conv, 4 + 2 * n)
            pool.wait_ge(biased, H + 2 * H)
            pool.wait_ge(cf_ready, 2)
            load(slot(8, 0, 1024), a["norm2_g_2"].to_broadcast([P, D]), d_load)
            mod_row(slot(8, 1024), 0, 4, d_load)
            mod_row(slot(9, 0, 1024), 0, 3, d_load)
            for s in mod_out:
                pool.wait_ge(s, 16 * N_MOD // 2)
            mod_row(gain_b, 0, 5, g2_in)
            pool.wait_ge(hn_ready, 12)
            load(slot(9, 0, 1024), a["final_norm_g_2"].rearrange("(o d) -> o d", o=1).to_broadcast([P, D]), g2_in)
            pool.wait_ge(xe_dve, 1)
            pool.wait_ge(xe_act, 1)
            for s in range(4):
                if s >= 2:
                    pool.wait_ge(xpiece, done_u(s - 2))
                nc.gpsimd.tensor_copy(xe[:, s % 2], xet[:, :, s * CAP:(s + 1) * CAP]).then_inc(xe_static, 1)
            pool.wait_ge(xe_dve, GROUPS)
            pool.wait_ge(xe_act, GROUPS)
            with pool.Fori(0, GROUPS - 1) as g:
                for q in range(4):
                    pool.wait_ge(xpiece, g * BODY + done_u(4 + q - 2))
                    nc.gpsimd.tensor_copy(xe[:, q % 2], xet[:, :, bass.ds(g * 4 * CAP + (4 + q) * CAP, CAP)]
                                          ).then_inc(xe_static, 1)


        @block.tensor
        def _(pe):
            reader = {}

            def fill(b, sem_, count):
                for s_, c_ in reader.get(b, ()):
                    pe.wait_ge(s_, c_)
                reader[b] = ((sem_, count),)
                return bank[b]

            def fill2(b, pairs_):
                bk = fill(b, *pairs_[0])
                reader[b] = tuple(pairs_)
                return bk

            turn_count = [0]

            def turn(src, sem_, count):
                n = turn_count[0]
                turn_count[0] += 1
                for t in range(T):
                    pe.wait_ge(sem_, count + t)
                    for kh in range(2):
                        bk = fill(4 + 2 * t + kh, (turned_dve, turned_act)[kh], 2 * n + t + 1)
                        for kk in range(4):
                            k = 4 * kh + kk
                            m = pe.transpose(bk[:, kk * P:(kk + 1) * P], src[:, t, k * P:(k + 1) * P], ident)
                        m.then_inc(turned, 1)

            def turned_tile(t):
                pe.wait_ge(turned_dve, 2 * turn_count[0] - 1 + t)
                pe.wait_ge(turned_act, 2 * turn_count[0] - 1 + t)

            def turned_all():
                pe.wait_ge(turned_dve, 2 * turn_count[0])
                pe.wait_ge(turned_act, 2 * turn_count[0])

            units = [0]
            piece = [0]

            def take():
                n = piece[0]
                pe.wait_ge(piece_in[n % RING], 16 * (n // RING + 1))
                piece[0] += 1
                return ring[n % RING]

            def chan_unit(w, c, act_t, sem_, count, parts=(0, 1)):
                u = units[0]
                bk = fill(bank_of[u], sem_, count) if 0 in parts else bank[bank_of[u]]
                for i in parts:
                    for k in range(K):
                        m = pe.matmul(bk[:, i * S:(i + 1) * S], w[:, k, (c + i) * P:(c + i + 1) * P], act_t[:, k, :],
                                      start=(k == 0), stop=(k == K - 1))
                if 1 in parts:
                    m.then_inc(unit, 1)
                    units[0] += 1

            def tok_unit(w, t, act_t, sem_, count, late=None):
                bk = fill(bank_of[units[0]], sem_, count)
                for k in range(K):
                    if late and k == late[2]:
                        pe.wait_ge(*late[0:2])
                    m = pe.matmul(bk[:], act_t[:, k, t * P:(t + 1) * P], w[:, k, :], start=(k == 0), stop=(k == K - 1))
                m.then_inc(unit, 1)
                units[0] += 1

            mod_at = [0, 0]
            mod_w = [None]
            cT = cols[:, R3:R3 + 16].rearrange("p (w k) -> p w k", w=2)

            def modulation(n):
                for _ in range(n):
                    m, k = mod_at
                    u = units[0]
                    if k == 0:
                        mod_w[0] = wide(take())
                        fill(bank_of[u], mod_added, m + 1)
                    for c in range(4):
                        q = pe.matmul(bank[bank_of[u]][32 * c:32 * c + 2, 0:P], cT[:, :, k],
                                      mod_w[0][:, k, c * P:(c + 1) * P], start=(k == 0), stop=(k == K - 1))
                    mod_at[1] += 1
                    if k == K - 1:
                        q.then_inc(unit, 1)
                        units[0] += 1
                        mod_at[:] = [m + 1, 0]

            def wide(r):
                return r[:].rearrange("p (k n) -> p k n", k=K)

            hT = chan(slot(1))
            pe.wait_ge(const_in, 16)
            turn(tok(slot(0)), hn_ready, 1)
            pe.wait_ge(conv_in, 32)
            pe.transpose(fill(0, cols_ready, 1)[:, 0:96], rows1[0:96, :], ident[0:96, 0:96]).then_inc(rows_turned, 1)
            turned_all()
            bk = fill(4, ab_copied, 1)
            for t in range(T):
                for k in range(K):
                    m = pe.matmul(bk[:, t * 16:(t + 1) * 16], hT[:, k, t * P:(t + 1) * P], w_ab[:, k, :],
                                  start=(k == 0), stop=(k == K - 1))
            m.then_inc(ab_done, 1)
            for n in range(6):
                w = wide(take())
                for c in (0, 2):
                    chan_unit(w, c, hT, conv_done, units[0] + 1)
                if n == 1:
                    pe.wait_ge(small_in, 16 * 15)
                    bk = fill(5, cols_ready, 3)
                    pe.transpose(bk[:, 0:96], rows2[0:96, :], ident[0:96, 0:96])
                    pe.transpose(bk[:, 96:112], rows3[0:16, :], ident[0:16, 0:16]).then_inc(rows_turned, 1)
            bk = fill(5, l2_sd, 1)
            for j in range(8):
                pe.wait_ge(sq_ready, j + 1)
                sq = chan(slot((0, 2)[j // 4], (j % 4) * 512, (j % 4) * 512 + 512))
                for i in range(2):
                    for t in range(T):
                        c = (j // 4) * 16 + t * 8 + (2 * j + i) % 8
                        m = pe.matmul(bk[:, c:c + 1], sq[:, i, t * P:(t + 1) * P], ones[:, 0:1], start=True, stop=True)
            m.then_inc(l2_summed, 1)
            pe.wait_ge(gate_ready, 1)
            bk = fill(4, cum_copied, 1)
            pe.matmul(bk[:, 0:8], incl, glog[:, 0, :], start=True, stop=True)
            pe.matmul(bk[:, 8:16], incl, glog[:, 1, :], start=True, stop=False)
            pe.matmul(bk[:, 8:16], ones, glog[:, 0, :], start=False, stop=True).then_inc(cum_done, 1)
            for n in range(2):
                w = wide(take())
                for t in range(T):
                    tok_unit(w, t, hT, z_ready, 2 * n + t + 1)

            def turn_factors(src, n):
                for j in range(4):
                    bk = fill(4 + j, qk_ready, 4 * n + j + 1)
                    for hh in range(2):
                        for t in range(T):
                            m = pe.transpose(bk[:, hh * S + t * P:hh * S + (t + 1) * P], src[:, t, 2 * j + hh, :], ident)
                    m.then_inc(f_turned, 1)

            pe.wait_ge(fk_ready, 1)
            turn_factors(fac0, 0)
            pe.wait_ge(silu_done, 12)
            for t in range(T):
                for hb in range(2):
                    bk = fill(4 + 2 * t + hb, v_ready, 2 * t + hb + 1)
                    for i in range(4):
                        h = 4 * hb + i
                        m = pe.transpose(bk[:, i * P:(i + 1) * P], chan(slot(9))[:, h, t * P:(t + 1) * P], ident)
                    m.then_inc(v_turned, 1)
            pe.wait_ge(csilu_ready, 1)
            modulation(8)
            pe.wait_ge(fkb_ready, 1)
            turn_factors(fac1, 1)
            pe.wait_ge(fq_ready, 1)
            turn_factors(fac0, 2)
            modulation(8)
            pe.wait_ge(qk_ready, 12)
            pe.wait_ge(gb_ready, 1)
            for h in range(H):
                if h % 2 == 0:
                    bk = fill(4 + (h // 2) % 2, diff_ready, h + 2)
                    for hh in range(2):
                        for t in range(T):
                            m = pe.transpose(bk[:, hh * S + t * P:hh * S + (t + 1) * P], gb[:, t, h + hh, :], ident)
                    m.then_inc(g_turned, 1)
                bk = fill(h % 2, prod_a, h + 1)
                pe.matmul(bk[:], kT[:, h, 0:P], kbq[:, h, :, :], start=True, stop=True).then_inc(pair_a, 1)
                bk = fill(2 + h % 2, prod_b, h + 1)
                pe.matmul(bk[:, 0:S].rearrange("p (r s) -> p r s", r=2), kT[:, h, P:S], kbq[:, h, :, P:S],
                          start=True, stop=True).then_inc(pair_b, 1)
                modulation(3)
            modulation(8)
            for lv in range(1, LEVELS):
                for g in range(4):
                    pe.wait_ge(mask_ready, 4 * lv + g + 1)
                    pe.wait_ge(x_upd, 4 * (lv - 1) + g + 1)
                    bk = fill(2 + g % 2, y_ready, 4 * (lv - 1) + g + 1)
                    for i in range(4):
                        m = pe.matmul(bk[:, i * P:(i + 1) * P], masked[:, 4 * g + i, :], X[:, 4 * g + i, :],
                                      start=True, stop=True)
                    m.then_inc(y_filled, 1)
                if lv >= LEVELS - 2:
                    modulation(4)
                for g in range(4):
                    pe.wait_ge(y_ready, 4 * (lv - 1) + g + 1)
                    pe.wait_ge(xt_upd, 4 * (lv - 1) + g + 1)
                    if lv < LEVELS - 1:
                        bk = fill(4 + g % 2, x_upd, 4 * lv + g + 1)
                        for i in range(4):
                            m = pe.matmul(bk[:, i * 64:(i + 1) * 64].rearrange("p (n b) -> p n b", b=2 ** lv),
                                      XT[:, 4 * g + i, :], block_half(ybuf[:, 4 * g + i, :], lv, 0),
                                      start=True, stop=True)
                    if lv > LAST_TURN:
                        bk = fill(6 + g % 2, xt_upd, 4 * lv + g + 1)
                    for i in range(4 if lv > LAST_TURN else 0):
                        m = pe.matmul(bk[:, i * 64:(i + 1) * 64].rearrange("p (n b) -> p n b", b=2 ** lv),
                                      ybuf[:, 4 * g + i, :], block_half(XT[:, 4 * g + i, :], lv, 1),
                                      start=True, stop=True)
                    m.then_inc(inv_filled, 1)
            pe.wait_ge(v_ready, 4)
            for hb in range(2):
                pe.wait_ge(xt_upd, 4 * (LEVELS - 1) + 2 * hb + 2)
                bk = fill(hb, v0_ready, hb + 1)
                for i in range(4):
                    h = 4 * hb + i
                    m = pe.matmul(bk[:, i * P:(i + 1) * P], XT[:, 2 * h, :], vtok[:, 0, h, :], start=True, stop=True)
                m.then_inc(solve_filled, 1)
            for hb in range(2):
                pe.wait_ge(v0_ready, hb + 1)
                bk = fill(2 + hb, r1_ready, hb + 1)
                for i in range(4):
                    h = 4 * hb + i
                    m = pe.matmul(bk[:, i * P:(i + 1) * P], pairs[:, h, P:2 * P], vtok[:, 0, h, :], start=True, stop=True)
                m.then_inc(solve_filled, 1)
                bk = fill(6 + hb, o_ready, hb + 1)
                for i in range(4):
                    h = 4 * hb + i
                    m = pe.matmul(bk[:, i * P:(i + 1) * P], pairs[:, h, 2 * P:3 * P], vtok[:, 0, h, :],
                                  start=True, stop=True)
                m.then_inc(solve_filled, 1)
            for hb in range(2):
                pe.wait_ge(r1_ready, hb + 1)
                bk = fill(4 + hb, v1_ready, hb + 1)
                for i in range(4):
                    h = 4 * hb + i
                    m = pe.matmul(bk[:, i * P:(i + 1) * P], XT[:, 2 * h + 1, :], vtok[:, 1, h, :], start=True, stop=True)
                m.then_inc(solve_filled, 1)
            for hb in range(2):
                pe.wait_ge(v1_ready, hb + 1)
                bk = fill(hb, o_ready, 3 + hb)
                for i in range(4):
                    h = 4 * hb + i
                    pe.matmul(bk[:, i * P:(i + 1) * P], pairs[:, h, 3 * P:4 * P], vtok[:, 0, h, :], start=True, stop=False)
                    m = pe.matmul(bk[:, i * P:(i + 1) * P], pairs[:, h, 5 * P:6 * P], vtok[:, 1, h, :],
                                  start=False, stop=True)
                m.then_inc(solve_filled, 1)
            modulation(16)
            turn(tok(slot(0)), hn_ready, 3)
            for c in range(2):
                w = wide(take())
                for t in range(T):
                    if c == 0:
                        turned_tile(t)
                    tok_unit(w, t, chan(slot(2)), x_added, 2 * c + t + 1)
            pe.wait_ge(hot_in, 48)
            bk = fill(5, t5_row, 1)
            pe.matmul(bk[0:8, 0:384], relb[0:32, 0:8], slot(9, 0, 384)[0:32, :], start=True, stop=True).then_inc(t5_filled, 1)
            modulation(8)
            turn(tok(slot(0)), hn_ready, 5)
            kvT, bT = chan(slot(1)), chan(slot(2))
            turned_all()
            for n in range(2):
                w = wide(take())
                for c in (0, 2):
                    chan_unit(w, c, kvT, k_copied, 2 * n + c // 2 + 1)
            turn(tok(slot(7)), hn_ready, 7)
            for n in range(2):
                w = wide(take())
                for t in range(T):
                    tok_unit(w, t, kvT, v_copied, 2 * n + t + 1)
            turned_all()
            for n in range(2):
                w = wide(take())
                for c in (0, 2):
                    chan_unit(w, c, bT, q_copied, 2 * n + c // 2 + 1)
            zw = [None]

            def z_part(h):
                if h % 4 == 0:
                    zw[0] = wide(take())
                chan_unit(zw[0], (h % 4) // 2 * 2, bT, zb_copied, h // 2 + 1, (h % 2,))

            def m_scores(h):
                bk = fill(4 + h % 2, biased, h + 1)
                pe.matmul(bk[:, 0:S], mqT[:, h, P:S], mkT[:, h, :], start=True, stop=True)
                pe.matmul(bk[:, S:S + P], mqT[:, h, 0:P], mkT[:, h, 0:P], start=True, stop=True).then_inc(scored, 1)

            def m_out(h):
                pe.wait_ge(normed, h + 1)
                bk = fill(6 + h % 2, pt_ready, h + 1)
                p = msc[:, h % 2]
                pe.transpose(bk[:, 0:P], p[:, S:S + P], ident)
                pe.transpose(bk[:, P:S], p[:, 0:P], ident)
                pe.transpose(bk[:, S:S + P], p[:, P:S], ident).then_inc(p_turned, 1)

            def m_values(h):
                pe.wait_ge(pt_ready, h + 1)
                bk = fill(2 + h % 2, o_copied, h + 1)
                p = mpt[:, h % 2]
                pe.matmul(bk[:, 0:S], mv[:, 0, h, :], p[:, 0:S], start=True, stop=False)
                pe.matmul(bk[:, P:S], mv[:, 1, h, :], p[:, S:S + P], start=False, stop=True).then_inc(head_out, 1)

            pe.wait_ge(k_copied, 4)
            pe.wait_ge(q_copied, 4)
            pe.wait_ge(v_copied, 4)
            m_scores(0)
            for h in range(H + 2):
                if h + 1 < H:
                    m_scores(h + 1)
                if h < H:
                    z_part(h)
                if 1 <= h <= H:
                    m_out(h - 1)
                if h >= 2:
                    m_values(h - 2)
            pe.wait_ge(yt_ready, 1)
            for c in range(2):
                w = wide(take())
                for t in range(T):
                    tok_unit(w, t, myT, x_added, 4 + 2 * c + t + 1, late=(yt_ready, 2, K // 2) if c + t == 0 else None)
            turn(tok(slot(3)), ctx_normed, 1)
            nT, cT2 = chan(slot(1)), chan(slot(2))
            turned_all()
            wk, wv = wide(take()), wide(take())
            for c in (0, 2):
                chan_unit(wk, c, cT2, w_read, c // 2 + 1)
            for t in range(T):
                tok_unit(wv, t, cT2, w_act, t + 1)
            turn(tok(slot(0)), hn_ready, 9)
            w1s, w2s, feat = gain_b[0:33, 0:64], gain_b[0:64, 64:128], gain_b[0:33, 128:384]
            f1, f2 = gain_b[0:64, 384:640], gain_b[0:64, 640:896]
            turned_all()
            pe.wait_ge(filt_in, 16 * 5)
            bk = fill(4, filt_arg, 1)
            pe.matmul(bk[0:64, 0:S], w1s, feat, start=True, stop=True).then_inc(filt_filled, 1)
            for c in (0, 2):
                chan_unit(wk, c, nT, w_read, 2 + c // 2 + 1)
            pe.wait_ge(filt_sin, 1)
            bk = fill(5, filt_arg, 2)
            pe.matmul(bk[0:64, 0:S], w2s, f1, start=True, stop=True).then_inc(filt_filled, 1)
            for t in range(T):
                tok_unit(wv, t, nT, w_act, 2 + t + 1)
            w = wide(take())
            for c in (0, 2):
                chan_unit(w, c, nT, w_read, 4 + c // 2 + 1)
            pe.wait_ge(filt_sin, 2)
            for j in range(T):
                for di in range(2):
                    bk = fill(4 + 2 * j + di, filt_dec, 2 * j + di + 1)
                    pe.matmul(bk[:], f2[:, j * P:(j + 1) * P], gain_a[0:64, di * 512:di * 512 + 512],
                              start=True, stop=True).then_inc(filt_filled, 1)
            w = wide(take())
            chan_unit(w, 0, nT, w_act, 5)
            chan_unit(w, 2, nT, w_act, 6)
            pe.wait_ge(filt_mix, 2)
            pe.wait_ge(dft_in, 16)
            for m_ in range(2):
                for f in range(T):
                    bk = fill(4 + 2 * m_ + f, spec_ready, 2 * m_ + f + 1)
                    for j in range(T):
                        q = pe.matmul(bk[:], dft[:, m_, j, f * P:(f + 1) * P], mix[:, m_, j, :],
                                      start=(j == 0), stop=(j == T - 1))
                    q.then_inc(spec_filled, 1)

            def n_scores(i):
                h, t = i // 2, i % 2
                lo = 64 * (h % 2)
                bk = fill(4 + i % 2, biased, H + i + 1)
                q = nq[lo:lo + 64, h // 2, t * P:(t + 1) * P]
                pe.matmul(bk[:, 0:S], q, nk[lo:lo + 64, h // 2, :], start=True, stop=True)
                pe.matmul(bk[:, S:2 * S], q, nkc[lo:lo + 64, h // 2, :], start=True, stop=True).then_inc(scored, 1)

            def n_turn(i):
                pe.wait_ge(normed, H + i + 1)
                bk = fill(6 + i % 2, pt_ready, H + i + 1)
                for kt in range(4):
                    m = pe.transpose(bk[:, kt * P:(kt + 1) * P], nsc[:, i % 2, kt * P:(kt + 1) * P], ident)
                m.then_inc(p_turned, 1)

            def n_values(h):
                lo = 64 * (h % 2)
                pe.wait_ge(pt_ready, H + 2 * h + 2)
                bk = fill(h % 2, cat_ready, h + 1)
                for kt in range(4):
                    v = (nv if kt < 2 else nvc)[:, kt % 2, h * 64:h * 64 + 64]
                    m = pe.matmul(bk[lo:lo + 64, 0:S], v, npt[h % 2][:, kt, :], start=(kt == 0), stop=(kt == 3))
                m.then_inc(head_out, 1)

            pe.wait_ge(w_read, 6)
            pe.wait_ge(w_act, 4)
            hw = [None]

            def hy_part(i):
                if i in (0, 4):
                    hw[0] = wide(take()) if i == 0 else take()[:, 0:K * S].rearrange("p (k n) -> p k n", k=K)
                chan_unit(hw[0], i % 4 // 2 * 2, nT, hy_in_ready, i // 2 + 1, (i % 2,))

            def z_turn(o):
                pe.wait_ge(*((hy_in_ready, 3) if o == 0 else (hy_ready, 1)))
                bk = fill(3, zt_ready, o + 1)
                for t in range(T):
                    for c in range(2):
                        m = pe.transpose(bk[:, t * S + c * P:t * S + (c + 1) * P], hyu[:, 4 + c, t * P:(t + 1) * P], ident)
                m.then_inc(z_turned, 1)

            def z_spectrum(o):
                pe.wait_ge(zt_ready, o + 1)
                pe.wait_ge(spec_ready, 4)
                for f in range(T):
                    bk = fill(2 + f, zf_used, 2 * o + f + 1)
                    for m_ in range(2):
                        for t in range(T):
                            q = pe.matmul(bk[:, m_ * S:(m_ + 1) * S], dft[:, m_, t, f * P:(f + 1) * P],
                                          zt[:, t, :], start=(t == 0), stop=(t == T - 1))
                    q.then_inc(zf_filled, 1)

            def z_back(o):
                pe.wait_ge(yf_ready, 2 * o + 2)
                bk = fill(2, hy_ready, o + 1)
                for c in range(2):
                    n = 0
                    for f in range(T):
                        for m_ in range(2):
                            q = pe.matmul(bk[:, c * S:(c + 1) * S], yf[:, f, m_, c * P:(c + 1) * P],
                                          dft[:, 2 + m_, f, :], start=(n == 0), stop=(n == 3))
                            n += 1
                q.then_inc(hy_filled, 1)

            def channel_sum(src, ready, done, sem_):
                pe.wait_ge(*ready)
                bk = fill(3, *done)
                for c in range(2):
                    m = pe.matmul(bk[:, 0:S], ones, src[:, c, :], start=(c == 0), stop=(c == 1))
                m.then_inc(sem_, 1)

            n_scores(0)
            for i in range(2 * H + 3):
                if i + 1 < 2 * H:
                    n_scores(i + 1)
                if i < 6:
                    hy_part(i)
                if i in (8, 13):
                    z_spectrum(i // 13)
                if i == 11:
                    channel_sum(cfy, (cf_cent, 1), (cf_cent, 3), cf_sum)
                if 1 <= i <= 2 * H:
                    n_turn(i - 1)
                if i >= 3 and i % 2 == 1:
                    n_values((i - 3) // 2)
                if i in (7, 12):
                    z_turn(i // 12)
                if i in (10, 15):
                    z_back(i // 15)
                if i == 2 * H:
                    channel_sum(chan(cfsq), (cf_act, 1), (cf_act, 2), cf_sum)
            pe.wait_ge(cat_ready, H)
            pe.wait_ge(hy_ready, 2)
            for c in range(2):
                w = wide(take())
                for t in range(T):
                    tok_unit(w, t, catT, x_added, 8 + 2 * c + t + 1, late=(cf_ready, 2, K - 2) if c + t == 0 else None)
            modulation(8)
            turn(tok(slot(0)), hn_ready, 11)
            pe.wait_ge(router_in, 16)
            h2T = chan(slot(1))
            turned_tile(0)
            bk = fill(4, route_exp, 1)
            for t in range(T):
                if t:
                    turned_all()
                for k in range(K):
                    m = pe.matmul(bk[:, t * 16:(t + 1) * 16], h2T[:, k, t * P:(t + 1) * P], w_ab[:, k, :],
                                  start=(k == 0), stop=(k == K - 1))
            m.then_inc(route_filled, 1)
            modulation(8)
            pe.wait_ge(aff_ready, 1)
            bk = fill(5, top_ready, 1)
            for t in range(T):
                m = pe.transpose(bk[0:16, t * P:(t + 1) * P], aff[:, t, :], ident)
            m.then_inc(aff_turned, 1)
            pe.wait_ge(top_ready, 2)
            bk = fill(6, top_ready, 3)
            for t in range(T):
                m = pe.transpose(bk[:, t * 16:(t + 1) * 16], chosen_t[0:16, t * P:(t + 1) * P], ident[0:16, 0:16])
            m.then_inc(aff_turned, 1)
            pe.wait_ge(top_ready, 3)
            bk = fill(7, sel_ready, 1)
            pe.matmul(bk[:, 0:16], strict, chosen[:, 0, :], start=True, stop=True)
            pe.matmul(bk[:, 16:32], strict, chosen[:, 1, :], start=True, stop=False)
            pe.matmul(bk[:, 16:32], ones, chosen[:, 0, :], start=False, stop=True).then_inc(route_filled, 1)
            pe.wait_ge(sel_ready, 2)
            h2 = tok(slot(0)).rearrange("p t (c k) -> p t k c", k=K)

            def gather(grp, half, b):
                bk = fill(b, (xe_dve, xe_act)[half], grp + 1)
                for kk in range(4):
                    for t in range(T):
                        m = pe.matmul(bk[:, kk * P:(kk + 1) * P], h2[:, t, 4 * half + kk, :],
                                      sel[:, t, grp * P:(grp + 1) * P], start=(t == 0), stop=(t == 1))
                m.then_inc(xe_filled, 1)

            def turn_selg(half):
                bk = fill(7, selgt_ready, half + 1)
                for gg in range(2):
                    g = 2 * half + gg
                    for t in range(T):
                        m = pe.transpose(bk[:, gg * S + t * P:gg * S + (t + 1) * P], selg[:, t, g * P:(g + 1) * P], ident)
                m.then_inc(selg_turned, 1)

            def between(s, half):
                if s < GROUPS - 1:
                    gather(s + 1, half, 7)
                elif s == GROUPS - 1:
                    if half == 0:
                        pe.wait_ge(selg_ready, 1)
                    turn_selg(half)

            for half in range(2):
                gather(0, half, half)
            for b in range(8):
                for s_, c_ in reader.get(b, ()):
                    pe.wait_ge(s_, c_)

            def wait_piece(n, g):
                c = 16 * (n // RING + 1)
                pe.wait_ge(piece_in[n % RING], c if g is None else g * (16 * BODY // RING) + c)

            def at(base, step, g):
                return base if g is None else g * step + base

            def wide_product(n, s, bk, g):
                for j in range(4):
                    wait_piece(n + j, g)
                    w = ring[(n + j) % RING][:].rearrange("p (k n) -> p k n", k=2)
                    for kk in range(2):
                        for q in range(4):
                            m = pe.matmul(bk[32 * q:32 * q + 32, :], xe[:, s % 2, 2 * j + kk, :],
                                          w[:, kk, q * 512:q * 512 + 512], start=(j + kk == 0), stop=(j + kk == 4))
                    m.then_inc(xpiece, 1)

            def turn_act(s, g):
                pe.wait_ge(act_made, at(s + 1, 4, g))
                for b in range(4):
                    m = pe.transpose(bank[4][:, b * P:(b + 1) * P],
                                     act.rearrange("p (c b) -> p b c", b=4)[:, b, :], ident)
                m.then_inc(act_turned, 1)

            def narrow_product(n, s, g):
                pe.wait_ge(actt_ready, at(s + 1, 4, g))
                if s >= 4 or g is not None:
                    pe.wait_ge(y_copied, at(s - 2, 4, g))
                q = s % 4
                for j in range(4):
                    wait_piece(n + j, g)
                    w = ring[(n + j) % RING][:].rearrange("p (k n) -> p k n", k=4)
                    for b in range(4):
                        for half in range(2):
                            m = pe.matmul(bank[5 + half][32 * q:32 * q + 32, :], actt[:, b, 32 * j:32 * j + 32],
                                          w[:, b, half * 512:half * 512 + 512],
                                          start=(j + b == 0), stop=(j + b == 6))
                    m.then_inc(xpiece, 1)

            def expert_step(n, s, g):
                pe.wait_ge(xe_static, at(s + 1, 4, g))
                if s >= 2:
                    pe.wait_ge(gate_silu, at(s - 1, 4, g))
                wide_product(n, s, bank[s % 2], g)
                if s >= 1:
                    turn_act(s - 1, g)
                if s >= 2:
                    pe.wait_ge(act_made, at(s - 1, 4, g))
                wide_product(n + 4, s, bank[2 + s % 2], g)
                if g is None:
                    between(s, 0)
                if s >= 1:
                    narrow_product(n + 8, s - 1, g)
                if g is None:
                    between(s, 1)
                return n + (8 if s == 0 else NP_ROW)

            n = NPRE
            for s in range(4):
                n = expert_step(n, s, None)
            with pe.Fori(0, GROUPS - 1) as g:
                m_ = n
                for q in range(4):
                    m_ = expert_step(m_, 4 + q, g)
            n += (GROUPS - 1) * BODY
            turn_act(NEXP - 1, None)

            def combine(groups):
                for half in range(2):
                    for t in range(T):
                        for g in groups:
                            m = pe.matmul(bank[2 * half + t][:], selgt[:, g, t * P:(t + 1) * P],
                                          yexp[:, g, half * 512:half * 512 + 512],
                                          start=(g == 0), stop=(g == GROUPS - 1))
                        if groups[-1] == GROUPS - 1:
                            m.then_inc(comb_filled, 1)

            pe.wait_ge(selgt_ready, 2)
            pe.wait_ge(y_copied, NEXP - 4)
            combine(range(GROUPS - 1))
            narrow_product(n, NEXP - 1, None)
            pe.wait_ge(y_copied, NEXP)
            combine([GROUPS - 1])

        @block.scalar
        def _(act_e):
            w_ = act_e.wait_ge

            def f(dst, src, func, **kw):
                return nc.scalar.activation(dst, src, func, **kw)

            def load(dst, src, s_):
                act_e.dma_start(dst, src).then_inc(s_, 16)

            def stats(n, src, junk, sem_, count, by_tile=True):
                for t in range(T):
                    w_(sem_, count + (t if by_tile else 0))
                    if n:
                        w_(rstd_ready, T * (n - 1) + t + 1)
                    f(junk[:, t, :], src[:, t, :], ACT.Square, accum_out=sums[:, t:t + 1]).then_inc(squares, 1)
                    w_(squares, T * n + t + 1)
                    f(devs[:, t:t + 1], sums[:, t:t + 1], ACT.Sqrt, bias=eps_c, scale=1.0 / D).then_inc(sd_ready, 1)

            def turned_copies(n, dst):
                for t in range(T):
                    w_(turned, 4 * n + 2 * t + 2)
                    f(chan(dst)[:, 4:8, t * P:(t + 1) * P], bank[5 + 2 * t][:].rearrange("p (k n) -> p k n", k=4),
                      ACT.Copy).then_inc(turned_act, 1)

            w_(consts_set, 1)
            stats(0, x, tok(slot(0)), x_in, 16, False)
            turned_copies(0, slot(1))
            r = 0
            for src in (a["cf_dw_w_2"][0].rearrange("j (t p) -> (j t) p", p=P),
                        a["cf_dw_b_2"][0].rearrange("(t p) -> t p", p=P),
                        a["cf_ln_g_2"][0].rearrange("(t p) -> t p", p=P),
                        a["cf_ln_b_2"][0].rearrange("(t p) -> t p", p=P),
                        a["hy_short_w_2"][0].rearrange("j (t p) -> (j t) p", p=P),
                        a["hy_short_b_2"][0].rearrange("(t p) -> t p", p=P),
                        a["hy_bias_d_2"][0].rearrange("o (t p) -> (o t) p", p=P)):
                load(rows2[r:r + src.shape[0], :], src, small_in)
                r += src.shape[0]
            load(rows3[0:8, :], a["c_2"][0].rearrange("(k p) -> k p", p=P), small_in)
            load(rows3[8:16, :], a["c_ctx_2"].rearrange("(k p) -> k p", p=P), small_in)
            load(alog, a["a_log"].to_broadcast([P, 8]), small_in)
            load(dtb, a["a_dt_bias"].to_broadcast([P, 8]), small_in)
            load(out_g, a["a_out_norm_g"].to_broadcast([P, P]), small_in)
            for i, name in enumerate(("hy_filt_b1_2", "hy_filt_freq_2", "hy_filt_b2_2")):
                load(filt[0:64, i:i + 1], a[name][0].rearrange("(p o) -> p o", o=1), small_in)
            bmod(act_e, 0)
            bmod(act_e, 1)
            for u in range(12):
                if u == 4:
                    w_(small_in, 16 * 15)
                    w_(ga_ready, 1)
                    f(gtmp, ga, ACT.Abs).then_inc(act_chain, 1)
                    w_(act_chain, 1)
                    f(gtmp, gtmp, ACT.Exp, scale=-1.0).then_inc(act_chain, 1)
                    f(ealog, alog, ACT.Exp)
                    f(beta, ab[:, :, 8:16], ACT.Exp, scale=-1.0)
                    w_(act_chain, 2)
                    f(gtmp, gtmp, ACT.Ln, bias=one_c).then_inc(gate_act, 1)
                w_(conv_done, u + 1)
                q = raw[:, u * 512:(u + 1) * 512]
                f(q, q, ACT.Silu).then_inc(silu_done, 1)
                if u < 8:
                    w_(silu_done, u + 1)
                    f(slot((0, 2)[u // 4], (u % 4) * 512, (u % 4) * 512 + 512), q, ACT.Square).then_inc(sq_ready, 1)
            w_(cols_ready, 3)
            f(cols[:, R3:R3 + 16], cols[:, R3:R3 + 16], ACT.Silu).then_inc(csilu_ready, 1)
            w_(l2_summed, 1)
            f(l2sd, bank[5][:, 0:32], ACT.Sqrt, bias=eps_c).then_inc(l2_sd, 1)
            for n in range(2):
                for t in range(T):
                    w_(unit, 12 + 2 * n + t + 1)
                    f(tok(zsil)[:, t, n * 512:(n + 1) * 512], bank[2 * n + t][:], ACT.Silu).then_inc(z_ready, 1)
            w_(l2r_ready, 2)
            w_(f_turned, 4)
            f(slot(0).rearrange("p (n c) -> p n c", c=P), l2r[:, 0:16].unsqueeze(2).to_broadcast([P, 16, P]),
              ACT.Copy).then_inc(fq_ready, 1)
            for h in range(H):
                w_(diff_ready, h + 1)
                f(decay[:, h % 2], decay[:, h % 2], ACT.Exp).then_inc(decay_ready, 1)
            for lv in range(1, LEVELS):
                for g in range(4):
                    w_(y_filled, 4 * (lv - 1) + g + 1)
                    f(slot(3, g * 512, (g + 1) * 512), bank[2 + g % 2][:], ACT.Copy).then_inc(y_ready, 1)
            v2, o2 = tok(slot(5)), tok(osb)

            def o_copy(t, hb):
                w_(solve_filled, (4 + 2 * hb, 9 + hb)[t])
                f(o2[:, t, hb * 512:(hb + 1) * 512], bank[(6 + hb, hb)[t]][:], ACT.Copy).then_inc(o_ready, 1)

            def o_squares(t):
                w_(o_ready, 2 * t + 2)
                f(tok(slot(4))[:, t, :], o2[:, t, :], ACT.Square).then_inc(o_sq, 1)

            def o_sds(t):
                w_(o_ms, t + 1)
                q = osum[:, t * H:(t + 1) * H]
                f(q, q, ACT.Sqrt, bias=eps_c, scale=1.0 / P).then_inc(o_sd, 1)

            for hb in range(2):
                w_(solve_filled, hb + 1)
                f(v2[:, 0, hb * 512:(hb + 1) * 512], bank[hb][:], ACT.Copy).then_inc(v0_ready, 1)
            for hb in range(2):
                o_copy(0, hb)
            for hb in range(2):
                w_(solve_filled, 7 + hb)
                f(v2[:, 1, hb * 512:(hb + 1) * 512], bank[4 + hb][:], ACT.Copy).then_inc(v1_ready, 1)
            o_squares(0)
            for hb in range(2):
                o_copy(1, hb)
            o_sds(0)
            o_squares(1)
            o_sds(1)
            turned_copies(1, slot(2))
            stats(1, x, tok(slot(0)), x_added, 3)
            turned_copies(2, slot(1))

            def unit_copy(u, dst, sem_, func=ACT.Copy):
                w_(unit, u + 1)
                f(dst, bank[bank_of[u]][:], func).then_inc(sem_, 1)

            def blocks(ap, n):
                return ap.rearrange("p (b n) -> p b n", n=n)

            for j in range(4):
                unit_copy(U_K + j, slot(3, j * 512, (j + 1) * 512), k_copied)
            turned_copies(3, slot(2))
            for j in range(4):
                u = U_Q + j
                w_(unit, u + 1)
                f(blocks(slot(5, j * 512, (j + 1) * 512), P), flipped(bank[bank_of[u]][:], P),
                  ACT.Copy).then_inc(q_copied, 1)
            for h in range(H + 1):
                if h < H:
                    b = h % 2
                    w_(maxed, h + 1)
                    f(msc[:, b, 0:S], msc[:, b, 0:S], ACT.Exp, bias=hd[:, b, 0:1], accum_out=hd[:, b, 2:3])
                    f(msc[:, b, S:S + P], msc[:, b, S:S + P], ACT.Exp, bias=hd[:, b, 1:2],
                      accum_out=hd[:, b, 3:4]).then_inc(exped, 1)
                if h >= 1:
                    w_(p_turned, h)
                    if h >= 3:
                        w_(head_out, h - 2)
                    f(blocks(mpt[:, (h - 1) % 2], P), flipped(bank[6 + (h - 1) % 2][:, 0:384], P),
                      ACT.Copy).then_inc(pt_ready, 1)
                if h >= 2 and h % 2 == 0:
                    j = h // 2 - 1
                    unit_copy(U_Z + j, slot(6, j * 512, (j + 1) * 512), zb_copied)
            w_(zb_copied, 4)
            for j in range(2):
                q = slot(6, j * 1024, (j + 1) * 1024)
                f(q, q, ACT.Silu).then_inc(zb_silu, 1)
            stats(2, tok(slot(3)), tok(slot(0)), ctx_in, 16, False)
            turned_copies(4, slot(2))
            stats(3, x, tok(slot(0)), x_added, 7)
            stats(4, x, tok(slot(0)), x3_ready, 1)
            for j in range(2):
                unit_copy(U_CTX + 2 + j, slot(5, j * 512, (j + 1) * 512), w_act)
            turned_copies(5, slot(1))
            w1, w2 = gain_b[0:64, 384:640], gain_b[0:64, 640:896]
            w_(filt_arg, 1)
            f(w1, w1, ACT.Sin).then_inc(filt_sin, 1)
            w_(filt_arg, 2)
            f(w2, w2, ACT.Sin).then_inc(filt_sin, 1)
            for j in range(2):
                unit_copy(U_NV + j, slot(4, j * 512, (j + 1) * 512), w_act)
            unit_copy(U_CF, slot(5, 1024, 1536), w_act)
            unit_copy(U_CF + 1, slot(5, 1536), w_act, ACT.Sigmoid)
            for s in mod_out:
                w_(s, 16 * 5)
            for i in range(4):
                w_(spec_filled, i + 1)
                f(spec[i // 2][:, i % 2, :], bank[4 + i][:], ACT.Copy).then_inc(spec_ready, 1)
            for i in range(2 * H + 3):
                if i < 2 * H:
                    b = i % 2
                    w_(maxed, H + i + 1)
                    f(nsc[:, b], nsc[:, b], ACT.Exp, bias=hd[:, b, 0:1], accum_out=hd[:, b, 2:3]).then_inc(exped, 1)
                if 1 <= i <= 2 * H:
                    h, t = (i - 1) // 2, (i - 1) % 2
                    w_(p_turned, H + i)
                    if h >= 2:
                        w_(head_out, H + h - 1)
                    f(npt[h % 2][:, :, t * P:(t + 1) * P].rearrange("p k (b n) -> p k b n", n=64),
                      flipped(bank[6 + t][:], 64).rearrange("p (k b) n -> p k b n", k=4),
                      ACT.Copy).then_inc(pt_ready, 1)
                if i >= 3 and i % 2 == 1:
                    h = (i - 3) // 2
                    lo = 64 * (h % 2)
                    w_(head_out, H + h + 1)
                    f(catT[lo:lo + 64, h // 2, :], bank[h % 2][lo:lo + 64, 0:S], ACT.Copy).then_inc(cat_ready, 1)
                if i in (7, 12):
                    w_(z_turned, 1 + i // 12)
                    f(slot(1, 0, 512), bank[3][:], ACT.Copy).then_inc(zt_ready, 1)
                if i == 2 * H:
                    w_(cf_cent, 3)
                    f(cfsq, slot(6, 1536), ACT.Square).then_inc(cf_act, 1)
            w_(cf_sum, 2)
            f(cfsd, bank[3][:, 0:S], ACT.Sqrt, bias=eps_c, scale=1.0 / S).then_inc(cf_act, 1)
            w_(cf_n, 1)
            for c in range(2):
                f(catT[:, 6 + c, :], cfy[:, c, :], ACT.Silu, scale=cols[:, LNG + c:LNG + c + 1],
                  bias=cols[:, LNB + c:LNB + c + 1]).then_inc(cf_ready, 1)
            w_(hy_ready, 2)
            for m in (10, 11):
                bmod(act_e, m)
            stats(5, x, tok(slot(0)), x_added, 11)
            turned_copies(6, slot(1))
            w_(route_max, 1)
            for t in range(T):
                m = f(aff[:, t, :], bank[4][:, t * 16:(t + 1) * 16], ACT.Exp, bias=rmax[:, t:t + 1],
                      accum_out=rsum[:, t:t + 1])
            m.then_inc(route_exp, 1)
            for m in (10, 11):
                w_(mod_added, m + 1)
                mod_send(act_e, m)

            def gathered(grp, b):
                w_(xe_filled, 2 * grp + 2)
                f(xet[:, 4:8, grp * P:(grp + 1) * P], bank[b][:].rearrange("p (k n) -> p k n", k=4),
                  ACT.Copy).then_inc(xe_act, 1)

            gathered(0, 1)

            def step(s, g):
                def at(base, stride):
                    return base if g is None else g * stride + base
                w_(xpiece, at(done_a(s), BODY))
                if s >= 1:
                    w_(act_made, at(s, 4))
                f(hs, bank[s % 2][:], ACT.Silu).then_inc(gate_silu, 1)
                if s >= 1:
                    w_(act_turned, at(s, 4))
                    if s >= 2:
                        w_(xpiece, at(done_y(s - 2), BODY))
                    f(slot(7, 1024, 1536), bank[4][:], ACT.Copy).then_inc(actt_ready, 1)

            for s in range(4):
                step(s, None)
                if s < GROUPS - 1:
                    gathered(s + 1, 7)
                else:
                    for half in range(2):
                        w_(selg_turned, half + 1)
                        f(selgt[:, 2 * half:2 * half + 2, :], bank[7][:].rearrange("p (g n) -> p g n", g=2),
                          ACT.Copy).then_inc(selgt_ready, 1)
            with act_e.Fori(0, GROUPS - 1) as g:
                for q in range(4):
                    step(4 + q, g)
            w_(act_turned, NEXP)
            w_(xpiece, done_y(NEXP - 2))
            f(slot(7, 1024, 1536), bank[4][:], ACT.Copy).then_inc(actt_ready, 1)
            stats(6, x, tok(slot(1)), x_added, 15)

        @block.vector
        def _(dve):
            v = nc.vector
            w_ = dve.wait_ge
            steps = [0]

            def link(ins):
                ins.then_inc(dve_chain, 1)
                steps[0] += 1
                w_(dve_chain, steps[0])

            def stt(dst, a_, s_, b_, op0=ALU.mult, op1=ALU.mult):
                return v.scalar_tensor_tensor(dst, a_, s_, b_, op0, op1)

            def invert(n, t):
                w_(sd_ready, T * n + t + 1)
                v.reciprocal(rstd[:, t:t + 1], devs[:, t:t + 1]).then_inc(rstd_ready, 1)
                w_(rstd_ready, T * n + t + 1)

            def turned_copies(n, dst):
                for t in range(T):
                    w_(turned, 4 * n + 2 * t + 1)
                    v.tensor_copy(chan(dst)[:, 0:4, t * P:(t + 1) * P],
                                  bank[4 + 2 * t][:].rearrange("p (k n) -> p k n", k=4)).then_inc(turned_dve, 1)

            v.memset(eps_c, EPS)
            v.memset(one_c, 1.0).then_inc(consts_set, 1)
            h0 = tok(slot(0))
            w_(gain_in, 16)
            for t in range(T):
                invert(0, t)
                stt(h0[:, t, :], x[:, t, :], rstd[:, t:t + 1], gain_a).then_inc(hn_ready, 1)
            turned_copies(0, slot(1))
            w_(rows_turned, 1)
            v.tensor_copy(cols[:, CW:CW + 96], bank[0][:, 0:96]).then_inc(cols_ready, 1)
            w_(ab_done, 1)
            v.tensor_copy(ab, bank[4][:, 0:32].rearrange("p (t n) -> p t n", t=T)).then_inc(ab_copied, 1)
            w_(cols_ready, 1)

            def taps(u):
                w_(unit, u + 1)
                src = chan(bank[u % 4][:])
                dst = chan(raw[:, u * 512:(u + 1) * 512])
                for j in (3, 2, 1, 0):
                    sh = 3 - j
                    for i in range(2):
                        wt = cols[:, CW + 24 * j + 2 * u + i:CW + 24 * j + 2 * u + i + 1]
                        if j == 3:
                            m = v.tensor_scalar(dst[:, i, :], src[:, i, :], wt, None, ALU.mult)
                        else:
                            m = stt(dst[:, i, sh:], src[:, i, 0:S - sh], wt, dst[:, i, sh:], op1=ALU.add)
                    if j:
                        link(m)
                m.then_inc(conv_done, 1)

            for u in range(4):
                taps(u)
            w_(rows_turned, 2)
            for c, o, n in ((R2, 0, 96), (R3, 96, 16)):
                v.tensor_copy(cols[:, c:c + n], bank[5][:, o:o + n]).then_inc(cols_ready, 1)
            w_(ab_copied, 1)
            w_(small_in, 16 * 15)
            v.tensor_tensor(ga, ab[:, :, 0:8], dtb.unsqueeze(1).to_broadcast([P, T, 8]), ALU.add).then_inc(ga_ready, 1)
            w_(ga_ready, 1)
            taps(4)
            w_(gate_act, 1)
            link(stt(gtmp, ga, 0.0, gtmp, ALU.max, ALU.add))
            stt(glog, gtmp, -1.0, ealog.unsqueeze(1).to_broadcast([P, T, 8])).then_inc(gate_ready, 1)
            link(v.tensor_scalar(beta, beta, 1.0, None, ALU.add))
            link(v.reciprocal(beta, beta))
            for u in range(5, 12):
                taps(u)
            w_(cum_done, 1)
            v.tensor_copy(gcum, bank[4][:, 0:16].rearrange("p (t n) -> p t n", t=T)).then_inc(cum_copied, 1)
            w_(cum_copied, 1)
            w_(l2_sd, 1)
            link(v.reciprocal(l2r, l2sd))
            v.tensor_copy(slot(0).rearrange("p (n c) -> p n c", c=P),
                          l2r[:, 16:32].unsqueeze(2).to_broadcast([P, 16, P])).then_inc(fk_ready, 1)
            v.tensor_scalar(l2r[:, 0:16], l2r[:, 0:16], float(P) ** -0.5, None, ALU.mult).then_inc(l2r_ready, 1)
            v.tensor_tensor(l2kb, l2r[:, 16:32], beta.rearrange("p t n -> p (t n)"), ALU.mult).then_inc(l2r_ready, 1)

            def scaled(n, dst, src):
                for j in range(4):
                    w_(f_turned, 4 * n + j + 1)
                    v.tensor_tensor(dst(j), chan(src[:, j * 512:(j + 1) * 512]), chan(bank[4 + j][:]),
                                    ALU.mult).then_inc(qk_ready, 1)

            q_raw, k_raw = raw[:, 0:2048], raw[:, 2048:4096]
            scaled(0, lambda j: kT[:, 2 * j:2 * j + 2, :], k_raw)
            for t in range(T):
                for hb in range(2):
                    w_(v_turned, 2 * t + hb + 1)
                    v.tensor_tensor(vtok[:, t, 4 * hb:4 * hb + 4, :],
                                    bank[4 + 2 * t + hb][:].rearrange("p (h d) -> p h d", h=4),
                                    beta[:, t, 4 * hb:4 * hb + 4].unsqueeze(2).to_broadcast([P, 4, P]),
                                    ALU.mult).then_inc(v_ready, 1)
            scaled(1, lambda j: kbq[:, 2 * j:2 * j + 2, 0, :], k_raw)
            w_(cum_copied, 1)
            v.tensor_copy(slot(1).rearrange("p (n c) -> p n c", c=P),
                          gcum.rearrange("p t n -> p (t n)").unsqueeze(2).to_broadcast([P, 16, P])).then_inc(gb_ready, 1)
            scaled(2, lambda j: kbq[:, 2 * j:2 * j + 2, 1, :], q_raw)

            def add_mod(m):
                w_(unit, U_MOD[m] + 1)
                w_(bmod_in[m % 2], 16 * (m // 2 + 1))
                for c in range(4):
                    q = spare[0:2, (m % 2) * 512 + c * P:(m % 2) * 512 + (c + 1) * P]
                    last = v.tensor_tensor(q, bank[bank_of[U_MOD[m]]][32 * c:32 * c + 2, 0:P], q, ALU.add)
                last.then_inc(mod_added, 1)

            add_mod(0)
            add_mod(1)
            tile0_clip = cst[:, C_CLIP:C_CLIP + 2 * P]

            def differences(h):
                w_(g_turned, h // 2 + 1)
                if h >= 2:
                    w_(prod_b, h - 1)
                row = bank[4 + (h // 2) % 2][:, (h % 2) * S:(h % 2) * S + S]
                stt(decay[:, h % 2, 0:S], row, gcum[:, 0, h:h + 1], tile0_clip, ALU.subtract, ALU.min)
                stt(decay[:, h % 2, S:S + P], row[:, P:S], gcum[:, 1, h:h + 1], tile0_clip[:, 0:P], ALU.subtract,
                    ALU.min).then_inc(diff_ready, 1)

            differences(0)
            for h in range(H):
                if h + 1 < H:
                    differences(h + 1)
                w_(decay_ready, h + 1)
                e = decay[:, h % 2]
                w_(pair_a, h + 1)
                v.tensor_tensor(chan(pairs[:, h, 0:512]), chan(bank[h % 2][:]), e[:, 0:S].unsqueeze(1).to_broadcast(
                    [P, 2, S]), ALU.mult).then_inc(prod_a, 1)
                w_(pair_b, h + 1)
                v.tensor_tensor(pairs[:, h, 512:768].rearrange("p (m n) -> p m n", m=2),
                                bank[2 + h % 2][:, 0:S].rearrange("p (m n) -> p m n", m=2),
                                e[:, S:S + P].unsqueeze(1).to_broadcast([P, 2, P]), ALU.mult).then_inc(prod_b, 1)
                if h in (3, 5):
                    add_mod(2 + h // 5)
            w_(prod_b, H)
            idb = ident.unsqueeze(1).to_broadcast([P, 4, P])

            def less(q, half, bk, g, lv):
                q = block_half(q[:, 4 * g:4 * g + 4, :].rearrange("p s c -> p (s c)"), lv, half)
                return v.tensor_tensor(q, q, bk[:, 0:256].rearrange("p (n b) -> p n b", b=2 ** lv), ALU.subtract)

            def turn_blocks(dst, src, g):
                return v.transpose(dst[:, 4 * g:4 * g + 4, :].rearrange("p s c -> p (s c)"),
                                   src[:, 4 * g:4 * g + 4, :].rearrange("p s c -> p (s c)"))

            for lv in range(LEVELS):
                for g in range(4):
                    sl = slice(4 * g, 4 * g + 4)
                    if lv == 0:
                        w_(mask_ready, g + 1)
                        v.tensor_tensor(XT[:, sl, :], idb, coupled(0, g), ALU.subtract).then_inc(xt_upd, 1)
                        w_(xt_upd, g + 1)
                        turn_blocks(X, XT, g).then_inc(x_upd, 1)
                        continue
                    w_(inv_filled, 4 * (lv - 1) + g + 1)
                    w_(x_upd, 4 * (lv - 1) + g + 1 if lv < LEVELS - 1 else 4 * (LEVELS - 1))
                    w_(xt_upd, 4 * (lv - 1) + g + 1)
                    if lv < LEVELS - 1:
                        less(X, 0, bank[4 + g % 2], g, lv).then_inc(x_upd, 1)
                    if lv > LAST_TURN:
                        less(XT, 1, bank[6 + g % 2], g, lv).then_inc(xt_upd, 1)
                    else:
                        w_(x_upd, 4 * lv + g + 1)
                        turn_blocks(XT, X, g).then_inc(xt_upd, 1)
                if lv in (0, 1):
                    add_mod(4 + lv)
            add_mod(6)
            for hb in range(2):
                w_(solve_filled, 3 + 2 * hb)
                r = tok(slot(5))[:, 1, hb * 512:(hb + 1) * 512]
                v.tensor_tensor(r, r, bank[2 + hb][:], ALU.subtract).then_inc(r1_ready, 1)
            o3 = osb.rearrange("p (n d) -> p n d", d=P)
            for t in range(T):
                hs8 = slice(t * H, (t + 1) * H)
                w_(o_sq, t + 1)
                v.tensor_reduce(osum[:, hs8], slot(4).rearrange("p (n d) -> p n d", d=P)[:, hs8, :], AX.X,
                                ALU.add).then_inc(o_ms, 1)
            w_(zg_ready, 1)
            for t in range(T):
                hs8 = slice(t * H, (t + 1) * H)
                w_(o_sd, t + 1)
                link(v.reciprocal(orstd[:, hs8], osum[:, hs8]))
                link(v.tensor_tensor(o3[:, hs8, :], o3[:, hs8, :], orstd[:, hs8].unsqueeze(2).to_broadcast([P, H, P]),
                                     ALU.mult))
                v.tensor_tensor(h0[:, t, :], tok(osb)[:, t, :], tok(zsil)[:, t, :], ALU.mult).then_inc(hn_ready, 1)
            turned_copies(1, slot(2))
            add_mod(7)
            add_mod(8)

            def add_units(u0):
                for c in range(2):
                    for t in range(T):
                        u = u0 + 2 * c + t
                        w_(unit, u + 1)
                        q = x[:, t, c * 512:(c + 1) * 512]
                        v.tensor_tensor(q, q, bank[bank_of[u]][:], ALU.add).then_inc(x_added, 1)

            add_units(U_AOUT)
            w_(t5_filled, 1)
            w_(hot_in, 48)
            v.tensor_tensor(slot(9, 768, 1152)[0:8, :], bank[5][0:8, 0:384], slot(9, 384, 768)[0:8, :],
                            ALU.add).then_inc(t5_row, 1)
            w_(b_gain_in, 32)
            for t in range(T):
                invert(1, t)
                stt(h0[:, t, :], x[:, t, :], rstd[:, t:t + 1], gain_a).then_inc(hn_ready, 1)
            add_mod(9)
            turned_copies(2, slot(1))
            for t in range(T):
                stt(tok(slot(7))[:, t, :], x[:, t, :], rstd[:, t:t + 1], gain_b).then_inc(hn_ready, 1)
            turned_copies(3, slot(2))
            for j in range(4):
                w_(unit, U_V + j + 1)
                v.tensor_copy(tok(slot(4))[:, j % 2, (j // 2) * 512:(j // 2) * 512 + 512], bank[bank_of[U_V + j]][:]
                              ).then_inc(v_copied, 1)
            w_(t5_moved, 32)
            sc = float(P) ** -0.5
            for h in range(H + 2):
                if h < H:
                    b = h % 2
                    w_(scored, h + 1)
                    if h >= 2:
                        w_(p_turned, h - 1)
                        w_(normed, h - 1)
                    bk = bank[4 + b]
                    stt(msc[:, b, 0:S], bk[:, 0:S], sc, t5[:, h, :], op1=ALU.add)
                    stt(msc[:, b, S:S + P], bk[:, S:S + P], sc, t5[:, h, P:S], op1=ALU.add).then_inc(biased, 1)
                    w_(biased, h + 1)
                    v.tensor_reduce(hd[:, b, 0:1], msc[:, b, 0:S], AX.X, ALU.max, negate=True)
                    v.tensor_reduce(hd[:, b, 1:2], msc[:, b, S:S + P], AX.X, ALU.max, negate=True).then_inc(maxed, 1)
                if 1 <= h <= H:
                    b = (h - 1) % 2
                    w_(exped, h)
                    link(v.reciprocal(hd[:, b, 4:6], hd[:, b, 2:4]))
                    v.tensor_scalar(msc[:, b, 0:S], msc[:, b, 0:S], hd[:, b, 4:5], None, ALU.mult)
                    v.tensor_scalar(msc[:, b, S:S + P], msc[:, b, S:S + P], hd[:, b, 5:6], None,
                                    ALU.mult).then_inc(normed, 1)
                if h >= 2:
                    w_(head_out, h - 1)
                    v.tensor_copy(myT[:, h - 2, :], bank[2 + h % 2][:, 0:S]).then_inc(o_copied, 1)
            for j in range(2):
                w_(zb_silu, j + 1)
                w_(o_copied, 4 * j + 4)
                q = slot(7, j * 1024, (j + 1) * 1024)
                v.tensor_tensor(q, q, slot(6, j * 1024, (j + 1) * 1024), ALU.mult).then_inc(yt_ready, 1)
            w_(c_load, 16 * 5)
            stt(slot(6, 1024), slot(6, 1024), 1.0, slot(5, 0, 1024), ALU.add)
            link(stt(slot(5, 1024), slot(5, 1024), 1.0, slot(5, 0, 1024), ALU.add))
            c3 = tok(slot(3))
            for t in range(T):
                invert(2, t)
                link(stt(c3[:, t, :], c3[:, t, :], rstd[:, t:t + 1], slot(6, 1024)))
                v.tensor_tensor(c3[:, t, :], c3[:, t, :], slot(4, 0, 1024), ALU.add).then_inc(ctx_normed, 1)
            add_units(U_BOUT)
            w_(fin_in, 16)
            turned_copies(4, slot(2))
            for t in range(T):
                invert(3, t)
                stt(x[:, t, :], x[:, t, :], rstd[:, t:t + 1], gain_a).then_inc(x3_ready, 1)
            for t in range(T):
                invert(4, t)
                link(stt(h0[:, t, :], x[:, t, :], rstd[:, t:t + 1], slot(5, 1024)))
                v.tensor_tensor(h0[:, t, :], h0[:, t, :], slot(6, 0, 1024), ALU.add).then_inc(hn_ready, 1)

            def channels_in(u, dst, rows=False):
                w_(unit, u + 1)
                src = bank[bank_of[u]][:]
                if rows:
                    dst, src = dst.rearrange("p (b n) -> p b n", n=64), flipped(src, 64)
                v.tensor_copy(dst, src).then_inc(w_read, 1)

            for j in range(2):
                channels_in(U_CTX + j, slot(4, 1024 + 512 * j, 1536 + 512 * j))
            turned_copies(5, slot(1))

            def hy_conv(n):
                u = U_HY + n
                w_(unit, u + 1)
                src, dst = chan(bank[bank_of[u]][:]), hyu[:, 2 * n:2 * n + 2, :]
                for j in (1, 0, 2):
                    for i in range(2):
                        c = 2 * n + i
                        wt = cols[:, HYW + 6 * j + c:HYW + 6 * j + c + 1]
                        if j == 1:
                            m = v.tensor_scalar(dst[:, i, :], src[:, i, :], wt, cols[:, HYB + c:HYB + c + 1],
                                                ALU.mult, ALU.add)
                        elif j == 0:
                            m = stt(dst[:, i, 1:], src[:, i, 0:S - 1], wt, dst[:, i, 1:], op1=ALU.add)
                        else:
                            m = stt(dst[:, i, 0:S - 1], src[:, i, 1:], wt, dst[:, i, 0:S - 1], op1=ALU.add)
                    if j != 2:
                        link(m)
                m.then_inc(hy_in_ready, 1)

            import math
            two_pi = 2 * math.pi
            p1 = 6.28125
            p2 = float(int((two_pi - p1) * 2 ** 22)) / 2 ** 22
            p3 = two_pi - p1 - p2
            magic = 1.5 * 2 ** 23
            turns = slot(7, 0, S)[0:64, :]
            w_(filt_in, 16 * 5)
            for i, (dst, bias) in enumerate(((gain_b[0:64, 384:640], 0), (gain_b[0:64, 640:896], 2))):
                w_(filt_filled, i + 1)
                link(v.tensor_scalar(dst, bank[4 + i][0:64, 0:S], filt[0:64, bias:bias + 1], filt[0:64, 1:2],
                                     ALU.add, ALU.mult))
                link(v.tensor_scalar(turns, dst, 1 / two_pi, magic, ALU.mult, ALU.add))
                link(v.tensor_scalar(turns, turns, magic, None, ALU.subtract))
                for p in (p1, p2, p3):
                    link(stt(dst, turns, -p, dst, op1=ALU.add))
                v.tensor_scalar(dst, dst, 3.1415925, -3.1415925, ALU.min, ALU.max).then_inc(filt_arg, 1)
                if i == 0:
                    for j in range(2):
                        channels_in(U_NK + j, slot(3, 1024 + 512 * j, 1536 + 512 * j))
            for j in range(2):
                channels_in(U_NQ + j, slot(3, 512 * j, 512 * j + 512), rows=True)
            dec4 = dec.rearrange("p (m t n) -> p m t n", m=2, t=T)
            for j in range(T):
                for di in range(2):
                    w_(filt_filled, 2 + 2 * j + di + 1)
                    v.tensor_tensor(chan(filters[:, di, j, :]), chan(bank[4 + 2 * j + di][:]),
                                    dec4[:, di, j, :].unsqueeze(1).to_broadcast([P, 2, S]), ALU.mult
                                    ).then_inc(filt_dec, 1)
            w_(filt_dec, 4)
            v.tensor_tensor(slot(7, 0, 1024), slot(0, 0, 1024), slot(0, 1024), ALU.add).then_inc(filt_mix, 1)
            v.tensor_tensor(slot(7, 1024), slot(0, 0, 1024), slot(0, 1024), ALU.subtract).then_inc(filt_mix, 1)
            w_(filt_mix, 2)
            w_(nabias_ready, 1)
            def cf_tap(j):
                for c in range(2):
                    wt = cols[:, CFW + 2 * j + c:CFW + 2 * j + c + 1]
                    sh = j - 15
                    if sh == 0:
                        m = v.tensor_scalar(cfy[:, c, :], cfa[:, c, :], wt, cols[:, CFB + c:CFB + c + 1],
                                            ALU.mult, ALU.add)
                    else:
                        o0, o1 = max(0, -sh), S - max(0, sh)
                        m = stt(cfy[:, c, o0:o1], cfa[:, c, o0 + sh:o1 + sh], wt, cfy[:, c, o0:o1], op1=ALU.add)
                return m

            def spectra(o):
                for fq in range(T):
                    w_(zf_filled, 2 * o + fq + 1)
                    z = chan(bank[2 + fq][:])
                    kre, ks = (spec[m][:, fq, o * S:(o + 1) * S] for m in range(2))
                    v.tensor_tensor(tmp_a[:, 0], z[:, 0], kre, ALU.mult)
                    v.tensor_tensor(tmp_a[:, 1], z[:, 1], ks, ALU.mult)
                    v.tensor_tensor(tmp_b[:, 0], z[:, 0], ks, ALU.mult)
                    v.tensor_tensor(tmp_b[:, 1], z[:, 1], kre, ALU.mult).then_inc(zf_used, 1)
                    w_(zf_used, 2 * o + fq + 1)
                    v.tensor_tensor(yf[:, fq, 0, :], tmp_a[:, 0], tmp_a[:, 1], ALU.subtract)
                    v.tensor_tensor(yf[:, fq, 1, :], tmp_b[:, 0], tmp_b[:, 1], ALU.add).then_inc(yf_ready, 1)
                    w_(yf_ready, 2 * o + fq + 1)

            def hy_gate(o):
                w_(hy_filled, o + 1)
                for c in range(2):
                    m = stt(tmp_a[:, c], hyu[:, 4 + c, :], cols[:, HYD + 2 * o + c:HYD + 2 * o + c + 1],
                            chan(bank[2][:])[:, c], op1=ALU.add)
                link(m)
                dst = hyu[:, 4:6, :] if o == 0 else catT[:, 4:6, :]
                v.tensor_tensor(dst, tmp_a, hyu[:, 2 * o:2 * o + 2, :], ALU.mult).then_inc(hy_ready, 1)

            for i in range(2 * H + 3):
                if i < 2 * H:
                    h, t, b = i // 2, i % 2, i % 2
                    w_(scored, H + i + 1)
                    if i >= 2:
                        w_(p_turned, H + i - 1)
                        w_(normed, H + i - 1)
                    bk = bank[4 + b]
                    bias = nab[:, h, 2 - 2 * t:6 - 2 * t, :].rearrange("p r c -> p (r c)")
                    stt(nsc[:, b, 0:S], bk[:, 0:S], 0.125, bias, op1=ALU.add)
                    v.tensor_scalar(nsc[:, b, S:2 * S], bk[:, S:2 * S], 0.125, None, ALU.mult).then_inc(biased, 1)
                    w_(biased, H + i + 1)
                    v.tensor_reduce(hd[:, b, 0:1], nsc[:, b, :], AX.X, ALU.max, negate=True).then_inc(maxed, 1)
                if 1 <= i <= 2 * H:
                    b = (i - 1) % 2
                    w_(exped, H + i)
                    link(v.reciprocal(hd[:, b, 4:5], hd[:, b, 2:3]))
                    v.tensor_scalar(nsc[:, b, :], nsc[:, b, :], hd[:, b, 4:5], None, ALU.mult).then_inc(normed, 1)
                if i == 1:
                    w_(cf_conv, 1)
                for j in DVE_TAPS[2 * i - 2:2 * i] if i else ():
                    link(cf_tap(j))
                if i == 10:
                    w_(cf_conv, 2 + 2 * len(POOL_TAPS))
                    v.tensor_tensor(cfy, cfy, cf_sum_b, ALU.add).then_inc(cf_cent, 1)
                if i in (2, 4, 6):
                    hy_conv(i // 2 - 1)
                if i in (9, 14):
                    spectra(i // 14)
                if i in (11, 16):
                    hy_gate(i // 16)
                if i == 12:
                    w_(cf_sum, 1)
                    for c in range(2):
                        stt(cfy[:, c, :], bank[3][:, 0:S], -1.0 / S, cfy[:, c, :], op1=ALU.add).then_inc(cf_cent, 1)
            w_(cf_act, 2)
            link(v.reciprocal(cfsd, cfsd))
            v.tensor_tensor(cfy, cfy, cfsd.unsqueeze(1).to_broadcast([P, 2, S]), ALU.mult).then_inc(cf_n, 1)

            def add_gated(banks, gain, scratch):
                for i, (c, t, wait) in enumerate(banks):
                    w_(*wait[0:2])
                    q = x[:, t, c * 512:(c + 1) * 512]
                    tm = slot(0, i * 512, (i + 1) * 512)
                    link(v.tensor_tensor(tm, wait[2][:], gain[:, c * 512:(c + 1) * 512], ALU.mult))
                    v.tensor_tensor(q, q, tm, ALU.add).then_inc(x_added, 1)

            w_(g1_in, 16)
            add_gated([(c, t, (unit, U_OUT + 2 * c + t + 1, bank[bank_of[U_OUT + 2 * c + t]])) for c in range(2) for t in range(T)],
                      gain_a, 0)
            w_(d_load, 16 * 3)
            link(stt(slot(8, 1024), slot(8, 1024), 1.0, slot(8, 0, 1024), ALU.add))
            for t in range(T):
                invert(5, t)
                link(stt(h0[:, t, :], x[:, t, :], rstd[:, t:t + 1], slot(8, 1024)))
                v.tensor_tensor(h0[:, t, :], h0[:, t, :], slot(9, 0, 1024), ALU.add).then_inc(hn_ready, 1)
            add_mod(10)
            turned_copies(6, slot(1))
            w_(route_filled, 1)
            v.tensor_reduce(rmax, bank[4][:, 0:32].rearrange("p (t n) -> p t n", t=T), AX.X, ALU.max,
                            negate=True).then_inc(route_max, 1)
            w_(route_exp, 1)
            link(v.reciprocal(rinv, rsum))
            v.tensor_tensor(aff, aff, rinv.unsqueeze(2).to_broadcast([P, T, 16]), ALU.mult).then_inc(aff_ready, 1)
            add_mod(11)
            w_(aff_turned, 1)
            v.tensor_copy(aff_t, bank[5][0:16, 0:S]).then_inc(top_ready, 1)
            w_(top_ready, 1)
            src = aff_t
            for r in range(CAP // 8):
                link(v.max(m8[0:16, :], src))
                link(v.match_replace(left, m8[0:16, :], src, -1.0))
                src = left
            v.tensor_tensor(chosen_t, left, aff_t, ALU.not_equal).then_inc(top_ready, 1)
            w_(aff_turned, 2)
            v.tensor_copy(chosen, bank[6][:, 0:32].rearrange("p (t n) -> p t n", t=T)).then_inc(top_ready, 1)
            w_(top_ready, 3)
            w_(route_filled, 2)
            v.tensor_copy(pos, bank[7][:, 0:32].rearrange("p (t n) -> p t n", t=T)).then_inc(sel_ready, 1)
            w_(sel_ready, 1)
            iota = cst[:, C_IOTA:C_IOTA + CAP].unsqueeze(1).to_broadcast([P, NEXP, CAP])

            def over_slots(q, t):
                return q[:, t, :].unsqueeze(2).to_broadcast([P, NEXP, CAP])

            def per_slot(q, t):
                return q[:, t, :].rearrange("p (e s) -> p e s", e=NEXP)

            for t in range(T):
                m = v.tensor_tensor(per_slot(sel, t), over_slots(pos, t), iota, ALU.is_equal)
            link(m)
            for t in range(T):
                m = v.tensor_tensor(per_slot(sel, t), per_slot(sel, t), over_slots(chosen, t), ALU.mult)
            m.then_inc(sel_ready, 1)
            w_(sel_ready, 2)

            def gathered(grp, b):
                w_(xe_filled, 2 * grp + 1)
                v.tensor_copy(xet[:, 0:4, grp * P:(grp + 1) * P], bank[b][:].rearrange("p (k n) -> p k n", k=4)
                              ).then_inc(xe_dve, 1)

            gathered(0, 0)
            for t in range(T):
                m = v.tensor_tensor(per_slot(selg, t), per_slot(sel, t), over_slots(aff, t), ALU.mult)
            m.then_inc(selg_ready, 1)

            def rows_out(s, at, grp):
                q = s % 4
                for half in range(2):
                    m = v.tensor_copy(yexp[32 * q:32 * q + 32, grp, half * 512:half * 512 + 512],
                                      bank[5 + half][32 * q:32 * q + 32, :])
                m.then_inc(y_copied, 1)

            def step(s, g):
                def at(base, stride):
                    return base if g is None else g * stride + base
                w_(xpiece, at(done_u(s), BODY))
                w_(gate_silu, at(s + 1, 4))
                if s >= 1:
                    w_(act_turned, at(s, 4))
                v.tensor_tensor(act, hs, bank[2 + s % 2][:], ALU.mult).then_inc(act_made, 1)
                if g is None and s < GROUPS - 1:
                    gathered(s + 1, 7)
                if s >= 1:
                    w_(xpiece, at(done_y(s - 1), BODY))
                    if g is None:
                        rows_out(s - 1, at, 0)
                    else:
                        q = (s - 1) % 4
                        base = g + 1 if q < 3 else g
                        for half in range(2):
                            m = v.tensor_copy(
                                slots[32 * q:32 * q + 32, bass.ds(5 * 2048 + base * D + half * 512, 512)],
                                bank[5 + half][32 * q:32 * q + 32, :])
                        m.then_inc(y_copied, 1)

            for s in range(4):
                step(s, None)
            with dve.Fori(0, GROUPS - 1) as g:
                for q in range(4):
                    step(4 + q, g)
            w_(xpiece, done_y(NEXP - 1))
            rows_out(NEXP - 1, None, GROUPS - 1)
            w_(g2_in, 32)
            add_gated([(c, t, (comb_filled, 2 * c + t + 1, bank[2 * c + t])) for c in range(2) for t in range(T)],
                      gain_b, 0)
            w_(g2_in, 32)
            for t in range(T):
                invert(6, t)
                stt(x[:, t, :], x[:, t, :], rstd[:, t:t + 1], slot(9, 0, 1024)).then_inc(final_ready, 1)


_INS = ["x", "a_norm_g", "a_w_in", "a_conv_w", "a_log", "a_dt_bias", "a_out_norm_g", "a_w_out", "kv_norm_g", "w_kv",
        "b_norm_g", "b_w_in", "b_w_out", "rel_bias", "final_norm_g", "c_2", "ctx_2", "c_ctx_2", "w_mod_2", "b_mod_2",
        "norm1_g_2", "norm2_g_2", "w_in_2", "na_rpb_2", "hy_short_w_2", "hy_short_b_2", "hy_filt_w1_2",
        "hy_filt_b1_2", "hy_filt_freq_2", "hy_filt_w2_2", "hy_filt_b2_2", "hy_filt_w3_2", "hy_bias_d_2", "cf_dw_w_2",
        "cf_dw_b_2", "cf_ln_g_2", "cf_ln_b_2", "w_out_2", "router_w_2", "expert_w1_2", "expert_w3_2", "expert_w2_2",
        "final_norm_g_2"]


def kernel(**inputs):
    import numpy as _np
    import concourse.bacc as _bacc
    from concourse import mybir as _mybir
    from concourse.bass_utils import run_bass_kernel_spmd as _run

    nc = _bacc.Bacc("TRN2", target_bir_lowering=False, num_devices=1)
    arrays, aps = {}, {}
    tables = arrays_of_shapes()
    for name in _INS + list(tables):
        v = tables[name] if name in tables else _np.ascontiguousarray(inputs[name])
        arrays[f"in_{name}_dram"] = v
        aps[name] = nc.dram_tensor(f"in_{name}_dram", v.shape, _mybir.dt.from_np(v.dtype), kind="ExternalInput").ap()
    out = nc.dram_tensor("out_0_dram", (1, S, D), F32, kind="ExternalOutput").ap()
    program(nc, aps, out)
    r = _run(nc, [arrays], core_ids=[0])
    return r.results[0]["out_0_dram"]
```
